# Optimizing a Trainium2 kernel written in Bass

```python
import math
import jax, jax.numpy as jnp
from jax import lax
import numpy as np

D_MODEL = 1024
BATCH = 1
SEQ = 512
DEPTH = 2

N_MIXERS = 3
GRID_W = 64
EPS = 1e-6
N_HEADS = 16
HEAD_DIM = D_MODEL // N_HEADS
N_KV_HEADS = 4
Q_BLOCK = 128
ROPE_THETA = 10000.0
HY_ORDER = 2
HY_EMB_DIM = 33
HY_FILTER_WIDTH = 64
HY_FAST_DECAY = 0.3
HY_SLOW_DECAY = 1.5
HY_TARGET = 1e-2
S5_GROUP = 16
S5_GROUPS = D_MODEL // S5_GROUP
S5_STATE = 64
S5_DT_MIN = 1e-3
S5_DT_MAX = 1e-1
D_FF = 2816


def rmsnorm(x, g):
    xf = x.astype(jnp.float32)
    y = xf * lax.rsqrt(jnp.mean(xf * xf, axis=-1, keepdims=True) + EPS)
    return (y * g.astype(jnp.float32)).astype(x.dtype)

def dwconv3(x, w, b):
    L = x.shape[1]
    xp = jnp.pad(x, ((0, 0), (1, 1), (0, 0)))
    return xp[:, :L] * w[0] + xp[:, 1:L + 1] * w[1] + xp[:, 2:] * w[2] + b

def axial_rope_tables(L):
    rows = L // GRID_W
    n_freq = HEAD_DIM // 4
    inv = 1.0 / (ROPE_THETA ** (jnp.arange(n_freq, dtype=jnp.float32) / n_freq))
    r = jnp.arange(rows, dtype=jnp.float32)
    col = jnp.arange(GRID_W, dtype=jnp.float32)
    ang_r = jnp.broadcast_to(r[:, None, None] * inv, (rows, GRID_W, n_freq))
    ang_c = jnp.broadcast_to(col[None, :, None] * inv, (rows, GRID_W, n_freq))
    ang = jnp.concatenate([ang_r, ang_c], axis=-1).reshape(L, 2 * n_freq)
    return jnp.cos(ang), jnp.sin(ang)

def apply_rope(x, cos, sin):
    xf = x.astype(jnp.float32).reshape(x.shape[:-1] + (HEAD_DIM // 2, 2))
    x0, x1 = xf[..., 0], xf[..., 1]
    c = cos[None, :, None, :]
    s = sin[None, :, None, :]
    out = jnp.stack([x0 * c - x1 * s, x0 * s + x1 * c], axis=-1).reshape(x.shape)
    return out.astype(x.dtype)

def attention_mixer(h, w_qkv, w_o, q_gain, k_gain, cos, sin):
    Bsz, L, _ = h.shape
    G = N_HEADS // N_KV_HEADS
    qkv = h @ w_qkv
    q, k, v = jnp.split(qkv, [N_HEADS * HEAD_DIM, (N_HEADS + N_KV_HEADS) * HEAD_DIM], axis=-1)
    q = q.reshape(Bsz, L, N_HEADS, HEAD_DIM)
    k = k.reshape(Bsz, L, N_KV_HEADS, HEAD_DIM)
    v = v.reshape(Bsz, L, N_KV_HEADS, HEAD_DIM)
    q = apply_rope(rmsnorm(q, q_gain), cos, sin)
    k = apply_rope(rmsnorm(k, k_gain), cos, sin)
    nb = L // Q_BLOCK
    qb = q.reshape(Bsz, nb, Q_BLOCK, N_KV_HEADS, G, HEAD_DIM).transpose(1, 0, 2, 3, 4, 5)
    scale = HEAD_DIM ** -0.5

    def block(q_blk):
        s = jnp.einsum('bqkgd,bskd->bkgqs', q_blk, k, preferred_element_type=jnp.float32) * scale
        p = jax.nn.softmax(s, axis=-1).astype(v.dtype)
        return jnp.einsum('bkgqs,bskd->bqkgd', p, v)

    o = lax.map(block, qb)
    o = o.transpose(1, 0, 2, 3, 4, 5).reshape(Bsz, L, N_HEADS * HEAD_DIM)
    return o @ w_o

def hyena_pos_features(L):
    t = jnp.linspace(0.0, 1.0, L, dtype=jnp.float32)[:, None]
    bands = (HY_EMB_DIM - 1) // 2
    w = 2.0 * math.pi * jnp.arange(L, dtype=jnp.float32) / L
    f = jnp.linspace(1e-4, bands - 1, bands, dtype=jnp.float32)
    ang = w[:, None] * f[None, :]
    z = jnp.concatenate([t, jnp.cos(ang), -jnp.sin(ang)], axis=-1)
    deltas = jnp.abs(jnp.linspace(math.log(HY_TARGET) / HY_SLOW_DECAY,
                                  math.log(HY_TARGET) / HY_FAST_DECAY, D_MODEL, dtype=jnp.float32))
    decay = jnp.exp(-t * deltas[None, :])
    return z, decay

def hyena_mixer(h, w_in, conv_w, conv_b, f_w1, f_b1, f_w2, f_b2, f_w3, f_freq, skip, w_out, z, decay):
    Bsz, L, D = h.shape
    u = dwconv3(h @ w_in, conv_w, conv_b)
    v, x1, x2 = jnp.split(u, 3, axis=-1)
    a = jnp.sin(f_freq * (z @ f_w1 + f_b1))
    a = jnp.sin(f_freq * (a @ f_w2 + f_b2))
    filt = (a @ f_w3).astype(jnp.float32).reshape(L, HY_ORDER, 2, D) * decay[:, None, None, :]
    fwd = filt[:, :, 0]
    bwd = filt[:, :, 1]
    k2 = jnp.concatenate([fwd, jnp.zeros_like(fwd[:1]), bwd[1:][::-1]], axis=0)
    k2 = k2 / jnp.sum(jnp.abs(k2), axis=0, keepdims=True)
    kf = jnp.fft.rfft(k2, axis=0)
    gates = (x1, x2)
    zc = v
    for o in range(HY_ORDER):
        zf = jnp.fft.rfft(zc.astype(jnp.float32), n=2 * L, axis=1)
        y = jnp.fft.irfft(zf * kf[None, :, o], n=2 * L, axis=1)[:, :L]
        zc = gates[o] * (y.astype(h.dtype) + skip[o] * zc)
    return zc @ w_out

def s5_direction(u, A_re, A_im, log_dt, B_re, B_im, C_re, C_im, reverse):
    L = u.shape[1]
    lam = lax.complex(jnp.minimum(A_re.astype(jnp.float32), -1e-4), A_im.astype(jnp.float32))
    dt = jnp.exp(log_dt.astype(jnp.float32))[:, None]
    lam_bar = jnp.exp(lam * dt)
    b_c = lax.complex(B_re.astype(jnp.float32), B_im.astype(jnp.float32))
    b_bar = ((lam_bar - 1.0) / lam)[..., None] * b_c
    bu = jnp.einsum('blgh,gph->blgp', u.astype(jnp.complex64), b_bar)
    a = jnp.broadcast_to(lam_bar[None, None], (1, L) + lam_bar.shape)

    def combine(e1, e2):
        a1, b1 = e1
        a2, b2 = e2
        return a2 * a1, a2 * b1 + b2

    _, xs = lax.associative_scan(combine, (a, bu), axis=1, reverse=reverse)
    c_c = lax.complex(C_re.astype(jnp.float32), C_im.astype(jnp.float32))
    return jnp.einsum('blgp,ghp->blgh', xs, c_c).real

def s5_mixer(h, A_re, A_im, log_dt, B_re, B_im, C_re, C_im, d_skip, w_glu):
    Bsz, L, D = h.shape
    hf = h.astype(jnp.float32)
    u = hf.reshape(Bsz, L, S5_GROUPS, S5_GROUP)
    y_f = s5_direction(u, A_re[0], A_im[0], log_dt[0], B_re[0], B_im[0], C_re[0], C_im[0], False)
    y_b = s5_direction(u, A_re[1], A_im[1], log_dt[1], B_re[1], B_im[1], C_re[1], C_im[1], True)
    y = (y_f + y_b).reshape(Bsz, L, D) + d_skip.astype(jnp.float32) * hf
    y = jax.nn.gelu(y.astype(h.dtype))
    g_a, g_b = jnp.split(y @ w_glu, 2, axis=-1)
    return g_a * jax.nn.sigmoid(g_b)

def conv_ffn(h, w_up, conv_w, conv_b, w_down):
    gate, val = jnp.split(h @ w_up, 2, axis=-1)
    gate = dwconv3(gate, conv_w, conv_b)
    return (jax.nn.silu(gate) * val) @ w_down

def first_inputs(seed: int = 0) -> dict:
    key = jax.random.key(seed)
    ks = iter(jax.random.split(key, 48))
    f32 = jnp.float32

    def nrm(shape, scale):
        return jax.random.normal(next(ks), shape, f32) * scale

    n_attn = len(range(0, DEPTH, N_MIXERS))
    n_hy = len(range(1, DEPTH, N_MIXERS))
    n_s5 = len(range(2, DEPTH, N_MIXERS))
    D = D_MODEL
    G, P, Hg = S5_GROUPS, S5_STATE, S5_GROUP
    qkv_w = (N_HEADS + 2 * N_KV_HEADS) * HEAD_DIM
    return {
        'x': nrm((BATCH, SEQ, D), 1.0),
        'c': nrm((BATCH, D), 1.0),
        'ada_w': nrm((DEPTH, D, 6 * D), 0.5 * D ** -0.5),
        'ada_b': nrm((DEPTH, 6 * D), 0.02),
        'norm1_g': 1.0 + nrm((DEPTH, D), 0.02),
        'norm2_g': 1.0 + nrm((DEPTH, D), 0.02),
        'final_g': 1.0 + nrm((D,), 0.02),
        'attn_w_qkv': nrm((n_attn, D, qkv_w), D ** -0.5),
        'attn_w_o': nrm((n_attn, N_HEADS * HEAD_DIM, D), D ** -0.5),
        'attn_q_gain': 1.0 + nrm((n_attn, HEAD_DIM), 0.02),
        'attn_k_gain': 1.0 + nrm((n_attn, HEAD_DIM), 0.02),
        'hy_w_in': nrm((n_hy, D, 3 * D), D ** -0.5),
        'hy_conv_w': nrm((n_hy, 3, 3 * D), 3 ** -0.5),
        'hy_conv_b': nrm((n_hy, 3 * D), 0.02),
        'hy_f_w1': nrm((n_hy, HY_EMB_DIM, HY_FILTER_WIDTH), HY_EMB_DIM ** -0.5),
        'hy_f_b1': nrm((n_hy, HY_FILTER_WIDTH), 0.1),
        'hy_f_w2': nrm((n_hy, HY_FILTER_WIDTH, HY_FILTER_WIDTH), HY_FILTER_WIDTH ** -0.5),
        'hy_f_b2': nrm((n_hy, HY_FILTER_WIDTH), 0.1),
        'hy_f_w3': nrm((n_hy, HY_FILTER_WIDTH, HY_ORDER * 2 * D), HY_FILTER_WIDTH ** -0.5),
        'hy_f_freq': 1.0 + nrm((n_hy, HY_FILTER_WIDTH), 0.02),
        'hy_skip': nrm((n_hy, HY_ORDER, D), 1.0),
        'hy_w_out': nrm((n_hy, D, D), D ** -0.5),
        's5_A_re': -0.5 + nrm((n_s5, 2, G, P), 0.01),
        's5_A_im': math.pi * jnp.arange(P, dtype=f32) + nrm((n_s5, 2, G, P), 0.01),
        's5_log_dt': jax.random.uniform(next(ks), (n_s5, 2, G), f32, math.log(S5_DT_MIN), math.log(S5_DT_MAX)),
        's5_B_re': nrm((n_s5, 2, G, P, Hg), (2 * Hg) ** -0.5),
        's5_B_im': nrm((n_s5, 2, G, P, Hg), (2 * Hg) ** -0.5),
        's5_C_re': nrm((n_s5, 2, G, Hg, P), (2 * P) ** -0.5),
        's5_C_im': nrm((n_s5, 2, G, Hg, P), (2 * P) ** -0.5),
        's5_D': nrm((n_s5, D), 1.0),
        's5_w_glu': nrm((n_s5, D, 2 * D), D ** -0.5),
        'ffn_w_up': nrm((DEPTH, D, 2 * D_FF), D ** -0.5),
        'ffn_conv_w': nrm((DEPTH, 3, D_FF), 3 ** -0.5),
        'ffn_conv_b': nrm((DEPTH, D_FF), 0.02),
        'ffn_w_down': nrm((DEPTH, D_FF, D), D_FF ** -0.5),
    }

def first_block(x, c, ada_w, ada_b, norm1_g, norm2_g, final_g,
              attn_w_qkv, attn_w_o, attn_q_gain, attn_k_gain,
              hy_w_in, hy_conv_w, hy_conv_b, hy_f_w1, hy_f_b1, hy_f_w2, hy_f_b2, hy_f_w3, hy_f_freq,
              hy_skip, hy_w_out,
              s5_A_re, s5_A_im, s5_log_dt, s5_B_re, s5_B_im, s5_C_re, s5_C_im, s5_D, s5_w_glu,
              ffn_w_up, ffn_conv_w, ffn_conv_b, ffn_w_down):
    L = x.shape[1]
    cos, sin = axial_rope_tables(L)
    z, decay = hyena_pos_features(L)
    c_act = jax.nn.silu(c)
    for i in range(DEPTH):
        m, j = i % N_MIXERS, i // N_MIXERS
        mod = (c_act @ ada_w[i] + ada_b[i])[:, None, :]
        sh1, sc1, g1, sh2, sc2, g2 = jnp.split(mod, 6, axis=-1)
        h = rmsnorm(x, norm1_g[i]) * (1.0 + sc1) + sh1
        if m == 0:
            y = attention_mixer(h, attn_w_qkv[j], attn_w_o[j], attn_q_gain[j], attn_k_gain[j], cos, sin)
        elif m == 1:
            y = hyena_mixer(h, hy_w_in[j], hy_conv_w[j], hy_conv_b[j], hy_f_w1[j], hy_f_b1[j],
                            hy_f_w2[j], hy_f_b2[j], hy_f_w3[j], hy_f_freq[j], hy_skip[j], hy_w_out[j],
                            z, decay)
        else:
            y = s5_mixer(h, s5_A_re[j], s5_A_im[j], s5_log_dt[j], s5_B_re[j], s5_B_im[j],
                         s5_C_re[j], s5_C_im[j], s5_D[j], s5_w_glu[j])
        x = x + g1 * y
        h = rmsnorm(x, norm2_g[i]) * (1.0 + sc2) + sh2
        x = x + g2 * conv_ffn(h, ffn_w_up[i], ffn_conv_w[i], ffn_conv_b[i], ffn_w_down[i])
    return rmsnorm(x, final_g)


DEPTH_2 = 1

HEAD_DIM_2 = 64
N_HEADS_SWA = D_MODEL // (2 * HEAD_DIM_2)
N_KV_SWA = max(1, N_HEADS_SWA // 4)
N_HEADS_FOX = D_MODEL // (2 * HEAD_DIM_2)
WINDOW = 128
BLOCK = 128
D_FF_2 = ((8 * D_MODEL // 3 + 127) // 128) * 128
CONV_WIDTH = 3
NEG = -1e30

Q_A = N_HEADS_SWA * HEAD_DIM_2
KV_A = N_KV_SWA * HEAD_DIM_2
Q_B = N_HEADS_FOX * HEAD_DIM_2
F_B = N_HEADS_FOX
D_IN = Q_A + 2 * KV_A + 3 * Q_B + F_B
D_MIX = Q_A + Q_B


def rms_norm(x, g):
    xf = x.astype(jnp.float32)
    y = xf * lax.rsqrt(jnp.mean(xf * xf, axis=-1, keepdims=True) + EPS)
    return (y * g.astype(jnp.float32)).astype(x.dtype)

def modulate(h, shift, scale):
    return h * (1 + scale[:, None, :]) + shift[:, None, :]

def alibi_slopes(n_heads):
    return jnp.exp2(-8.0 * (jnp.arange(n_heads, dtype=jnp.float32) + 1) / n_heads)

def swa_attention(q, k, v, sinks):
    B, S, H, D = q.shape
    Hkv = k.shape[2]
    G = H // Hkv
    nb = S // BLOCK
    qb = q.reshape(B, nb, BLOCK, Hkv, G, D)

    def band(t):
        prev = jnp.pad(t[:, :S - BLOCK], ((0, 0), (BLOCK, 0), (0, 0), (0, 0)))
        return jnp.concatenate([prev.reshape(B, nb, BLOCK, Hkv, D),
                                t.reshape(B, nb, BLOCK, Hkv, D)], axis=2)

    kb, vb = band(k), band(v)
    scores = jnp.einsum('bnqhgd,bnkhd->bnhgqk', qb, kb).astype(jnp.float32) * (HEAD_DIM_2 ** -0.5)
    n_idx = jnp.arange(nb)[:, None, None]
    q_idx = jnp.arange(BLOCK)[None, :, None]
    k_idx = jnp.arange(2 * BLOCK)[None, None, :]
    dist = (BLOCK + q_idx) - k_idx
    key_abs = n_idx * BLOCK - BLOCK + k_idx
    valid = (dist >= 0) & (dist < WINDOW) & (key_abs >= 0)
    slopes = alibi_slopes(H).reshape(Hkv, G)[:, :, None, None]
    scores = scores - slopes * dist[0].astype(jnp.float32)
    scores = jnp.where(valid[None, :, None, None], scores, NEG)
    sink = sinks.astype(jnp.float32).reshape(Hkv, G)[:, :, None, None]
    m = jnp.maximum(scores.max(axis=-1, keepdims=True), sink)
    p = jnp.exp(scores - m)
    probs = p / (p.sum(axis=-1, keepdims=True) + jnp.exp(sink - m))
    out = jnp.einsum('bnhgqk,bnkhd->bnqhgd', probs.astype(v.dtype), vb)
    return out.reshape(B, S, H, D)

def forgetting_attention(q, k, v, f_logit):
    B, S, H, D = q.shape
    nb = S // BLOCK
    F = jnp.cumsum(jax.nn.log_sigmoid(f_logit.astype(jnp.float32)), axis=1)
    Fk = F.transpose(0, 2, 1)
    qb = q.reshape(B, nb, BLOCK, H, D).transpose(1, 0, 2, 3, 4)
    Fq = Fk.reshape(B, H, nb, BLOCK).transpose(2, 0, 1, 3)
    k_pos = jnp.arange(S)

    def one_block(args):
        qi, Fi, n = args
        s = jnp.einsum('bqhd,bkhd->bhqk', qi, k).astype(jnp.float32) * (HEAD_DIM_2 ** -0.5)
        s = s + (Fi[..., None] - Fk[:, :, None, :])
        q_pos = n * BLOCK + jnp.arange(BLOCK)
        s = jnp.where(k_pos[None, :] <= q_pos[:, None], s, NEG)
        p = jax.nn.softmax(s, axis=-1)
        return jnp.einsum('bhqk,bkhd->bqhd', p.astype(v.dtype), v)

    out = lax.map(one_block, (qb, Fq, jnp.arange(nb)))
    return out.transpose(1, 0, 2, 3, 4).reshape(B, S, H, D)

def causal_dwconv(u, w, b):
    C = u.shape[-1]
    y = lax.conv_general_dilated(u, w[:, None, :], window_strides=(1,),
                                 padding=[(CONV_WIDTH - 1, 0)],
                                 dimension_numbers=('NWC', 'WIO', 'NWC'),
                                 feature_group_count=C)
    return y + b

def hybrid_mixer(h, w_in, b_f, sinks, w_out):
    B, S, _ = h.shape
    z = h @ w_in
    o = 0
    qa = z[..., o:o + Q_A].reshape(B, S, N_HEADS_SWA, HEAD_DIM_2); o += Q_A
    ka = z[..., o:o + KV_A].reshape(B, S, N_KV_SWA, HEAD_DIM_2); o += KV_A
    va = z[..., o:o + KV_A].reshape(B, S, N_KV_SWA, HEAD_DIM_2); o += KV_A
    qb = z[..., o:o + Q_B].reshape(B, S, N_HEADS_FOX, HEAD_DIM_2); o += Q_B
    kb = z[..., o:o + Q_B].reshape(B, S, N_HEADS_FOX, HEAD_DIM_2); o += Q_B
    vb = z[..., o:o + Q_B].reshape(B, S, N_HEADS_FOX, HEAD_DIM_2); o += Q_B
    fb = z[..., o:o + F_B] + b_f
    ya = swa_attention(qa, ka, va, sinks).reshape(B, S, Q_A)
    yb = forgetting_attention(qb, kb, vb, fb).reshape(B, S, Q_B)
    return jnp.concatenate([ya, yb], axis=-1) @ w_out

def conv_glu_mlp(h, w_up, conv_w, conv_b, w_down):
    u = causal_dwconv(h @ w_up, conv_w, conv_b)
    a, g = jnp.split(u, 2, axis=-1)
    return (jax.nn.silu(g) * a) @ w_down

def second_inputs(seed: int = 0) -> dict:
    key = jax.random.key(seed)
    ks = jax.random.split(key, 16)
    f32 = jnp.float32
    nrm = lambda k, shp, s: jax.random.normal(k, shp, f32) * s
    return {
        "x": nrm(ks[0], (BATCH, SEQ, D_MODEL), 1.0),
        "c": nrm(ks[1], (BATCH, D_MODEL), 1.0),
        "w_ada": nrm(ks[2], (D_MODEL, 6 * D_MODEL), 0.5 * D_MODEL ** -0.5),
        "b_ada": nrm(ks[3], (6 * D_MODEL,), 0.02),
        "g_attn": 1.0 + nrm(ks[4], (D_MODEL,), 0.05),
        "w_in": nrm(ks[5], (D_MODEL, D_IN), D_MODEL ** -0.5),
        "b_f": 2.0 + nrm(ks[6], (N_HEADS_FOX,), 0.5),
        "sinks": nrm(ks[7], (N_HEADS_SWA,), 0.5),
        "w_out": nrm(ks[8], (D_MIX, D_MODEL), D_MIX ** -0.5),
        "g_mlp": 1.0 + nrm(ks[9], (D_MODEL,), 0.05),
        "w_up": nrm(ks[10], (D_MODEL, 2 * D_FF_2), D_MODEL ** -0.5),
        "conv_w": nrm(ks[11], (CONV_WIDTH, 2 * D_FF_2), CONV_WIDTH ** -0.5),
        "conv_b": nrm(ks[12], (2 * D_FF_2,), 0.02),
        "w_down": nrm(ks[13], (D_FF_2, D_MODEL), D_FF_2 ** -0.5),
        "g_final": 1.0 + nrm(ks[14], (D_MODEL,), 0.05),
    }

def second_block(x, c, w_ada, b_ada, g_attn, w_in, b_f, sinks, w_out,
              g_mlp, w_up, conv_w, conv_b, w_down, g_final):
    mod = jax.nn.silu(c) @ w_ada + b_ada
    sh1, sc1, ga1, sh2, sc2, ga2 = jnp.split(mod, 6, axis=-1)
    for _ in range(DEPTH_2):
        h = modulate(rms_norm(x, g_attn), sh1, sc1)
        x = x + ga1[:, None, :] * hybrid_mixer(h, w_in, b_f, sinks, w_out)
        h2 = modulate(rms_norm(x, g_mlp), sh2, sc2)
        x = x + ga2[:, None, :] * conv_glu_mlp(h2, w_up, conv_w, conv_b, w_down)
    return rms_norm(x, g_final)


def setup_inputs(seed=0):
    out = dict(first_inputs(seed))
    for name, value in second_inputs(seed + 1).items():
        if name != "x":
            out[name + "_2"] = value
    return out


def reference(
    x, c, ada_w, ada_b, norm1_g, norm2_g, final_g, attn_w_qkv, attn_w_o, attn_q_gain,
    attn_k_gain, hy_w_in, hy_conv_w, hy_conv_b, hy_f_w1, hy_f_b1, hy_f_w2, hy_f_b2, hy_f_w3,
    hy_f_freq, hy_skip, hy_w_out, s5_A_re, s5_A_im, s5_log_dt, s5_B_re, s5_B_im, s5_C_re,
    s5_C_im, s5_D, s5_w_glu, ffn_w_up, ffn_conv_w, ffn_conv_b, ffn_w_down, c_2, w_ada_2,
    b_ada_2, g_attn_2, w_in_2, b_f_2, sinks_2, w_out_2, g_mlp_2, w_up_2, conv_w_2, conv_b_2,
    w_down_2, g_final_2,
):
    x = first_block(
        x, c, ada_w, ada_b, norm1_g, norm2_g, final_g, attn_w_qkv, attn_w_o, attn_q_gain,
        attn_k_gain, hy_w_in, hy_conv_w, hy_conv_b, hy_f_w1, hy_f_b1, hy_f_w2, hy_f_b2, hy_f_w3,
        hy_f_freq, hy_skip, hy_w_out, s5_A_re, s5_A_im, s5_log_dt, s5_B_re, s5_B_im, s5_C_re,
        s5_C_im, s5_D, s5_w_glu, ffn_w_up, ffn_conv_w, ffn_conv_b, ffn_w_down,
    )
    return second_block(
        x, c_2, w_ada_2, b_ada_2, g_attn_2, w_in_2, b_f_2, sinks_2, w_out_2, g_mlp_2, w_up_2,
        conv_w_2, conv_b_2, w_down_2, g_final_2,
    )


_drawn_inputs = setup_inputs


def setup_inputs(seed=0):
    import zlib

    import numpy as np

    out = dict(_drawn_inputs(seed))
    spreads = {}
    factors = {'norm1_g': 4.119,
     'norm2_g': 6.176,
     'final_g': 2.676,
     'attn_q_gain': 8.0,
     'attn_k_gain': 8.0,
     'hy_conv_b': 4.703,
     'hy_f_b1': 4.968,
     'hy_f_b2': 3.024,
     'hy_f_freq': 8.0,
     'ffn_conv_b': 8.0,
     'g_attn_2': 6.253,
     'sinks_2': 198.89,
     'g_mlp_2': 3.548,
     'conv_b_2': 8.0}
    for name, (base, spread) in spreads.items():
        noise = np.random.default_rng([zlib.crc32(name.encode()), seed]).standard_normal(out[name].shape)
        drawn = base * np.exp(spread * noise) if base else spread * noise
        out[name] = __import__('jax').numpy.asarray(drawn.astype(out[name].dtype))
    for name, factor in factors.items():
        out[name] = (out[name] * factor).astype(out[name].dtype)
    return out
```

```python
import math

import concourse.bass as bass
import numpy as np
from concourse import mybir
from concourse.alu_op_type import AluOpType as ALU

F32 = mybir.dt.float32
F32R = mybir.dt.float32r
ACT = mybir.ActivationFunctionType
AX = mybir.AxisListType

P = 128
L = 512
D = 1024
KT = D // P
LT = L // P
FF = 2816
FT = FF // P
FH = FT // 2
EPS = 1e-6
HD = 64
HEADS = 16
KV_HEADS = 4
SWA_HEADS = 8
SWA_KV = 2
FOX_HEADS = 8
WINDOW = 128
NEG = -1e30
SCALE = HD ** -0.5
GRID_W = 64
ORDERS = 2
EMB = 33
FW = 64
CH = 256
NCH = D // CH
TWO_PI = 2.0 * math.pi
TWO_PI_HI = 6.28125
TWO_PI_LO = float(np.float32(TWO_PI - TWO_PI_HI))
ROUND = 1.5 * 2.0 ** 23
PI_BELOW = 3.1415925

VECTORS = [
    ("c", KT), ("c_2", KT), ("ada_b", 2 * 6 * KT), ("b_ada_2", 6 * KT),
    ("norm1_g", 2 * KT), ("norm2_g", 2 * KT), ("final_g", KT),
    ("g_attn_2", KT), ("g_mlp_2", KT), ("g_final_2", KT),
    ("ffn_conv_w", 2 * 3 * FT), ("ffn_conv_b", 2 * FT),
    ("hy_conv_w", 3 * 3 * KT), ("hy_conv_b", 3 * KT), ("hy_skip", ORDERS * KT),
    ("conv_w_2", 3 * 2 * FT), ("conv_b_2", 2 * FT),
]
COL = {}
_at = 0
for _name, _n in VECTORS:
    COL[_name] = _at
    _at += _n
VECTOR_ROWS = _at
PT_TILES = -(-VECTOR_ROWS // P)
SHORT = ["attn_q_gain", "attn_k_gain", "hy_f_b1", "hy_f_b2", "hy_f_freq"]


def shape_constants():
    out = {}
    n = np.arange(L, dtype=np.float64)
    w = 2.0 * np.pi * (n + 0.5) / (2 * L)
    kern = np.outer(n, w)
    sig = np.outer(n + 0.5, w)
    out["dft_kernel"] = np.stack([np.cos(kern), np.sin(kern)]).astype(np.float32)
    out["dft_signal"] = np.stack([np.cos(sig), np.sin(sig)]).astype(np.float32)
    t = np.linspace(0.0, 1.0, L, dtype=np.float32)
    bands = (EMB - 1) // 2
    wl = (np.float32(2.0 * math.pi) * np.arange(L, dtype=np.float32) / np.float32(L)).astype(np.float32)
    f = np.linspace(1e-4, bands - 1, bands, dtype=np.float32)
    ang = (wl[:, None] * f[None, :]).astype(np.float32).astype(np.float64)
    out["pos_t"] = np.concatenate([t[:, None], np.cos(ang), -np.sin(ang)], axis=1).astype(np.float32).T.copy()
    deltas = np.abs(np.linspace(math.log(1e-2) / 1.5, math.log(1e-2) / 0.3, D, dtype=np.float32))
    out["decay"] = np.exp(-(t[:, None] * deltas[None, :]).astype(np.float64)).astype(np.float32)
    nf = HD // 4
    inv = (np.float32(1.0) / (np.float32(10000.0) ** (np.arange(nf, dtype=np.float32) / np.float32(nf)))).astype(np.float32)
    tok = np.arange(L)
    row = (tok // GRID_W).astype(np.float32)[:, None] * inv
    col = (tok % GRID_W).astype(np.float32)[:, None] * inv
    a = np.concatenate([row, col], axis=1).astype(np.float32).astype(np.float64)
    per_channel = np.repeat(a, 2, axis=1).T
    both = np.concatenate([per_channel, per_channel], axis=0)
    out["rope"] = np.stack([np.cos(both), np.sin(both)]).astype(np.float32)
    perm = np.zeros((P, P), np.float32)
    for m in range(0, P, 2):
        perm[m + 1, m] = -1.0
        perm[m, m + 1] = 1.0
    out["swap"] = perm
    out["identity"] = np.eye(P, dtype=np.float32)
    head_mean = np.zeros((P, 2), np.float32)
    head_mean[:HD, 0] = 1.0 / HD
    head_mean[HD:, 1] = 1.0 / HD
    out["head_mean"] = head_mean
    q = np.arange(P)[:, None]
    k = np.arange(2 * P)[None, :]
    dist = (P + q) - k
    valid = (dist >= 0) & (dist < WINDOW)
    slopes = np.exp2(-8.0 * (np.arange(SWA_HEADS, dtype=np.float32) + 1) / SWA_HEADS)
    b = -slopes[None, :, None] * dist[:, None, :].astype(np.float32)
    out["alibi"] = np.where(valid[:, None, :], b, np.float32(NEG)).astype(np.float32)
    out["causal"] = np.where(np.arange(P)[None, :] <= q, 0.0, NEG).astype(np.float32)
    return out


def build_program(nc, A, C, out):
    CONST0 = 16512
    X0 = CONST0 + 8192
    HH0 = X0 + KT * L * 4
    HL0 = HH0 + KT * L * 4
    UNIT = 2 * KT * P
    RAW0 = HL0 + KT * L * 4
    HI0 = RAW0 + 2 * UNIT * 4
    LO0 = HI0 + 2 * UNIT * 4
    AREA = LO0 + 2 * UNIT * 4
    TOP = 229344
    TRIPLE = 3 * D
    ADA0 = (TOP - 3 * TRIPLE * 4) // 32 * 32

    def at(name, offset, shape, dt=F32):
        return nc.alloc_sbuf_tensor_at(name, shape, dt, offset=offset)

    def sizeof(shape):
        return 4 * int(np.prod(shape[1:]))

    def region(start, *wanted):
        made = []
        for name, shape, dt in wanted:
            made.append(at(name, start, shape, dt))
            start += (sizeof(shape) + 31) // 32 * 32
            assert start <= TOP, name
        return made

    (ident, ones, eps_col, vec, mod, gsc, silu_c, head_mean, swap_m, gain_cols, fcols, rms_cols, rstd_cols,
     mxs, nmx, sums, recs, es, bf_col, sink_b, nrm_cols) = region(
        CONST0,
        ("ident", [P, P], F32), ("ones_col", [P, 2], F32), ("eps_col", [P, 1], F32),
        ("vec", [P, VECTOR_ROWS], F32), ("mod", [P, 3, 6 * KT], F32), ("gsc", [P, 3, 2, KT], F32),
        ("silu_c", [P, 2, KT], F32), ("head_mean", [P, 2], F32), ("swap_m", [P, P], F32),
        ("gain_cols", [P, 2], F32), ("fcols", [FW, 3], F32), ("rms_cols", [P, 2, 8], F32),
        ("rstd_cols", [P, 2, 8], F32), ("mxs", [P, 4], F32), ("nmx", [P, 4], F32), ("sums", [P, 4], F32),
        ("recs", [P, 4], F32), ("es", [P, 4], F32), ("bf_col", [FOX_HEADS, 1], F32),
        ("sink_b", [P, SWA_HEADS], F32), ("nrm_cols", [P, 4], F32))
    x = at("x_res", X0, [P, KT, L])
    hh = at("h_hi", HH0, [P, KT, L], F32R)
    hl = at("h_lo", HL0, [P, KT, L], F32R)
    raw = [at(f"w_raw{i}", RAW0 + i * UNIT * 4, [P, UNIT]) for i in range(2)]
    whi = [at(f"w_hi{i}", HI0 + i * UNIT * 4, [P, UNIT], F32R) for i in range(2)]
    wlo = [at(f"w_lo{i}", LO0 + i * UNIT * 4, [P, UNIT], F32R) for i in range(2)]
    ada_raw = [at(f"ada_raw{i}", ADA0 + i * TRIPLE * 4, [P, TRIPLE]) for i in range(2)]
    ada_acc = at("ada_acc", ADA0 + 2 * TRIPLE * 4, [P, TRIPLE])
    bank = [nc.alloc_psum_tensor(f"bank{i}", [P, 512], F32) for i in range(8)]

    spectra = nc.dram_tensor("spectra", (ORDERS, NCH, P, LT, 2, CH), F32).ap()

    vec_raw = at("vec_raw", X0, [P, PT_TILES, P])
    sum_f, dif_f = region(X0, ("sum_f", [P, LT, 512], F32), ("dif_f", [P, LT, 512], F32))
    decay = at("decay_sb", HH0, [P, LT, D])
    fw3 = at("fw3", HL0, [FW, 4 * D])
    fwd, bwd, afwd, abwd, asum, spec_out, rn_row, zt, a1, a2, fw1, fw2 = region(
        HI0, ("fwd", [P, 2, 512], F32), ("bwd", [P, 2, 512], F32), ("afwd", [P, 512], F32),
        ("abwd", [P, 512], F32), ("asum", [P, 2, 512], F32), ("spec_out", [P, 2, 512], F32),
        ("rn_row", [P, 512], F32), ("pos_sb", [EMB, L], F32), ("a1", [FW, L], F32),
        ("a2", [FW, L], F32), ("fw1", [EMB, FW], F32), ("fw2", [FW, FW], F32))
    tk_h, tk_l, sum_h, sum_l, dif_h, dif_l = region(
        AREA, ("tk_h", [P, 2, LT, 512], F32R), ("tk_l", [P, 2, LT, 512], F32R),
        ("sum_h", [P, LT, 512], F32R), ("sum_l", [P, LT, 512], F32R),
        ("dif_h", [P, LT, 512], F32R), ("dif_l", [P, LT, 512], F32R))
    assert AREA + 65536 <= ADA0
    arg, turns = region(AREA + 32768, ("sin_arg", [FW, L], F32), ("sin_turns", [FW, L], F32))
    x_rows = at("x_rows", HH0, [P, LT, D])

    NORM0 = AREA + 57344
    nsq, nt1, nacc = region(NORM0, ("norm_sq", [P, 2, 512], F32), ("norm_t", [P, 2, 512], F32),
                            ("norm_sum", [P, 512], F32))
    assert NORM0 + 10240 <= ADA0

    qh, kh, vh, rope, qsq, qf, qt = region(
        AREA, ("q_heads", [HD, HEADS, L], F32), ("k_heads", [HD, KV_HEADS, L], F32),
        ("v_rows", [P, LT, KV_HEADS * HD], F32), ("rope_sb", [P, 2, L], F32),
        ("q_sq", [P, 2, 512], F32), ("q_f", [P, 2, 512], F32), ("q_t", [P, 2, 512], F32))
    rx, = region(AREA + 61440, ("head_factors", [P, 2, 512], F32))
    assert AREA + 65536 <= ADA0
    probs1, = region(AREA + 45056, ("probs1", [P, 2, 512], F32))
    probsT1, = region(AREA + 49152, ("probsT1", [P, 2, LT, 512], F32))

    hid_h, hid_l, fc, fs, fh = region(
        AREA, ("hid_h", [P, FH, L], F32R), ("hid_l", [P, FH, L], F32R), ("conv_g", [P, 2, L], F32),
        ("silu_g", [P, 2, L], F32), ("hid_f", [P, 2, L], F32))
    fv, = region(AREA + 69632, ("conv_v", [P, 2, L], F32))

    u, td_h, td_l, y_h, y_l, pt1, y_f = region(
        AREA, ("hyena_u", [P, 3 * KT, L], F32), ("td_h", [P, 2, LT, 512], F32R), ("td_l", [P, 2, LT, 512], F32R),
        ("y_h", [P, LT, 2, CH], F32R), ("y_l", [P, LT, 2, CH], F32R), ("pt1", [P, 2, CH], F32),
        ("y_f", [P, 2, CH], F32))
    pt2, = region(CONST0 + 8192 - 2048, ("pt2", [P, 2, CH], F32))
    z_h = at("z_hi", AREA + KT * L * 4, [P, KT, L], F32R)
    z_l = at("z_lo", AREA + 2 * KT * L * 4, [P, KT, L], F32R)
    zt_h = hh[:].rearrange("p a b -> p (a b)").rearrange("p (n c) -> p n c", n=LT)
    zt_l = hl[:].rearrange("p a b -> p (a b)").rearrange("p (n c) -> p n c", n=LT)

    qa, ka, va, qfx, kfx, vfx, alibi, causal, probs2, probsT2, biased = region(
        AREA, ("qa", [HD, SWA_HEADS, L], F32), ("ka", [HD, SWA_KV, L], F32), ("va", [P, LT, SWA_KV * HD], F32),
        ("qfx", [HD + 2, FOX_HEADS, L], F32), ("kfx", [HD + 2, FOX_HEADS, L], F32),
        ("vfx", [P, LT, FOX_HEADS * HD], F32), ("alibi_sb", [P, SWA_HEADS, 2 * P], F32),
        ("causal_sb", [P, P], F32), ("probs2", [P, 2, 512], F32), ("probsT2", [P, 2, LT, 512], F32),
        ("biased", [P, 2, 2 * P], F32))
    wf, wf_h, wf_l, f_rows = region(
        CONST0 + 8192 - 2048, ("wf", [P, KT, FOX_HEADS], F32), ("wf_h", [P, KT, FOX_HEADS], F32R),
        ("wf_l", [P, KT, FOX_HEADS], F32R), ("f_rows", [P, LT * FOX_HEADS], F32))
    out_rows = at("out_rows", AREA, [P, LT, D])

    def sem(name):
        return nc.alloc_semaphore(name)

    def sems(prefix, names):
        return {n: sem(f"{prefix}_{n}") for n in names.split()}

    raw_in = [sem("raw_in0"), sem("raw_in1")]
    raw_done, hi_done, used = sem("raw_done"), sem("hi_done"), sem("units_used")
    ada_in = [sem("ada_in0"), sem("ada_in1")]
    ada_st, ada_mm, ada_ev = sem("ada_steps"), sem("ada_columns"), sem("ada_mods")
    prep = sems("prep", "small vecs consts x trans cols silu")
    sn = sems("sin", "pe chain act")
    fl = sems("filt", "in fb fbused fa as_ pm nmm nrec nbt nrow phi plo mhi mlo sp ev st")
    xs = sems("xload", "in pe ev")

    def load(sp, r, it, parts):
        if r >= 2:
            sp.wait_ge(raw_done, r - 1 + 2 * it)
        for dst, src in parts(raw[r % 2]):
            sp.dma_start(dst, src).then_inc(raw_in[r % 2], 16)

    def split_hi(act, r, s, it, n):
        act.wait_ge(raw_in[r % 2], 32 * (r // 2 + 1) + 32 * it)
        if s >= 2:
            act.wait_ge(used, s - 1 + 2 * it)
        nc.scalar.activation(whi[s % 2][:, :n], raw[r % 2][:, :n], ACT.Copy).then_inc(hi_done, 1)

    def split_lo(dve, r, s, it, n):
        dve.wait_ge(hi_done, s + 1 + 2 * it)
        nc.vector.tensor_tensor(wlo[s % 2][:, :n], raw[r % 2][:, :n], whi[s % 2][:, :n].bitcast(F32),
                                ALU.subtract).then_inc(raw_done, 1)

    def three_pass(out_ap, lhs, rhs, first, last, check=True):
        nc.tensor.matmul(out_ap, lhs[0], rhs[0], start=first, stop=False)
        nc.tensor.matmul(out_ap, lhs[0], rhs[1], start=False, stop=False)
        return nc.tensor.matmul(out_ap, lhs[1], rhs[0], start=False, stop=last)

    def over(eng, n, body):
        pairs = n // 2
        if pairs > 1:
            with eng.Fori(0, pairs) as it:
                body(0, it)
                body(1, it)
        elif pairs == 1:
            body(0, 0)
            body(1, 0)
        if n % 2:
            body(n - 1, 0)

    def split_ahead(eng, split, n_units, r0, s0, n_el, nxt, body, take=2):
        def unit(c, it):
            split(eng, r0 + c + 2, s0 + c + 2, it, n_el)
            body(c, it)
        over(eng, n_units - 2, unit)
        for k in range(2):
            if nxt and k < take:
                split(eng, nxt[0] + k, nxt[1] + k, 0, nxt[2])
            body(n_units - 2 + k, 0)

    ring = {}
    r_at = s_at = 0
    for name, units, n_el, weights in (
            [("tk", 2, UNIT, False), ("qkv", 6, UNIT, True), ("wo", 4, UNIT, True)]
            + [(f"{k}0_{h}", FH if k == "up" else KT, UNIT if k == "up" else FH * P, True) for h in (0, 1) for k in ("up", "dn")]
            + [("hyin", 12, UNIT, True), ("td", 2, UNIT, False), ("spec", ORDERS * NCH, UNIT, False), ("hyout", 4, UNIT, True)]
            + [(f"{k}1_{h}", FH if k == "up" else KT, UNIT if k == "up" else FH * P, True) for h in (0, 1) for k in ("up", "dn")]
            + [("win", 9, UNIT, True), ("wout", 4, UNIT, True)]
            + [(f"{k}2_{h}", FH if k == "up" else KT, UNIT if k == "up" else FH * P, True) for h in (0, 1) for k in ("up", "dn")]):
        ring[name] = (r_at, s_at, n_el, units)
        r_at += units
        s_at += units if weights else 0

    def cols2(w, c0, it_step, it, c1=None):
        src = w.rearrange("(k p) n -> p k n", p=P)

        def parts(slot):
            v = slot[:].rearrange("p (k n) -> p k n", k=KT)
            if c1 is None:
                return [(v[:, k:k + KT // 2, :], src[:, k:k + KT // 2, bass.ds(c0 + it_step * it, 2 * P)])
                        for k in (0, KT // 2)]
            return [(v[:, :, 0:P], src[:, :, bass.ds(c0 + it_step * it, P)]),
                    (v[:, :, P:2 * P], src[:, :, bass.ds(c1 + it_step * it, P)])]
        return parts

    def down_parts(w, half, c, it):
        src = w[half * FH * P:(half + 1) * FH * P, :].rearrange("(k p) n -> p k n", p=P)

        def parts(slot):
            v = slot[:, :FH * P].rearrange("p (k n) -> p k n", k=FH)
            return [(v[:, a:b, :], src[:, a:b, bass.ds(c * P + 2 * P * it, P)]) for a, b in ((0, 6), (6, FH))]
        return parts

    def slot_w(s):
        return (whi[s % 2][:].rearrange("p (k n) -> p k n", k=KT), wlo[s % 2][:].rearrange("p (k n) -> p k n", k=KT))

    def slot_d(s):
        return tuple(w[s % 2][:, :FH * P].rearrange("p (k n) -> p k n", k=FH) for w in (whi, wlo))

    def col(name, i):
        return vec[:, COL[name] + i:COL[name] + i + 1]

    def dcol(name, i, it, step):
        if isinstance(it, int):
            return col(name, i + step * it)
        return vec[:, bass.ds(COL[name] + i + step * it, 1)]

    def tile_of(t, i, it, step, sl=slice(None)):
        if isinstance(it, int):
            return t[:, i + step * it, sl]
        return t[:, bass.ds(i + step * it, 1), sl].rearrange("p a n -> p (a n)")

    def ada_source(T, c, it):
        w = A["ada_w"][T // 2] if T < 4 else A["w_ada_2"]
        return w[bass.ds(c * P + 2 * P * it, P), (T % 2) * TRIPLE:(T % 2 + 1) * TRIPLE]

    def ada_load_one(pool, T, c, it):
        if c >= 2:
            pool.wait_ge(ada_st, 9 * T + c + 2 * it)
        elif T:
            pool.wait_ge(ada_st, 9 * T - 1 + c)
        pool.dma_start(ada_raw[c % 2][:], ada_source(T, c, it)).then_inc(ada_in[c % 2], 16)

    def ada_load_first(pool, T):
        ada_load_one(pool, T, 0, 0)
        ada_load_one(pool, T, 1, 0)

    def ada_load_rest(pool, T):
        with pool.Fori(0, KT // 2 - 1) as it:
            ada_load_one(pool, T, 2, it)
            ada_load_one(pool, T, 3, it)

    def ada_zero(dve, T):
        if T:
            dve.wait_ge(ada_mm, T)
        nc.vector.memset(ada_acc[:], 0.0).then_inc(ada_st, 1)

    def ada_step(dve, T, c, it):
        dve.wait_ge(ada_in[c % 2], 16 * (4 * T + c // 2 + 1) + 16 * it)
        dve.wait_ge(ada_st, 9 * T + 1 + c + 2 * it)
        which = T // 4
        s = silu_c[:, which, c:c + 1] if isinstance(it, int) else silu_c[:, which, bass.ds(c + 2 * it, 1)]
        nc.vector.scalar_tensor_tensor(ada_acc[:], ada_raw[c % 2][:], s, ada_acc[:], ALU.mult, ALU.add)\
          .then_inc(ada_st, 1)

    def ada_columns(pe, T):
        pe.wait_ge(ada_st, 9 * T + 9)
        for i in range(3 * KT):
            last = nc.tensor.matmul(bank[6][:, i:i + 1], ada_acc[:, i * P:(i + 1) * P], ones[:, 0:1], start=True, stop=True)
        last.then_inc(ada_mm, 1)

    def ada_mods(dve, T):
        dve.wait_ge(ada_mm, T + 1)
        b, h = T // 2, T % 2
        bias = COL["ada_b"] + T * 3 * KT if T < 4 else COL["b_ada_2"] + h * 3 * KT
        gain = (COL["norm1_g"] if h == 0 else COL["norm2_g"]) + b * KT if b < 2 else \
            COL["g_attn_2"] if h == 0 else COL["g_mlp_2"]
        m = mod[:, b, h * 3 * KT:(h + 1) * 3 * KT]
        nc.vector.tensor_tensor(m, bank[6][:, 0:3 * KT], vec[:, bias:bias + 3 * KT], ALU.add).then_inc(ada_ev, 1)
        dve.wait_ge(ada_ev, 2 * T + 1)
        nc.vector.scalar_tensor_tensor(gsc[:, b, h, :], m[:, KT:2 * KT], 1.0, vec[:, gain:gain + KT],
                                       ALU.add, ALU.mult).then_inc(ada_ev, 1)

    vec_pieces = []
    for name, n in VECTORS:
        rows = A[name]
        rows = rows.rearrange(" ".join("abcd"[:len(rows.shape)]) + " -> (" + " ".join("abcd"[:len(rows.shape)]) + ")") \
            if len(rows.shape) > 1 else rows
        rows = rows.rearrange("(r p) -> r p", p=P)
        done = 0
        while done < n:
            g = COL[name] + done
            take = min(n - done, P - g % P)
            vec_pieces.append((vec_raw[g % P:g % P + take, g // P, :], rows[done:done + take, :]))
            done += take

    def column(name):
        a = A[name]
        return a.rearrange("a p -> p a") if len(a.shape) == 2 else a.rearrange("(p a) -> p a", a=1)

    SMALL = [(ident[:], C["identity"]), (head_mean[:], C["head_mean"]), (swap_m[:], C["swap"]),
             (gain_cols[0:HD, 0:1], column("attn_q_gain")), (gain_cols[HD:P, 0:1], column("attn_q_gain")),
             (gain_cols[0:HD, 1:2], column("attn_k_gain")), (gain_cols[HD:P, 1:2], column("attn_k_gain")),
             (bf_col[:], column("b_f_2")),
             (sink_b[:], A["sinks_2"].rearrange("(a h) -> a h", a=1).broadcast_to([P, SWA_HEADS]))]
    FIRST = [(zt[:], C["pos_t"]), (fw1[:], A["hy_f_w1"][0]), (fw2[:], A["hy_f_w2"][0]),
             (fcols[:, 0:1], column("hy_f_b1")), (fcols[:, 1:2], column("hy_f_b2")), (fcols[:, 2:3], column("hy_f_freq"))]
    FILT = [(fw3[:], A["hy_f_w3"][0]), (decay[:], C["decay"].rearrange("(t p) d -> p t d", p=P))]

    def table_parts(table, part):
        src = C[table][part].rearrange("(t p) k -> p t k", p=P)

        def parts(slot):
            v = slot[:].rearrange("p (t k) -> p t k", t=LT)
            return [(v[:, t:t + 2, :], src[:, t:t + 2, :]) for t in (0, 2)]
        return parts

    def prep_sp(sp):
        for dst, src in vec_pieces:
            sp.dma_start(dst, src).then_inc(prep["vecs"], 16)
        for part in range(2):
            load(sp, ring["tk"][0] + part, 0, table_parts("dft_kernel", part))
        for dst, src in FILT:
            sp.dma_start(dst, src).then_inc(fl["in"], 16)

    def prep_act(act):
        for dst, src in FIRST:
            act.dma_start(dst, src).then_inc(prep["small"], 16)
        for dst, src in SMALL:
            act.dma_start(dst, src).then_inc(prep["consts"], 16)

    def prep_dve(dve):
        nc.vector.memset(ones[:], 1.0)
        nc.vector.memset(eps_col[:], EPS).then_inc(prep["cols"], 1)
        dve.wait_ge(prep["trans"], 1)
        nc.vector.tensor_copy(vec[:, 0:4 * P], bank[6][:, 0:4 * P])
        nc.vector.tensor_copy(vec[:, 4 * P:VECTOR_ROWS], bank[7][:, 0:VECTOR_ROWS - 4 * P]).then_inc(prep["cols"], 1)

    def prep_pe(pe):
        pe.wait_ge(prep["vecs"], 16 * len(vec_pieces))
        pe.wait_ge(prep["consts"], 16 * len(SMALL))
        for t in range(PT_TILES):
            n = min(P, VECTOR_ROWS - t * P)
            last = nc.tensor.transpose(bank[6 + t // 4][:, (t % 4) * P:(t % 4) * P + n], vec_raw[0:n, t, :], ident[0:n, 0:n])
        last.then_inc(prep["trans"], 1)

    def silu_act(act):
        act.wait_ge(prep["cols"], 2)
        nc.scalar.activation(silu_c[:].rearrange("p a k -> p (a k)"), vec[:, COL["c"]:COL["c"] + 2 * KT], ACT.Silu)\
          .then_inc(prep["silu"], 1)

    def sin_pe(pe):
        pe.wait_ge(prep["small"], 16 * len(FIRST))
        nc.tensor.matmul(bank[0][0:FW, :], fw1[:], zt[:], start=True, stop=True).then_inc(sn["pe"], 1)
        pe.wait_ge(sn["act"], 1)
        nc.tensor.matmul(bank[1][0:FW, :], fw2[:], a1[:], start=True, stop=True).then_inc(sn["pe"], 1)

    def sin_dve(dve):
        n = 0
        for i in range(2):
            dve.wait_ge(sn["pe"], i + 1)
            for step in range(6):
                if n:
                    dve.wait_ge(sn["chain"], n)
                if step == 0:
                    if i:
                        dve.wait_ge(sn["act"], i)
                    ins = nc.vector.tensor_scalar(arg[:], bank[i][0:FW, :], fcols[:, i:i + 1], fcols[:, 2:3], ALU.add, ALU.mult)
                elif step == 1:
                    ins = nc.vector.tensor_scalar(turns[:], arg[:], 1.0 / TWO_PI, ROUND, ALU.mult, ALU.add)
                elif step == 2:
                    ins = nc.vector.tensor_scalar(turns[:], turns[:], ROUND, None, ALU.subtract)
                elif step == 3:
                    ins = nc.vector.scalar_tensor_tensor(arg[:], turns[:], -TWO_PI_HI, arg[:], ALU.mult, ALU.add)
                elif step == 4:
                    ins = nc.vector.scalar_tensor_tensor(arg[:], turns[:], -TWO_PI_LO, arg[:], ALU.mult, ALU.add)
                else:
                    ins = nc.vector.tensor_scalar(arg[:], arg[:], PI_BELOW, -PI_BELOW, ALU.min, ALU.max)
                ins.then_inc(sn["chain"], 1)
                n += 1

    def sin_act(act):
        for i, dst in enumerate((a1, a2)):
            act.wait_ge(sn["chain"], 6 * (i + 1))
            nc.scalar.activation(dst[:], arg[:], ACT.Sin).then_inc(sn["act"], 1)

    fl_st = [sem("filt_stored0"), sem("filt_stored1")]
    GROUPS = 2 * ORDERS
    tab_done = sem("tk_tables")

    def tables_act(act, name, hi):
        r0 = ring[name][0]
        for part in range(2):
            act.wait_ge(raw_in[(r0 + part) % 2], 32 * ((r0 + part) // 2 + 1))
            nc.scalar.activation(hi[:, part], raw[(r0 + part) % 2][:].rearrange("p (t k) -> p t k", t=LT), ACT.Copy)\
              .then_inc(tab_done, 1)

    def tables_dve(dve, name, hi, lo, before):
        r0 = ring[name][0]
        for part in range(2):
            dve.wait_ge(tab_done, before + part + 1)
            nc.vector.tensor_tensor(lo[:, part], raw[(r0 + part) % 2][:].rearrange("p (t k) -> p t k", t=LT),
                                    hi[:, part].bitcast(F32), ALU.subtract).then_inc(raw_done, 1)

    def filt_mm(pe, n):
        g, t = divmod(n, LT)
        o, dh = divmod(g, 2)
        if n >= 2:
            pe.wait_ge(fl["fbused"], n - 1)
        for d in range(2):
            c0 = (2 * o + d) * D + dh * 512
            ins = nc.tensor.matmul(bank[2 * (n % 2) + d][:], a2[:, t * P:(t + 1) * P], fw3[:, c0:c0 + 512], start=True, stop=True)
        ins.then_inc(fl["fb"], 1)

    def norm_mm(pe, n):
        pe.wait_ge(fl["fa"], n + 1)
        if n >= LT and n % LT == 0:
            pe.wait_ge(fl["nrec"], 2 * (n // LT))
        for b in range(4):
            ins = nc.tensor.matmul(bank[7][:, b:b + 1], asum[:, n % 2, b * P:(b + 1) * P], ones[:, 0:1],
                                   start=(n % LT == 0 and b == 0), stop=(n % LT == LT - 1), skip_group_check=True)
        ins.then_inc(fl["nmm"], 1)

    def norm_row_mm(pe, g):
        pe.wait_ge(fl["nrec"], 2 * g + 2)
        if g:
            pe.wait_ge(fl["nrow"], g)
        for b in range(4):
            ins = nc.tensor.transpose(bank[6][:, b * P:(b + 1) * P], nrm_cols[:, b:b + 1].broadcast_to([P, P]), ident[:])
        ins.then_inc(fl["nbt"], 1)

    def spectra_mm(pe, g, part, k):
        e = 8 * g + 4 * part + k
        if e >= 2:
            pe.wait_ge(fl["ev"], e - 1)
        src = ((sum_h, sum_l), (dif_h, dif_l))[part]
        for t in range(LT):
            if k == 0:
                pe.wait_ge(fl["mlo" if part else "plo"], LT * g + t + 1)
            ks = slice(k * P, (k + 1) * P)
            ins = three_pass(bank[4 + e % 2][:], (tk_h[:, part, t, ks], tk_l[:, part, t, ks]),
                             (src[0][:, t], src[1][:, t]), t == 0, t == LT - 1)
        ins.then_inc(fl["sp"], 1)

    def filter_pe(pe):
        pe.wait_ge(sn["act"], 2)
        pe.wait_ge(fl["in"], 32)
        for n in range(LT):
            filt_mm(pe, n)
        pe.wait_ge(raw_done, 2)
        for g in range(GROUPS):
            for t in range(LT):
                norm_mm(pe, LT * g + t)
            for part in range(2):
                for k in range(LT):
                    spectra_mm(pe, g, part, k)
                    if part == 0 and k == 0:
                        norm_row_mm(pe, g)
                    nxt = {(0, 1): 0, (0, 2): 1, (1, 0): 2, (1, 1): 3}.get((part, k))
                    if nxt is not None and g + 1 < GROUPS:
                        filt_mm(pe, LT * (g + 1) + nxt)

    def filter_dve(dve):
        chain = [0]
        step = sem("filt_zero_row")

        def fb(n):
            g, t = divmod(n, LT)
            dve.wait_ge(fl["fb"], n + 1)
            if n >= 2:
                dve.wait_ge(fl["pm"], n - 1)
                dve.wait_ge(fl["as_"], n - 1)
            dec = decay[:, t, (g % 2) * 512:(g % 2) * 512 + 512]
            nc.vector.tensor_tensor(fwd[:, n % 2], bank[2 * (n % 2)][:], dec, ALU.mult)
            ins = nc.vector.tensor_tensor(bwd[:, n % 2], bank[2 * (n % 2) + 1][:], dec, ALU.mult)
            if t == 0:
                ins.then_inc(step, 1)
                chain[0] += 1
                dve.wait_ge(step, chain[0])
                ins = nc.vector.memset(bwd[0:1, n % 2, :], 0.0)
            ins.then_inc(fl["fbused"], 1)

        def asum_(n):
            dve.wait_ge(fl["as_"], n + 1)
            if n >= 2:
                dve.wait_ge(fl["nmm"], n - 1)
            nc.vector.tensor_tensor(asum[:, n % 2], afwd[:], abwd[:], ALU.add).then_inc(fl["fa"], 1)

        def lo(n, part):
            dve.wait_ge(fl["mhi" if part else "phi"], n + 1)
            src, h, l_ = ((sum_f, sum_h, sum_l), (dif_f, dif_h, dif_l))[part]
            nc.vector.tensor_tensor(l_[:, n % LT], src[:, n % LT], h[:, n % LT].bitcast(F32), ALU.subtract)\
              .then_inc(fl["mlo" if part else "plo"], 1)

        def rec(g):
            dve.wait_ge(fl["nmm"], LT * (g + 1))
            nc.vector.reciprocal(nrm_cols[:], bank[7][:, 0:4]).then_inc(fl["nrec"], 1)
            dve.wait_ge(fl["nrec"], 2 * g + 1)
            nc.vector.tensor_scalar(nrm_cols[:], nrm_cols[:], 1.0 / L, None, ALU.mult).then_inc(fl["nrec"], 1)

        def ev(g, part, k):
            e = 8 * g + 4 * part + k
            dve.wait_ge(fl["sp"], e + 1)
            dve.wait_ge(fl["nrow"], g + 1)
            if e >= 2:
                dve.wait_ge(fl_st[e % 2], 16 * (e // 2))
            nc.vector.tensor_tensor(spec_out[:, e % 2], bank[4 + e % 2][:], rn_row[:], ALU.mult).then_inc(fl["ev"], 1)

        dve.wait_ge(fl["in"], 32)
        for n in range(LT):
            fb(n)
            if n:
                asum_(n - 1)
        asum_(LT - 1)
        for n in range(LT):
            lo(n, 0)
        rec(0)
        dve.wait_ge(prep["silu"], 1)
        ada_zero(dve, 0)
        for g in range(GROUPS):
            m = LT * (g + 1)
            more = g + 1 < GROUPS
            for t in range(LT):
                lo(LT * g + t, 1)
            ev(g, 0, 0)
            ev(g, 0, 1)
            if more:
                fb(m)
            ev(g, 0, 2)
            if more:
                fb(m + 1)
                asum_(m)
            ev(g, 0, 3)
            if more:
                asum_(m + 1)
            ada_step(dve, 0, 2 * g, 0)
            ev(g, 1, 0)
            if more:
                fb(m + 2)
            ev(g, 1, 1)
            if more:
                fb(m + 3)
                asum_(m + 2)
                asum_(m + 3)
                for t in range(LT):
                    lo(m + t, 0)
            ada_step(dve, 0, 2 * g + 1, 0)
            ev(g, 1, 2)
            ev(g, 1, 3)
            if more:
                rec(g + 1)

    def filter_act(act):
        def abs_(n):
            act.wait_ge(fl["fbused"], n + 1)
            if n:
                act.wait_ge(fl["fa"], n)
            nc.scalar.activation(afwd[:], fwd[:, n % 2], ACT.Abs)
            nc.scalar.activation(abwd[:], bwd[:, n % 2], ACT.Abs).then_inc(fl["as_"], 1)

        def hi(n, part):
            act.wait_ge(fl["pm"], n + 1)
            if n >= LT:
                act.wait_ge(fl["sp"], 8 * (n // LT - 1) + 4 * (part + 1))
            src, h = ((sum_f, sum_h), (dif_f, dif_h))[part]
            nc.scalar.activation(h[:, n % LT], src[:, n % LT], ACT.Copy).then_inc(fl["mhi" if part else "phi"], 1)

        for n in range(LT):
            abs_(n)
        for n in range(LT):
            hi(n, 0)
        for g in range(GROUPS):
            for t in range(LT):
                hi(LT * g + t, 1)
            act.wait_ge(fl["nbt"], g + 1)
            if g:
                act.wait_ge(fl["ev"], 8 * g)
            nc.scalar.activation(rn_row[:], bank[6][:], ACT.Copy).then_inc(fl["nrow"], 1)
            if g + 1 < GROUPS:
                for t in range(LT):
                    abs_(LT * (g + 1) + t)
                for t in range(LT):
                    hi(LT * (g + 1) + t, 0)

    def filter_pool(pool):
        for n in range(GROUPS * LT):
            t = n % LT
            pool.wait_ge(fl["fbused"], n + 1)
            if n >= LT:
                pool.wait_ge(fl["plo"], n - LT + 1)
                pool.wait_ge(fl["mlo"], n - LT + 1)
            nc.gpsimd.tensor_tensor(sum_f[:, t], fwd[:, n % 2], bwd[:, n % 2], ALU.add)
            nc.gpsimd.tensor_tensor(dif_f[:, t], fwd[:, n % 2], bwd[:, n % 2], ALU.subtract).then_inc(fl["pm"], 1)
            if t == LT - 1 and n >= LT:
                ada_load_one(pool, 0, n // LT * 2, 0)
                ada_load_one(pool, 0, n // LT * 2 + 1, 0)

    def filter_sp(sp):
        for e in range(8 * GROUPS):
            g, part, k = e // 8, e // 4 % 2, e % 4
            o, dh = divmod(g, 2)
            sp.wait_ge(fl["ev"], e + 1)
            sp.dma_start(spectra[o, 2 * dh:2 * dh + 2, :, k, part, :].rearrange("q p c -> p q c"),
                         spec_out[:, e % 2].rearrange("p (q c) -> p q c", q=2)).then_inc(fl_st[e % 2], 16)

    def xload_sp(sp):
        sp.wait_ge(fl["fbused"], GROUPS * LT)
        sp.dma_start(x_rows[:], A["x"][0].rearrange("(t p) d -> p t d", p=P)).then_inc(xs["in"], 16)

    def xload_pe(pe):
        pe.wait_ge(xs["in"], 16)
        for k in range(KT):
            if k >= 4:
                pe.wait_ge(xs["ev"], k - 3)
            for t in range(LT):
                ins = nc.tensor.transpose(bank[k % 4][:, t * P:(t + 1) * P], x_rows[:, t, k * P:(k + 1) * P], ident[:])
            ins.then_inc(xs["pe"], 1)

    def xload_act(act):
        act.wait_ge(fl["plo"], GROUPS * LT)
        act.wait_ge(fl["mlo"], GROUPS * LT)
        for k in range(KT):
            act.wait_ge(xs["pe"], k + 1)
            nc.scalar.activation(x[:, k], bank[k % 4][:], ACT.Copy).then_inc(xs["ev"], 1)

    norm_sems = sems("norm", "sq ac st rt rc bc t1 hi lo")
    ADDS = KT - 3
    norm_count = {"norms": 0, "modulated": 0}

    class Norm:
        def __init__(self, ready, scale, shift, mods, nxt=None):
            self.s = norm_sems
            self.late = (ring[nxt][0] + 1, ring[nxt][1] + 1, ring[nxt][2]) if nxt else None
            self.ready, self.scale, self.shift, self.mods = ready, scale, shift, mods
            self.a, self.b, self.m = KT * norm_count["norms"], norm_count["norms"], KT * norm_count["modulated"]
            norm_count["norms"] += 1
            norm_count["modulated"] += shift is not None
            self.done = (norm_sems["lo"], self.a)

        def act(self, act):
            s = self.s
            for t in range(KT):
                act.wait_ge(self.ready[0], self.ready[1] + t + 1)
                if t >= 2:
                    act.wait_ge(s["ac"], ADDS * self.b + max(t - 2, 1))
                nc.scalar.activation(nsq[:, t % 2], x[:, t], ACT.Square).then_inc(s["sq"], 1)
            act.preload_act_table(ACT.Sqrt)
            act.wait_ge(s["st"], self.b + 1)
            nc.scalar.activation(rms_cols[:, 0, 0:LT], bank[7][:, 0:LT], ACT.Sqrt, bias=eps_col[:], scale=1.0 / D)\
              .then_inc(s["rt"], 1)
            if self.late:
                r, su, n_el = self.late
                split_hi(act, r, su, 0, n_el)
            if self.shift is not None:
                for t in range(KT):
                    act.wait_ge(s["t1"], self.m + t + 1)
                    nc.scalar.activation(hh[:, t], nt1[:, t % 2], ACT.Identity, bias=self.shift(t)).then_inc(s["hi"], 1)

        def pool(self, pool):
            s = self.s
            if self.b:
                pool.wait_ge(s["st"], self.b)
            for t in range(1, KT - 2):
                pool.wait_ge(s["sq"], self.a + t + 1)
                if t >= 2:
                    pool.wait_ge(s["ac"], ADDS * self.b + t - 1)
                nc.gpsimd.tensor_tensor(nacc[:], nsq[:, 0] if t == 1 else nacc[:], nsq[:, t % 2], ALU.add).then_inc(s["ac"], 1)
            if self.late:
                r, su, n_el = self.late
                pool.wait_ge(hi_done, su + 1)
                nc.gpsimd.tensor_tensor(wlo[su % 2][:, :n_el], raw[r % 2][:, :n_el], whi[su % 2][:, :n_el].bitcast(F32),
                                        ALU.subtract).then_inc(raw_done, 1)

        def pe(self, pe):
            s = self.s
            pe.wait_ge(s["ac"], ADDS * (self.b + 1))
            for t, src in enumerate((nacc, nsq[:, 0], nsq[:, 1])):
                if t:
                    pe.wait_ge(s["sq"], self.a + KT - 2 + t)
                for b in range(LT):
                    ins = nc.tensor.matmul(bank[7][:, b:b + 1], src[:, b * P:(b + 1) * P], ones[:, 0:1],
                                           start=(t == 0 and b == 0), stop=(t == 2), skip_group_check=True)
            ins.then_inc(s["st"], 1)
            pe.wait_ge(s["rc"], self.b + 1)
            for b in range(LT):
                ins = nc.tensor.transpose(bank[6][:, b * P:(b + 1) * P], rstd_cols[:, 0, b:b + 1].broadcast_to([P, P]), ident[:])
            ins.then_inc(s["bc"], 1)

        def dve(self, dve):
            s = self.s
            dve.wait_ge(s["rt"], self.b + 1)
            nc.vector.reciprocal(rstd_cols[:, 0, 0:LT], rms_cols[:, 0, 0:LT]).then_inc(s["rc"], 1)
            if self.mods is not None:
                dve.wait_ge(ada_ev, self.mods)
            dve.wait_ge(s["bc"], self.b + 1)
            dve.wait_ge(self.ready[0], self.ready[1] + KT)
            for t in range(KT + 1):
                if self.shift is None:
                    if t < KT:
                        nc.vector.scalar_tensor_tensor(x[:, t], x[:, t], self.scale(t), bank[6][:], ALU.mult, ALU.mult)\
                          .then_inc(s["lo"], 1)
                    continue
                if t < KT:
                    if t >= 2:
                        dve.wait_ge(s["lo"], self.a + t - 1)
                    nc.vector.scalar_tensor_tensor(nt1[:, t % 2], x[:, t], self.scale(t), bank[6][:], ALU.mult, ALU.mult)\
                      .then_inc(s["t1"], 1)
                if t >= 1:
                    dve.wait_ge(s["hi"], self.m + t)
                    nc.vector.scalar_tensor_tensor(hl[:, t - 1], nt1[:, (t - 1) % 2], self.shift(t - 1),
                                                   hh[:, t - 1].bitcast(F32), ALU.add, ALU.subtract).then_inc(s["lo"], 1)
            if self.late:
                dve.wait_ge(raw_done, self.late[0] + 1)

    def mod_norm(ready, b, h, nxt=None):
        return Norm(ready, lambda t: gsc[:, b, h, t:t + 1],
                    lambda t: mod[:, b, h * 3 * KT + t:h * 3 * KT + t + 1], 2 * (2 * b + h) + 2, nxt)

    def gate(b, h, i, it, step):
        c0 = h * 3 * KT + 2 * KT + i
        if isinstance(it, int):
            return mod[:, b, c0 + step * it:c0 + step * it + 1]
        return mod[:, b, bass.ds(c0 + step * it, 1)]

    rp_in, qk = sem("rope_in"), sems("qk", "h0 qf st sw t rt rc rx bc done vd rot")
    NQK = 2 * 5
    qkv_r, qkv_s = ring["qkv"][0], ring["qkv"][1]

    def qkv_sp(sp):
        for i in range(6):
            load(sp, qkv_r + i, 0, cols2(A["attn_w_qkv"][0], 2 * P * i, 0, 0))
            if i == 0:
                sp.dma_start(rope[:], C["rope"].rearrange("s p l -> p s l")).then_inc(rp_in, 16)

    def project(s, h, dst):
        w = slot_w(s)
        for k in range(KT):
            ks = slice(h * P, (h + 1) * P)
            ins = three_pass(dst, (w[0][:, k, ks], w[1][:, k, ks]), (hh[:, k], hl[:, k]), k == 0, k == KT - 1)
        return ins

    def project_pair(pe, s, dsts, ready):
        w = slot_w(s)
        for k in range(KT):
            pe.wait_ge(ready[0], ready[1] + k + 1)
            for h in range(2):
                ks = slice(h * P, (h + 1) * P)
                ins = three_pass(dsts[h], (w[0][:, k, ks], w[1][:, k, ks]), (hh[:, k], hl[:, k]), k == 0, k == KT - 1)
                if h == 0:
                    first = ins
        return first, ins

    def project_rows(pe, s, c0, n, dst):
        w = slot_w(s)
        for t in range(LT):
            for k in range(KT):
                ts = slice(t * P, (t + 1) * P)
                ins = three_pass(dst(t), (hh[:, k, ts], hl[:, k, ts]), (w[0][:, k, c0:c0 + n], w[1][:, k, c0:c0 + n]),
                                 k == 0, k == KT - 1)
        return ins

    def qkv_pe(pe, norm):
        def stat(T):
            pe.wait_ge(qk["qf"], T + 1)
            if T >= 1:
                pe.wait_ge(qk["rt"], T)
            for b in range(LT):
                ins = nc.tensor.matmul(bank[7][:, 2 * b:2 * b + 2], qsq[:, T % 2, b * P:(b + 1) * P], head_mean[:],
                                       start=True, stop=True)
            ins.then_inc(qk["st"], 1)
            if T >= 2:
                pe.wait_ge(qk["t"], T - 1)
            nc.tensor.matmul(bank[4 + T % 2][:], swap_m[:], qf[:, T % 2], start=True, stop=True).then_inc(qk["sw"], 1)

        def factors(T):
            pe.wait_ge(qk["rx"], T + 1)
            if T >= 1:
                pe.wait_ge(qk["done"], T)
            for b in range(LT):
                ins = nc.tensor.transpose(bank[6][:, b * P:(b + 1) * P],
rx[:, T % 2, b * P:(b + 1) * P], ident[:])
            ins.then_inc(qk["bc"], 1)

        for i in range(6):
            pe.wait_ge(raw_done, qkv_r + i + 1)
            if i < 5:
                for h in range(2):
                    T = 2 * i + h
                    if T >= 4:
                        pe.wait_ge(qk["qf"], T - 3)
                    if T == 0:
                        first, second = project_pair(pe, qkv_s, (bank[0][:], bank[1][:]), norm.done)
                        first.then_inc(qk["h0"], 1)
                        second.then_inc(used, 1)
                    elif T > 1:
                        project(qkv_s + i, h, bank[T % 4][:]).then_inc(used if h else qk["h0"], 1)
                    if T >= 2:
                        stat(T - 2)
                    if T >= 3:
                        factors(T - 3)
            else:
                pe.wait_ge(qk["qf"], 8)
                project_rows(pe, qkv_s + i, 0, KV_HEADS * HD,
                             lambda t: bank[2 + t // 2][:, (t % 2) * 256:(t % 2) * 256 + 256]).then_inc(used, 1)
        factors(7)
        stat(8)
        factors(8)
        stat(9)
        factors(9)

    def qkv_pool(pool):
        for T in range(NQK):
            pool.wait_ge(qk["rc"], T + 1)
            if T >= 2:
                pool.wait_ge(qk["bc"], T - 1)
            nc.gpsimd.tensor_copy(rx[:, T % 2].rearrange("p (a c) -> p a c", c=HD),
                                  rstd_cols[:, T % 2, :].unsqueeze(2).broadcast_to([P, 2 * LT, HD])).then_inc(qk["rx"], 1)

    def head_dst(T, h):
        return qh[:, 2 * T + h] if T < 8 else kh[:, 2 * (T - 8) + h]

    def qkv_act(act, splits):
        def tile_in(T):
            if T % 2:
                act.wait_ge(used, qkv_s + T // 2 + 1)
            else:
                act.wait_ge(qk["h0"], T // 2 + 1)
            if T >= 2:
                act.wait_ge(qk["st"], T - 1)
                act.wait_ge(qk["rot"], T - 1)
            nc.scalar.activation(qsq[:, T % 2], bank[T % 4][:], ACT.Square)
            g = 0 if T < 8 else 1
            nc.scalar.activation(qf[:, T % 2], bank[T % 4][:], ACT.Copy, scale=gain_cols[:, g:g + 1]).then_inc(qk["qf"], 1)

        def root(T):
            act.wait_ge(qk["st"], T + 1)
            if T >= 2:
                act.wait_ge(qk["rc"], T - 1)
            nc.scalar.activation(rms_cols[:, T % 2, :], bank[7][:, 0:8], ACT.Sqrt, bias=eps_col[:]).then_inc(qk["rt"], 1)

        for T in range(NQK):
            if T % 2 == 0:
                splits(T // 2)
            tile_in(T)
            if T >= 1:
                root(T - 1)
        root(NQK - 1)
        act.wait_ge(used, qkv_s + 6)
        nc.scalar.activation(vh[:, 0:2].rearrange("p t n -> p (t n)"), bank[2][:], ACT.Copy)
        nc.scalar.activation(vh[:, 2:4].rearrange("p t n -> p (t n)"), bank[3][:], ACT.Copy).then_inc(qk["vd"], 1)
        splits(5)

    def qkv_dve(dve, splits):
        dve.wait_ge(rp_in, 16)
        n = [0]
        ch = sem("rot_chain")

        def link(ins):
            n[0] += 1
            ins.then_inc(ch, 1)
            dve.wait_ge(ch, n[0])

        def rotate(T):
            dve.wait_ge(qk["sw"], T + 1)
            if T >= 2:
                dve.wait_ge(qk["done"], T - 1)
            nc.vector.tensor_tensor(qt[:, T % 2], bank[4 + T % 2][:], rope[:, 1], ALU.mult).then_inc(qk["t"], 1)
            link(nc.vector.tensor_tensor(qf[:, T % 2], qf[:, T % 2], rope[:, 0], ALU.mult))
            dve.wait_ge(qk["t"], T + 1)
            nc.vector.tensor_tensor(qt[:, T % 2], qt[:, T % 2], qf[:, T % 2], ALU.add).then_inc(qk["rot"], 1)

        def rec(T):
            dve.wait_ge(qk["rt"], T + 1)
            if T >= 2:
                dve.wait_ge(qk["rx"], T - 1)
            nc.vector.reciprocal(rstd_cols[:, T % 2, :], rms_cols[:, T % 2, :]).then_inc(qk["rc"], 1)

        def scale(T):
            dve.wait_ge(qk["bc"], T + 1)
            dve.wait_ge(qk["rot"], T + 1)
            nc.vector.tensor_tensor(head_dst(T, 0), qt[0:HD, T % 2], bank[6][0:HD, :], ALU.mult)
            nc.vector.tensor_tensor(head_dst(T, 1), qt[HD:P, T % 2], bank[6][HD:P, :], ALU.mult).then_inc(qk["done"], 1)

        for T in range(NQK):
            if T % 2 == 0:
                splits(T // 2)
            rec(T)
            rotate(T)
            if T >= 1:
                scale(T - 1)
        scale(NQK - 1)
        splits(5)

    attend_sems = sems("attend", "sc nm ex pr tr pt o oh ol")
    attend_heads = [0]

    class Attend:
        def __init__(self, name, heads, q, k, v, first, kind, tile0, probs, probsT):
            self.s = dict(attend_sems, ch=sem(f"{name}_chain"))
            self.heads, self.q, self.k, self.v, self.first, self.kind = heads, q, k, v, first, kind
            self.tile0, self.probs, self.probsT = tile0, probs, probsT
            self.steps = [(h, t) for h in range(heads) for t in range(LT)]
            self.i0, self.h0, self.j0 = LT * attend_heads[0], attend_heads[0], attend_heads[0] // 2
            attend_heads[0] += heads

        def last(self, t):
            return LT - 1 if self.kind == "plain" else t

        def width(self, t):
            return (self.last(t) - self.first(t) + 1) * P

        def pe(self, pe, start_waits):
            s, steps = self.s, self.steps
            for sm, v in start_waits:
                pe.wait_ge(sm, v)

            def scores(i):
                h, t = steps[i]
                if i >= 3:
                    pe.wait_ge(s["ex"], self.i0 + i - 2)
                nc.tensor.matmul(bank[i % 3][:, 0:self.width(t)], self.q(h, t), self.k(h, t), start=True, stop=True)\
                  .then_inc(s["sc"], 1)

            def turn(i):
                h, t = steps[i]
                pe.wait_ge(s["pr"], self.i0 + i + 1)
                if i >= 2:
                    pe.wait_ge(s["pt"], self.i0 + i - 1)
                for b in range(self.width(t) // P):
                    ins = nc.tensor.transpose(bank[3 + i % 2][:, b * P:(b + 1) * P], self.probs[:, i % 2, b * P:(b + 1) * P], ident[:])
                ins.then_inc(s["tr"], 1)

            def values(h):
                pe.wait_ge(s["pt"], self.i0 + LT * (h + 1))
                if h >= 2 and h % 2 == 0:
                    pe.wait_ge(s["ol"], self.j0 + h // 2)
                o = bank[5][HD * (h % 2):HD * (h % 2) + HD, :]
                pT = self.probsT[:, h % 2]
                if self.kind == "alibi":
                    for t in range(LT):
                        for k in range(self.first(t), t + 1):
                            ins = nc.tensor.matmul(o[:, t * P:(t + 1) * P], self.v(h, k), pT[:, k - self.first(t), t * P:(t + 1) * P],
                                                   start=k == self.first(t), stop=k == t)
                else:
                    for k in range(LT):
                        c0 = k * P if self.kind == "causal" else 0
                        ins = nc.tensor.matmul(o[:, c0:L], self.v(h, k), pT[:, k, c0:L], start=k == 0, stop=k == LT - 1,
                                               skip_group_check=self.kind == "causal")
                ins.then_inc(s["o"], 1)

            scores(0)
            scores(1)
            for i in range(len(steps)):
                if i + 2 < len(steps):
                    scores(i + 2)
                turn(i)
                if i % LT == 1 and i > LT:
                    values(i // LT - 1)
            values(self.heads - 1)

        def act(self, act, extra=None):
            s, steps = self.s, self.steps

            def move(i):
                h, t = steps[i]
                act.wait_ge(s["tr"], self.i0 + i + 1)
                if h >= 2:
                    act.wait_ge(s["o"], self.h0 + h - 1)
                n = self.width(t) // P
                nc.scalar.activation(self.probsT[:, h % 2, 0:n, t * P:(t + 1) * P],
                                     bank[3 + i % 2][:, 0:n * P].rearrange("p (k q) -> p k q", k=n), ACT.Copy).then_inc(s["pt"], 1)

            def heads_out(j):
                act.wait_ge(s["o"], self.h0 + 2 * j + 2)
                nc.scalar.activation(hh[:, self.tile0 + j], bank[5][:], ACT.Copy).then_inc(s["oh"], 1)

            for i, (h, t) in enumerate(steps):
                act.wait_ge(s["nm"], self.i0 + i + 1)
                if i >= 2:
                    act.wait_ge(s["tr"], self.i0 + i - 1)
                w = self.width(t)
                if self.kind == "alibi":
                    nc.scalar.activation(es[:, i % 4:i % 4 + 1], sink_b[:, h:h + 1], ACT.Exp, bias=nmx[:, i % 4:i % 4 + 1])
                    src, sc = biased[:, i % 2, 0:w], 1.0
                else:
                    src, sc = bank[i % 3][:, 0:w], SCALE
                nc.scalar.activation(self.probs[:, i % 2, 0:w], src, ACT.Exp, bias=nmx[:, i % 4:i % 4 + 1], scale=sc,
                                     accum_out=sums[:, i % 4:i % 4 + 1]).then_inc(s["ex"], 1)
                if i >= 1:
                    move(i - 1)
                if i % LT == 2 and i // LT >= 2 and i // LT % 2 == 0:
                    heads_out(i // LT // 2 - 1)
            move(len(steps) - 1)
            heads_out(self.heads // 2 - 1)

        def dve(self, dve, extra=None):
            s, steps, n = self.s, self.steps, [0]

            def link(ins):
                n[0] += 1
                ins.then_inc(s["ch"], 1)
                dve.wait_ge(s["ch"], n[0])

            def heads_out(j):
                dve.wait_ge(s["oh"], self.j0 + j + 1)
                nc.vector.tensor_tensor(hl[:, self.tile0 + j], bank[5][:], hh[:, self.tile0 + j].bitcast(F32), ALU.subtract)\
                  .then_inc(s["ol"], 1)

            def maximum(i):
                h, t = steps[i]
                w, c = self.width(t), slice(i % 4, i % 4 + 1)
                dve.wait_ge(s["sc"], self.i0 + i + 1)
                src = bank[i % 3][:, 0:w]
                if self.kind == "causal":
                    link(nc.vector.tensor_tensor(src[:, w - P:w], src[:, w - P:w], causal[:], ALU.add))
                if self.kind == "alibi":
                    if i >= 2:
                        dve.wait_ge(s["ex"], self.i0 + i - 1)
                    src = biased[:, i % 2, 0:w]
                    link(nc.vector.scalar_tensor_tensor(src, bank[i % 3][:, 0:w], SCALE, alibi[:, h, 2 * P - w:2 * P],
                                                        ALU.mult, ALU.add))
                link(nc.vector.reduce_max(mxs[:, c], src, axis=AX.X))
                if self.kind == "alibi":
                    link(nc.vector.tensor_scalar(mxs[:, c], mxs[:, c], sink_b[:, h:h + 1], None, ALU.max))
                if i >= 4:
                    dve.wait_ge(s["ex"], self.i0 + i - 3)
                nc.vector.tensor_scalar(nmx[:, c], mxs[:, c], -1.0 if self.kind == "alibi" else -SCALE, None, ALU.mult)\
                  .then_inc(s["nm"], 1)

            def normalise(i):
                h, t = steps[i]
                w, c = self.width(t), slice(i % 4, i % 4 + 1)
                dve.wait_ge(s["ex"], self.i0 + i + 1)
                if self.kind == "alibi":
                    link(nc.vector.tensor_tensor(sums[:, c], sums[:, c], es[:, c], ALU.add))
                link(nc.vector.reciprocal(recs[:, c], sums[:, c]))
                nc.vector.tensor_scalar(self.probs[:, i % 2, 0:w], self.probs[:, i % 2, 0:w], recs[:, c], None, ALU.mult)\
                  .then_inc(s["pr"], 1)

            maximum(0)
            for i in range(len(steps)):
                if i + 1 < len(steps):
                    maximum(i + 1)
                normalise(i)
                if i % LT == 3 and i // LT >= 2 and i // LT % 2 == 0:
                    heads_out(i // LT // 2 - 1)
                if extra is not None:
                    extra(i)
            heads_out(self.heads // 2 - 1)

    G = HEADS // KV_HEADS
    attn1 = Attend("attn", HEADS, lambda h, t: qh[:, h, t * P:(t + 1) * P], lambda h, t: kh[:, h // G, :],
                   lambda h, k: vh[:, k, (h // G) * HD:(h // G + 1) * HD], lambda t: 0, "plain", 0, probs1, probsT1)
    GA = SWA_HEADS // SWA_KV
    swa = Attend("swa", SWA_HEADS, lambda h, t: qa[:, h, t * P:(t + 1) * P],
                 lambda h, t: ka[:, h // GA, max(t - 1, 0) * P:(t + 1) * P],
                 lambda h, k: va[:, k, (h // GA) * HD:(h // GA + 1) * HD], lambda t: max(t - 1, 0), "alibi", 0, probs2, probsT2)
    fox = Attend("fox", FOX_HEADS, lambda h, t: qfx[:, h, t * P:(t + 1) * P], lambda h, t: kfx[:, h, 0:(t + 1) * P],
                 lambda h, k: vfx[:, k, h * HD:(h + 1) * HD], lambda t: 0, "causal", SWA_HEADS // 2, probs2, probsT2)

    class Back:
        def __init__(self, name, key, w, b, src, ready):
            self.s = sems(name, "t0 x")
            self.r0, self.s0 = ring[key][0:2]
            self.w, self.b, self.src, self.ready = w, b, src, ready

        def sp(self, sp):
            for i in range(4):
                load(sp, self.r0 + i, 0, cols2(self.w, 2 * P * i, 0, 0))

        def pe(self, pe):
            for i in range(4):
                pe.wait_ge(raw_done, self.r0 + i + 1)
                w = slot_w(self.s0 + i)
                for h in range(2):
                    if i >= 2:
                        pe.wait_ge(self.s["x"], 2 * i + h - 3)
                    for k in range(KT):
                        if i == 0 and h == 0:
                            for sm, v in self.ready(k):
                                pe.wait_ge(sm, v)
                        ks = slice(h * P, (h + 1) * P)
                        ins = three_pass(bank[(2 * i + h) % 4][:], (w[0][:, k, ks], w[1][:, k, ks]),
                                         (self.src[0][:, k], self.src[1][:, k]), k == 0, k == KT - 1)
                    ins.then_inc(used if h else self.s["t0"], 1)

        def dve(self, dve, split):
            for i in range(4):
                for h in range(2):
                    m = 2 * i + h
                    dve.wait_ge(self.s["t0"], i + 1)
                    if h:
                        dve.wait_ge(used, self.s0 + i + 1)
                        split(i)
                    nc.vector.scalar_tensor_tensor(x[:, m], bank[m % 4][:], gate(self.b, 0, m, 0, 0), x[:, m],
                                                   ALU.mult, ALU.add).then_inc(self.s["x"], 1)

        def act(self, act, split):
            for i in range(4):
                split(i)

    class Ffn:
        def __init__(self, b, w_up, w_down, norm, conv_w, conv_b, gate_off, both, nxt, T):
            self.s = sems(f"ffn{b}", "t0 a1 cv cg sl hd hi hl dn xd")
            self.b, self.w_up, self.w_down, self.norm = b, w_up, w_down, norm
            self.conv_w, self.conv_b, self.gate_off, self.both = conv_w, conv_b, gate_off, both
            self.nxt, self.T = nxt, T
            self.up = [ring[f"up{b}_{h}"] for h in (0, 1)]
            self.dn = [ring[f"dn{b}_{h}"] for h in (0, 1)]
            self.val_off = FF - gate_off

        def sp(self, sp):
            for half in (0, 1):
                def up(c, it, half=half):
                    c0 = (FH * half + c) * P
                    load(sp, self.up[half][0] + c, it, cols2(self.w_up, self.gate_off + c0, 2 * P, it, self.val_off + c0))
                over(sp, FH, up)

                def down(c, it, half=half):
                    load(sp, self.dn[half][0] + c, it, down_parts(self.w_down, half, c, it))
                over(sp, KT, down)

        def pe(self, pe):
            s = self.s
            for half in (0, 1):
                r0, s0 = self.up[half][0:2]

                def up(c, it, half=half, r0=r0, s0=s0, gated=False):
                    U = FH * half + c
                    pe.wait_ge(raw_done, r0 + c + 1 + 2 * it)
                    if U >= 2:
                        pe.wait_ge(s["hd"], U - 1 + 2 * it)
                    banks = (bank[2 * (U % 2)][:], bank[2 * (U % 2) + 1][:])
                    if gated:
                        first, second = project_pair(pe, s0 + c, banks, self.norm.done)
                        first.then_inc(s["t0"], 1)
                        second.then_inc(used, 1)
                    else:
                        project(s0 + c, 0, banks[0]).then_inc(s["t0"], 1)
                        project(s0 + c, 1, banks[1]).then_inc(used, 1)
                if half == 0:
                    up(0, 0, gated=True)
                    up(1, 0)
                    over(pe, FH - 2, lambda c, it: up(c + 2, it))
                else:
                    up(0, 0)
                    up(1, 0)
                    if self.T is not None:
                        ada_columns(pe, self.T)
                    over(pe, FH - 2, lambda c, it: up(c + 2, it))
                r0, s0 = self.dn[half][0:2]

                def down(c, it, half=half, r0=r0, s0=s0):
                    V = KT * half + c
                    pe.wait_ge(raw_done, r0 + c + 1 + 2 * it)
                    if V >= 2:
                        pe.wait_ge(s["xd"], V - 1 + 2 * it)
                    w = slot_d(s0 + c)
                    for k in range(FH):
                        if isinstance(it, int) and c == 0:
                            pe.wait_ge(s["hl"], FH * half + k + 1)
                        ins = three_pass(bank[4 + V % 2][:], (w[0][:, k], w[1][:, k]), (hid_h[:, k], hid_l[:, k]),
                                         k == 0, k == FH - 1)
                    ins.then_inc(used, 1)
                down(0, 0)
                down(1, 0)
                over(pe, KT - 2, lambda c, it: down(c + 2, it))

        def act(self, act):
            s = self.s
            for half in (0, 1):
                r0, s0, n_el, n = self.up[half]

                def up(c, it, half=half, s0=s0):
                    U = FH * half + c
                    p = U % 2
                    act.wait_ge(s["t0"], U + 1 + 2 * it)
                    g = self.cols(half, c, it, "g")
                    mid = g[2] if self.both else g[1]
                    nc.scalar.activation(fc[:, p], bank[2 * p][:], ACT.Identity, bias=g[3], scale=mid).then_inc(s["a1"], 1)
                    act.wait_ge(used, s0 + c + 1 + 2 * it)
                    if self.both:
                        v = self.cols(half, c, it, "v")
                        nc.scalar.activation(fv[:, p], bank[2 * p + 1][:], ACT.Identity, bias=v[3], scale=v[2]).then_inc(s["a1"], 1)
                    act.wait_ge(s["cg"], U + 1 + 2 * it)
                    nc.scalar.activation(fs[:, p], fc[:, p], ACT.Silu).then_inc(s["sl"], 1)
                    act.wait_ge(s["hd"], U + 1 + 2 * it)
                    nc.scalar.activation(tile_of(hid_h, c, it, 2), fh[:, p], ACT.Copy).then_inc(s["hi"], 1)
                act.preload_act_table(ACT.Silu)
                split_ahead(act, split_hi, n, r0, s0, n_el, self.dn[half][0:3], up)
                nxt = self.up[1][0:3] if half == 0 else self.nxt
                r0, s0, n_el, n = self.dn[half]
                split_ahead(act, split_hi, n, r0, s0, n_el, nxt, lambda c, it: None, 2 - half)

        def cols(self, half, c, it, which):
            n = 2 * FT if self.both else FT
            w0 = 0 if self.both else self.b * 3 * FT
            b0 = 0 if self.both else self.b * FT
            off = FH * half + c + ((self.gate_off if which == "g" else self.val_off) // P if self.both else 0)
            return [dcol(self.conv_w, w0 + tap * n + off, it, 2) for tap in range(3)] + [dcol(self.conv_b, b0 + off, it, 2)]

        def dve(self, dve):
            s = self.s
            for half in (0, 1):
                r0, s0, n_el, n = self.up[half]

                def up(c, it, half=half):
                    U = FH * half + c
                    p = U % 2
                    g = self.cols(half, c, it, "g")
                    if not self.both:
                        dve.wait_ge(s["a1"], U + 1 + 2 * it)
                        nc.vector.scalar_tensor_tensor(fc[:, p, 1:L], bank[2 * p][:, 0:L - 1], g[0], fc[:, p, 1:L],
                                                       ALU.mult, ALU.add).then_inc(s["cv"], 1)
                        dve.wait_ge(s["cv"], U + 1 + 2 * it)
                        nc.vector.scalar_tensor_tensor(fc[:, p, 0:L - 1], bank[2 * p][:, 1:L], g[2], fc[:, p, 0:L - 1],
                                                       ALU.mult, ALU.add).then_inc(s["cg"], 1)
                        val = bank[2 * p + 1][:]
                    else:
                        v = self.cols(half, c, it, "v")
                        dve.wait_ge(s["a1"], 2 * U + 1 + 4 * it)
                        nc.vector.scalar_tensor_tensor(fc[:, p, 1:L], bank[2 * p][:, 0:L - 1], g[1], fc[:, p, 1:L],
                                                       ALU.mult, ALU.add).then_inc(s["cv"], 1)
                        dve.wait_ge(s["cv"], 3 * U + 1 + 6 * it)
                        nc.vector.scalar_tensor_tensor(fc[:, p, 2:L], bank[2 * p][:, 0:L - 2], g[0], fc[:, p, 2:L],
                                                       ALU.mult, ALU.add).then_inc(s["cg"], 1)
                        dve.wait_ge(s["a1"], 2 * U + 2 + 4 * it)
                        nc.vector.scalar_tensor_tensor(fv[:, p, 1:L], bank[2 * p + 1][:, 0:L - 1], v[1], fv[:, p, 1:L],
                                                       ALU.mult, ALU.add).then_inc(s["cv"], 1)
                        dve.wait_ge(s["cv"], 3 * U + 2 + 6 * it)
                        nc.vector.scalar_tensor_tensor(fv[:, p, 2:L], bank[2 * p + 1][:, 0:L - 2], v[0], fv[:, p, 2:L],
                                                       ALU.mult, ALU.add).then_inc(s["cv"], 1)
                        dve.wait_ge(s["cv"], 3 * U + 3 + 6 * it)
                        val = fv[:, p]
                    dve.wait_ge(s["sl"], U + 1 + 2 * it)
                    nc.vector.tensor_tensor(fh[:, p], fs[:, p], val, ALU.mult).then_inc(s["hd"], 1)
                    dve.wait_ge(s["hi"], U + 1 + 2 * it)
                    nc.vector.tensor_tensor(tile_of(hid_l, c, it, 2), fh[:, p], tile_of(hid_h, c, it, 2).bitcast(F32),
                                            ALU.subtract).then_inc(s["hl"], 1)
                split_ahead(dve, split_lo, n, r0, s0, n_el, self.dn[half][0:3], up)
                nxt = self.up[1][0:3] if half == 0 else self.nxt
                r0, s0, n_el, n = self.dn[half]
                if self.T is not None:
                    if half:
                        ada_mods(dve, self.T)
                    ada_zero(dve, self.T + half)

                def down(c, it, half=half, s0=s0):
                    V = KT * half + c
                    dve.wait_ge(used, s0 + c + 1 + 2 * it)
                    xt = tile_of(x, c, it, 2)
                    nc.vector.scalar_tensor_tensor(xt, bank[4 + V % 2][:], gate(self.b, 1, c, it, 2), xt,
                                                   ALU.mult, ALU.add).then_inc(s["xd"], 1)
                    if self.T is not None and not (half and c == KT - 1):
                        ada_step(dve, self.T + half, c, it)
                split_ahead(dve, split_lo, n, r0, s0, n_el, nxt, down, 2 - half)

    hs = sems("hyena", "t0 m d1 d2 zh zl f px yf yh yl iv ze zu zh2 zl2 tr")
    in_r, in_s, in_n, IN_UNITS = ring["hyin"]
    spec_r = ring["spec"][0]
    out_r, out_s, out_n, _ = ring["hyout"]
    CHUNKS = ORDERS * NCH

    def hyena_sp(sp):
        over(sp, IN_UNITS, lambda c, it: load(sp, in_r + c, it, cols2(A["hy_w_in"][0], 2 * P * c, 4 * P, it)))
        for part in range(2):
            load(sp, ring["td"][0] + part, 0, table_parts("dft_signal", part))
        for i in range(2):
            sp.wait_ge(fl_st[i], 16 * 4 * GROUPS)
        for g in range(CHUNKS):
            src = spectra[g // NCH, g % NCH].rearrange("p k s c -> p (k s c)")
            load(sp, spec_r + g, 0, lambda slot: [(slot[:, a:a + UNIT // 2], src[:, a:a + UNIT // 2]) for a in (0, UNIT // 2)])

    def hyena_in_pe(pe, norm):
        def unit(c, it, gated=False):
            pe.wait_ge(raw_done, in_r + c + 1 + 2 * it)
            if c >= 2:
                pe.wait_ge(hs["d2"], 2 * (c - 1) + 4 * it)
            banks = (bank[2 * (c % 2)][:], bank[2 * (c % 2) + 1][:])
            if gated:
                first, second = project_pair(pe, in_s + c, banks, norm.done)
                first.then_inc(hs["t0"], 1)
                second.then_inc(used, 1)
            else:
                project(in_s + c, 0, banks[0]).then_inc(hs["t0"], 1)
                project(in_s + c, 1, banks[1]).then_inc(used, 1)
        unit(0, 0, gated=True)
        unit(1, 0)
        ada_columns(pe, 3)
        over(pe, IN_UNITS - 2, lambda c, it: unit(c + 2, it))

    def u_tile(c, it, h, sl=slice(None)):
        return tile_of(u, 2 * c + h, it, 4, sl)

    def hyena_in_act(act):
        act.preload_act_table(ACT.Identity)

        def unit(c, it):
            act.wait_ge(hs["t0"], c + 1 + 2 * it)
            for h in range(2):
                if h:
                    act.wait_ge(used, in_s + c + 1 + 2 * it)
                nc.scalar.activation(u_tile(c, it, h), bank[2 * (c % 2) + h][:], ACT.Identity,
                                     bias=dcol("hy_conv_b", 2 * c + h, it, 4),
                                     scale=dcol("hy_conv_w", 3 * KT + 2 * c + h, it, 4)).then_inc(hs["m"], 1)
        split_ahead(act, split_hi, IN_UNITS, in_r, in_s, in_n, None, unit)

    def hyena_in_dve(dve):
        def unit(c, it):
            for h in range(2):
                dve.wait_ge(hs["m"], 2 * c + h + 1 + 4 * it)
                t1 = u_tile(c, it, h, slice(1, L))
                nc.vector.scalar_tensor_tensor(t1, bank[2 * (c % 2) + h][:, 0:L - 1], dcol("hy_conv_w", 2 * c + h, it, 4), t1,
                                               ALU.mult, ALU.add).then_inc(hs["d1"], 1)
            for h in range(2):
                dve.wait_ge(hs["d1"], 2 * c + h + 1 + 4 * it)
                t0 = u_tile(c, it, h, slice(0, L - 1))
                nc.vector.scalar_tensor_tensor(t0, bank[2 * (c % 2) + h][:, 1:L], dcol("hy_conv_w", 6 * KT + 2 * c + h, it, 4), t0,
                                               ALU.mult, ALU.add).then_inc(hs["d2"], 1)
        split_ahead(dve, split_lo, IN_UNITS, in_r, in_s, in_n, None, unit)

    def turn_pe(pe, n):
        if n < KT:
            pe.wait_ge(hs["d2"], 2 * IN_UNITS)
            pe.wait_ge(ada_ev, 2 * 3 + 1)
        else:
            pe.wait_ge(hs["zu"], n - KT + 1)
        if n >= 2:
            pe.wait_ge(hs["zl"], n - 1)
        for t in range(LT):
            ins = nc.tensor.transpose(bank[6 + n % 2][:, t * P:(t + 1) * P], u[:, n % KT, t * P:(t + 1) * P], ident[:])
        ins.then_inc(hs["tr"], 1)

    def turned(w, n):
        return w[:, :, (n % KT) * P:(n % KT + 1) * P]

    def turn_act(act, n):
        act.wait_ge(hs["tr"], n + 1)
        if n >= KT:
            act.wait_ge(hs["f"], LT * ((n - KT) // 2 + 1))
        nc.scalar.activation(turned(zt_h, n), bank[6 + n % 2][:].rearrange("p (t c) -> p t c", t=LT), ACT.Copy)\
          .then_inc(hs["zh"], 1)

    def turn_dve(dve, n):
        dve.wait_ge(hs["zh"], n + 1)
        nc.vector.tensor_tensor(turned(zt_l, n), bank[6 + n % 2][:].rearrange("p (t c) -> p t c", t=LT),
                                turned(zt_h, n).bitcast(F32), ALU.subtract).then_inc(hs["zl"], 1)

    def forward_pe(pe, g):
        q = g % NCH
        pe.wait_ge(hs["zl"], KT * (g // NCH) + 2 * q + 2)
        for k in range(LT):
            if g:
                pe.wait_ge(hs["px"], LT * (g - 1) + k + 1)
            for part in range(2):
                for t in range(LT):
                    ks, cs = slice(k * P, (k + 1) * P), slice(q * CH, (q + 1) * CH)
                    ins = three_pass(bank[k][:, part * CH:(part + 1) * CH], (td_h[:, part, t, ks], td_l[:, part, t, ks]),
                                     (zt_h[:, t, cs], zt_l[:, t, cs]), t == 0, t == LT - 1)
            ins.then_inc(hs["f"], 1)

    def inverse_pe(pe, g):
        for c in range(2):
            if g:
                pe.wait_ge(hs["ze"], 2 * (g - 1) + c + 1)
            for k in range(LT):
                if c == 0:
                    pe.wait_ge(hs["yl"], LT * g + k + 1)
                for part in range(2):
                    cs = slice(c * P, (c + 1) * P)
                    ins = three_pass(bank[4 + c][:], (y_h[:, k, part, cs], y_l[:, k, part, cs]),
                                     (td_h[:, part, k], td_l[:, part, k]), k == 0 and part == 0, k == LT - 1 and part == 1)
            ins.then_inc(hs["iv"], 1)

    def hyena_pe(pe):
        for n in range(KT):
            turn_pe(pe, n)
        pe.wait_ge(raw_done, ring["td"][0] + 2)
        forward_pe(pe, 0)
        for g in range(CHUNKS):
            if g + 1 < CHUNKS:
                forward_pe(pe, g + 1)
            if 1 <= g <= NCH:
                turn_pe(pe, KT + 2 * (g - 1))
                turn_pe(pe, KT + 2 * (g - 1) + 1)
            inverse_pe(pe, g)

    def hyena_dve(dve):
        ada_mods(dve, 3)
        tables_dve(dve, "td", td_h, td_l, 2)
        for n in range(KT):
            turn_dve(dve, n)

        def low(i):
            dve.wait_ge(hs["yh"], i + 1)
            nc.vector.tensor_tensor(y_l[:, i % LT], y_f[:], y_h[:, i % LT].bitcast(F32), ALU.subtract).then_inc(hs["yl"], 1)

        def product(g):
            r = spec_r + g
            h = raw[r % 2][:].rearrange("p (k s c) -> p k s c", k=LT, s=2)
            dve.wait_ge(raw_in[r % 2], 32 * (r // 2 + 1))
            for k in range(LT):
                i = LT * g + k
                xk = bank[k][:].rearrange("p (s c) -> p s c", s=2)
                dve.wait_ge(hs["f"], i + 1)
                if i:
                    dve.wait_ge(hs["yf"], i)
                nc.vector.tensor_tensor(pt1[:], xk, h[:, k, 0, :].unsqueeze(1).broadcast_to([P, 2, CH]), ALU.mult)
                nc.vector.tensor_tensor(pt2[:], xk, h[:, k, 1, :].unsqueeze(1).broadcast_to([P, 2, CH]), ALU.mult)\
                  .then_inc(hs["px"], 1)
                if i:
                    low(i - 1)
                    dve.wait_ge(hs["yl"], i)
                dve.wait_ge(hs["px"], i + 1)
                ins = nc.vector.tensor_tensor(y_f[:, 0], pt1[:, 0], pt2[:, 1], ALU.subtract)
                if k == LT - 1:
                    ins.then_inc(raw_done, 1)
                nc.vector.tensor_tensor(y_f[:, 1], pt1[:, 1], pt2[:, 0], ALU.add).then_inc(hs["yf"], 1)

        def result(g):
            o, q = divmod(g, NCH)
            for c in range(2):
                ct, i = 2 * q + c, 2 * g + c
                z = u[:, ct]
                dve.wait_ge(hs["iv"], i + 1)
                nc.vector.scalar_tensor_tensor(z, z, col("hy_skip", o * KT + ct), bank[4 + c][:], ALU.mult, ALU.add)\
                  .then_inc(hs["ze"], 1)
                dve.wait_ge(hs["ze"], i + 1)
                nc.vector.tensor_tensor(z, z, u[:, KT * (1 + o) + ct], ALU.mult).then_inc(hs["zu"], 1)
                if o == 1:
                    dve.wait_ge(hs["zh2"], ct + 1)
                    nc.vector.tensor_tensor(z_l[:, ct], z, z_h[:, ct].bitcast(F32), ALU.subtract).then_inc(hs["zl2"], 1)

        product(0)
        for g in range(CHUNKS):
            if g + 1 < CHUNKS:
                product(g + 1)
            else:
                low(LT * CHUNKS - 1)
            if g == CHUNKS - 1:
                for k in range(2):
                    split_lo(dve, out_r + k, out_s + k, 0, out_n)
            if 1 <= g <= NCH:
                turn_dve(dve, KT + 2 * (g - 1))
                turn_dve(dve, KT + 2 * (g - 1) + 1)
            result(g)

    def hyena_act(act):
        tables_act(act, "td", td_h)
        for n in range(KT):
            turn_act(act, n)

        def high(g):
            for k in range(LT):
                i = LT * g + k
                act.wait_ge(hs["yf"], i + 1)
                if g and k == 0:
                    act.wait_ge(hs["iv"], 2 * g)
                nc.scalar.activation(y_h[:, k], y_f[:], ACT.Copy).then_inc(hs["yh"], 1)

        high(0)
        for g in range(CHUNKS):
            if g + 1 < CHUNKS:
                high(g + 1)
            else:
                for k in range(2):
                    split_hi(act, out_r + k, out_s + k, 0, out_n)
            if 1 <= g <= NCH:
                turn_act(act, KT + 2 * (g - 1))
                turn_act(act, KT + 2 * (g - 1) + 1)
            if g >= NCH:
                for c in range(2):
                    act.wait_ge(hs["zu"], 2 * g + c + 1)
                    nc.scalar.activation(z_h[:, 2 * (g % NCH) + c], u[:, 2 * (g % NCH) + c], ACT.Copy).then_inc(hs["zh2"], 1)

    hy = sems("hybrid", "in hp ea ed ft fc fb ch fa aux wfh stored ones")
    win_r, win_s = ring["win"][0:2]
    gates = nc.dram_tensor("gates", (2, FOX_HEADS, L), F32).ap()
    f_x, f_n, f_l, f_8, f_m8, f_one = [at(f"f_{i}", AREA + 72192 + 2048 * i, [FOX_HEADS, L]) for i in range(6)]

    def hybrid_sp(sp):
        for i in range(9):
            load(sp, win_r + i, 0, cols2(A["w_in_2"], 2 * P * i, 0, 0))
            if i == 1:
                c0 = 9 * 2 * P
                sp.wait_ge(n6.done[0], n6.done[1] + KT)
                sp.dma_start(alibi[:], C["alibi"]).then_inc(hy["in"], 16)
                sp.dma_start(causal[:], C["causal"]).then_inc(hy["in"], 16)
                sp.dma_start(wf[:], A["w_in_2"][:, c0:c0 + FOX_HEADS].rearrange("(k p) n -> p k n", p=P)).then_inc(hy["in"], 16)
        sp.wait_ge(hy["fb"], 1)
        for i, src in enumerate((f_8, f_m8)):
            sp.dma_start(gates[i], src[:]).then_inc(hy["stored"], 16)
        sp.wait_ge(hy["stored"], 32)
        sp.wait_ge(hy["ones"], 1)
        for i, dst in enumerate((qfx[HD:HD + 1], kfx[HD + 1:HD + 2])):
            sp.dma_start(dst, gates[i].unsqueeze(0)).then_inc(hy["aux"], 16)

    def hybrid_pool(pool):
        pool.wait_ge(n6.done[0], n6.done[1] + KT)
        pool.wait_ge(raw_done, win_r + 2)
        nc.gpsimd.memset(qfx[HD:HD + 2], 1.0)
        nc.gpsimd.memset(kfx[HD:HD + 2], 1.0).then_inc(hy["ones"], 1)

    HEAD_TILES = {}
    for T in range(14):
        i, h = divmod(T, 2)
        if i < 2:
            HEAD_TILES[T] = (qa[:, 2 * T], qa[:, 2 * T + 1])
        elif i == 2:
            if h == 0:
                HEAD_TILES[T] = (ka[:, 0], ka[:, 1])
        elif i < 5:
            j = T - 6
            HEAD_TILES[T] = (qfx[0:HD, 2 * j], qfx[0:HD, 2 * j + 1])
        else:
            j = T - 10
            HEAD_TILES[T] = (kfx[0:HD, 2 * j], kfx[0:HD, 2 * j + 1])

    def odd_heads(tiles):
        return sum(T in HEAD_TILES for T in range(tiles))

    def hybrid_pe(pe, norm):
        for i in range(9):
            pe.wait_ge(raw_done, win_r + i + 1)
            s = win_s + i
            for h in range(2):
                T = 2 * i + h
                if T >= 4:
                    pe.wait_ge(hy["ea"], T - 3)
                    pe.wait_ge(hy["ed"], odd_heads(T - 3))
                if T == 0:
                    first, second = project_pair(pe, s, (bank[0][:], bank[1][:]), norm.done)
                    first.then_inc(hy["hp"], 1)
                    second.then_inc(used, 1)
                    continue
                if T == 1:
                    continue
                if i >= 7:
                    w = slot_w(s)
                    for t in (2 * h, 2 * h + 1):
                        for k in range(KT):
                            ts = slice(t * P, (t + 1) * P)
                            ins = three_pass(bank[T % 4][:, (t % 2) * 256:(t % 2) * 256 + 256], (hh[:, k, ts], hl[:, k, ts]),
                                             (w[0][:, k], w[1][:, k]), k == 0, k == KT - 1)
                elif T == 5:
                    ins = project_rows(pe, s, P, P, lambda t: bank[T % 4][:, t * P:(t + 1) * P])
                else:
                    ins = project(s, h, bank[T % 4][:])
                ins.then_inc(used if h else hy["hp"], 1)
            if i == 4:
                ada_columns(pe, 5)
            if i == 1:
                pe.wait_ge(hy["wfh"], 2)
                for t in range(LT):
                    for k in range(KT):
                        ts = slice(t * P, (t + 1) * P)
                        ins = three_pass(bank[6][:, t * FOX_HEADS:(t + 1) * FOX_HEADS], (hh[:, k, ts], hl[:, k, ts]),
                                         (wf_h[:, k], wf_l[:, k]), k == 0, k == KT - 1)
                ins.then_inc(hy["ft"], 1)
            if i == 2:
                pe.wait_ge(hy["fc"], 1)
                for t in range(LT):
                    ins = nc.tensor.transpose(bank[7][0:FOX_HEADS, t * P:(t + 1) * P], f_rows[:, t * FOX_HEADS:(t + 1) * FOX_HEADS], ident[:])
                ins.then_inc(hy["ft"], 1)

    def tile_ready(eng, T):
        if T % 2:
            eng.wait_ge(used, win_s + T // 2 + 1)
        else:
            eng.wait_ge(hy["hp"], T // 2 + 1)

    def hybrid_act(act, splits):
        act.wait_ge(hy["in"], 48)
        nc.scalar.activation(wf_h[:], wf[:], ACT.Copy).then_inc(hy["wfh"], 1)
        for T in range(18):
            if T % 2 == 0:
                splits(T // 2)
            tile_ready(act, T)
            if T in HEAD_TILES:
                ins = nc.scalar.activation(HEAD_TILES[T][0], bank[T % 4][0:HD, :], ACT.Copy)
            elif T == 5:
                ins = nc.scalar.activation(va[:].rearrange("p t n -> p (t n)"), bank[T % 4][:], ACT.Copy)
            else:
                i, h = divmod(T, 2)
                ins = nc.scalar.activation(vfx[:, 2 * h:2 * h + 2, (i - 7) * 256:(i - 7) * 256 + 256],
                                           bank[T % 4][:].rearrange("p (t n) -> p t n", t=2), ACT.Copy)
            ins.then_inc(hy["ea"], 1)
            if T == 8:
                act.wait_ge(hy["ch"], 2)
                nc.scalar.activation(f_l[:], f_n[:], ACT.Exp).then_inc(hy["fa"], 1)
                act.wait_ge(hy["fa"], 1)
                nc.scalar.activation(f_l[:], f_l[:], ACT.Ln, bias=1.0).then_inc(hy["fa"], 1)

    def hybrid_dve(dve, splits):
        n = [0]

        def link(ins):
            n[0] += 1
            ins.then_inc(hy["ch"], 1)
            dve.wait_ge(hy["ch"], n[0])

        dve.wait_ge(hy["wfh"], 1)
        nc.vector.tensor_tensor(wf_l[:], wf[:], wf_h[:].bitcast(F32), ALU.subtract).then_inc(hy["wfh"], 1)
        for T in range(18):
            if T % 2 == 0:
                splits(T // 2)
            tile_ready(dve, T)
            if T in HEAD_TILES:
                nc.vector.tensor_copy(HEAD_TILES[T][1], bank[T % 4][HD:P, :]).then_inc(hy["ed"], 1)
            if T == 11:
                ada_mods(dve, 5)
            if T == 4:
                dve.wait_ge(hy["ft"], 1)
                nc.vector.tensor_copy(f_rows[:], bank[6][:, 0:LT * FOX_HEADS]).then_inc(hy["fc"], 1)
            if T == 7:
                dve.wait_ge(hy["ft"], 2)
                link(nc.vector.tensor_scalar(f_x[:], bank[7][0:FOX_HEADS, :], bf_col[:], None, ALU.add))
                link(nc.vector.scalar_tensor_tensor(f_n[:], f_x[:], -1.0, f_x[:], ALU.mult, ALU.min))
            if T == 10:
                dve.wait_ge(hy["fa"], 2)
                link(nc.vector.scalar_tensor_tensor(f_x[:], f_x[:], 0.0, f_l[:], ALU.min, ALU.subtract))
                nc.vector.memset(f_one[:], 1.0).then_inc(hy["ch"], 1)
                n[0] += 1
                dve.wait_ge(hy["ch"], n[0])
                link(nc.vector.tensor_tensor_scan(f_n[:], f_one[:], f_x[:], 0.0, ALU.mult, ALU.add))
                nc.vector.tensor_scalar(f_8[:], f_n[:], 1.0 / SCALE, None, ALU.mult)
                nc.vector.tensor_scalar(f_m8[:], f_n[:], -1.0 / SCALE, None, ALU.mult).then_inc(hy["fb"], 1)

    fo = sems("out", "pe ev")
    fo_dma = sem("out_stored")

    def out_pe(pe, norm):
        pe.wait_ge(norm.done[0], norm.done[1] + KT)
        for i in range(2 * LT):
            t, half = divmod(i, 2)
            if i >= 4:
                pe.wait_ge(fo["ev"], i - 3)
            for k in range(4):
                ins = nc.tensor.transpose(bank[i % 4][:, k * P:(k + 1) * P], x[:, 4 * half + k, t * P:(t + 1) * P], ident[:])
            ins.then_inc(fo["pe"], 1)

    def out_act(act):
        for i in range(2 * LT):
            t, half = divmod(i, 2)
            act.wait_ge(fo["pe"], i + 1)
            nc.scalar.activation(out_rows[:, t, half * 512:half * 512 + 512], bank[i % 4][:], ACT.Copy).then_inc(fo["ev"], 1)

    def out_sp(sp):
        for t in range(LT):
            sp.wait_ge(fo["ev"], 2 * t + 2)
            sp.dma_start(out[0, t * P:(t + 1) * P, :], out_rows[:, t]).then_inc(fo_dma, 16)
        sp.wait_ge(fo_dma, 16 * LT)

    back1 = Back("wo", "wo", A["attn_w_o"][0], 0, (hh, hl), lambda k: [(attn1.s["ol"], attn1.j0 + k + 1)])
    back2 = Back("hyout", "hyout", A["hy_w_out"][0], 1, (z_h, z_l), lambda k: [(hs["zl2"], k + 1)])
    back3 = Back("wout", "wout", A["w_out_2"], 2, (hh, hl),
                 lambda k: [(swa.s["ol"], swa.j0 + k + 1)] if k < 4 else [(fox.s["ol"], fox.j0 + k - 3)])
    n1 = mod_norm((xs["ev"], 0), 0, 0)
    n2 = mod_norm((back1.s["x"], 0), 0, 1, "up0_0")
    ffn0 = Ffn(0, A["ffn_w_up"][0], A["ffn_w_down"][0], n2, "ffn_conv_w", "ffn_conv_b", 0, False, ring["hyin"][0:3], 2)
    n3 = mod_norm((ffn0.s["xd"], KT), 1, 0, "hyin")
    n4 = mod_norm((back2.s["x"], 0), 1, 1, "up1_0")
    ffn1 = Ffn(1, A["ffn_w_up"][1], A["ffn_w_down"][1], n4, "ffn_conv_w", "ffn_conv_b", 0, False, ring["win"][0:3], 4)
    n5 = Norm((ffn1.s["xd"], KT), lambda t: col("final_g", t), None, None)
    n6 = mod_norm(n5.done, 2, 0, "win")
    n7 = mod_norm((back3.s["x"], 0), 2, 1, "up2_0")
    ffn2 = Ffn(2, A["w_up_2"], A["w_down_2"], n7, "conv_w_2", "conv_b_2", FF, True, None, None)
    n8 = Norm((ffn2.s["xd"], KT), lambda t: col("g_final_2", t), None, None)

    def ahead(split, eng, key, nxt):
        r0, s0, n_el, n = ring[key]

        def go(i):
            if i + 2 < n:
                split(eng, r0 + i + 2, s0 + i + 2, 0, n_el)
            elif nxt and not (i + 1 == n and nxt.startswith("up")):
                r, s, m, _ = ring[nxt]
                split(eng, r + i + 2 - n, s + i + 2 - n, 0, m)
        return go

    with nc.Block() as block:

        @block.sync
        def _(sp):
            prep_sp(sp)
            for i in range(2):
                load(sp, qkv_r + i, 0, cols2(A["attn_w_qkv"][0], 2 * P * i, 0, 0))
            filter_sp(sp)
            xload_sp(sp)
            sp.wait_ge(fl["ev"], 8 * GROUPS)
            sp.dma_start(rope[:], C["rope"].rearrange("s p l -> p s l")).then_inc(rp_in, 16)
            for i in range(2, 6):
                load(sp, qkv_r + i, 0, cols2(A["attn_w_qkv"][0], 2 * P * i, 0, 0))
            back1.sp(sp)
            ffn0.sp(sp)
            hyena_sp(sp)
            back2.sp(sp)
            ffn1.sp(sp)
            hybrid_sp(sp)
            back3.sp(sp)
            ffn2.sp(sp)
            out_sp(sp)

        @block.gpsimd
        def _(pool):
            ada_load_first(pool, 0)
            filter_pool(pool)
            ada_load_first(pool, 1)
            n1.pool(pool)
            qkv_pool(pool)
            ada_load_rest(pool, 1)
            n2.pool(pool)
            for T in (2, 3):
                ada_load_first(pool, T)
                ada_load_rest(pool, T)
            n3.pool(pool)
            n4.pool(pool)
            pool.wait_ge(used, out_s + 4)
            for T in (4, 5):
                ada_load_first(pool, T)
                ada_load_rest(pool, T)
            n5.pool(pool)
            n6.pool(pool)
            hybrid_pool(pool)
            n7.pool(pool)
            n8.pool(pool)

        @block.scalar
        def _(act):
            prep_act(act)
            silu_act(act)
            sin_act(act)
            tables_act(act, "tk", tk_h)
            filter_act(act)
            for i in range(2):
                act.wait_ge(fl_st[i], 16 * 4 * GROUPS)
            split_hi(act, qkv_r, qkv_s, 0, UNIT)
            split_hi(act, qkv_r + 1, qkv_s + 1, 0, UNIT)
            xload_act(act)
            n1.act(act)
            qkv_act(act, ahead(split_hi, act, "qkv", "wo"))
            attn1.act(act)
            back1.act(act, ahead(split_hi, act, "wo", "up0_0"))
            n2.act(act)
            ffn0.act(act)
            n3.act(act)
            hyena_in_act(act)
            hyena_act(act)
            back2.act(act, ahead(split_hi, act, "hyout", "up1_0"))
            n4.act(act)
            ffn1.act(act)
            n5.act(act)
            n6.act(act)
            hybrid_act(act, ahead(split_hi, act, "win", "wout"))
            swa.act(act)
            fox.act(act)
            back3.act(act, ahead(split_hi, act, "wout", "up2_0"))
            n7.act(act)
            ffn2.act(act)
            n8.act(act)
            out_act(act)

        @block.vector
        def _(dve):
            prep_dve(dve)
            sin_dve(dve)
            tables_dve(dve, "tk", tk_h, tk_l, 0)
            filter_dve(dve)
            ada_mods(dve, 0)
            split_lo(dve, qkv_r, qkv_s, 0, UNIT)
            split_lo(dve, qkv_r + 1, qkv_s + 1, 0, UNIT)
            n1.dve(dve)
            qkv_dve(dve, ahead(split_lo, dve, "qkv", "wo"))
            ada_zero(dve, 1)
            attn1.dve(dve, lambda i: ada_step(dve, 1, i // 8, 0) if i % 8 == 5 else None)
            ada_mods(dve, 1)
            back1.dve(dve, ahead(split_lo, dve, "wo", "up0_0"))
            n2.dve(dve)
            ffn0.dve(dve)
            n3.dve(dve)
            ada_step(dve, 3, KT - 1, 0)
            hyena_in_dve(dve)
            hyena_dve(dve)
            back2.dve(dve, ahead(split_lo, dve, "hyout", "up1_0"))
            n4.dve(dve)
            ffn1.dve(dve)
            n5.dve(dve)
            n6.dve(dve)
            ada_step(dve, 5, KT - 1, 0)
            hybrid_dve(dve, ahead(split_lo, dve, "win", "wout"))
            swa.dve(dve)
            fox.dve(dve)
            back3.dve(dve, ahead(split_lo, dve, "wout", "up2_0"))
            n7.dve(dve)
            ffn2.dve(dve)
            n8.dve(dve)

        @block.tensor
        def _(pe):
            prep_pe(pe)
            pe.wait_ge(prep["cols"], 2)
            sin_pe(pe)
            filter_pe(pe)
            ada_columns(pe, 0)
            xload_pe(pe)
            n1.pe(pe)
            qkv_pe(pe, n1)
            attn1.pe(pe, [(qk["done"], NQK), (qk["vd"], 1)])
            ada_columns(pe, 1)
            back1.pe(pe)
            n2.pe(pe)
            ffn0.pe(pe)
            n3.pe(pe)
            hyena_in_pe(pe, n3)
            hyena_pe(pe)
            back2.pe(pe)
            n4.pe(pe)
            ffn1.pe(pe)
            n5.pe(pe)
            n6.pe(pe)
            hybrid_pe(pe, n6)
            pe.wait_ge(hy["in"], 48)
            swa.pe(pe, [(hy["ea"], 18), (hy["ed"], len(HEAD_TILES)), (hy["aux"], 32)])
            fox.pe(pe, [(hy["aux"], 32), (swa.s["ol"], swa.j0 + SWA_HEADS // 2)])
            back3.pe(pe)
            n7.pe(pe)
            ffn2.pe(pe)
            n8.pe(pe)
            out_pe(pe, n8)


USED_INPUTS = ["x", "c", "ada_w", "ada_b", "norm1_g", "norm2_g", "final_g", "attn_w_qkv", "attn_w_o", "attn_q_gain",
               "attn_k_gain", "hy_w_in", "hy_conv_w", "hy_conv_b", "hy_f_w1", "hy_f_b1", "hy_f_w2", "hy_f_b2", "hy_f_w3",
               "hy_f_freq", "hy_skip", "hy_w_out", "ffn_w_up", "ffn_conv_w", "ffn_conv_b", "ffn_w_down", "c_2", "w_ada_2",
               "b_ada_2", "g_attn_2", "w_in_2", "b_f_2", "sinks_2", "w_out_2", "g_mlp_2", "w_up_2", "conv_w_2", "conv_b_2",
               "w_down_2", "g_final_2"]


def kernel(**inputs):
    import concourse.bacc as bacc
    from concourse.bass_utils import run_bass_kernel_spmd

    nc = bacc.Bacc("TRN2", target_bir_lowering=False, num_devices=1)
    arrays, A, C = {}, {}, {}
    for name in USED_INPUTS:
        a = np.ascontiguousarray(inputs[name])
        arrays[f"in_{name}"] = a
        A[name] = nc.dram_tensor(f"in_{name}", a.shape, mybir.dt.from_np(a.dtype), kind="ExternalInput").ap()
    for name, a in shape_constants().items():
        a = np.ascontiguousarray(a)
        arrays[f"table_{name}"] = a
        C[name] = nc.dram_tensor(f"table_{name}", a.shape, mybir.dt.from_np(a.dtype), kind="ExternalInput").ap()
    out = nc.dram_tensor("out", (1, L, D), F32, kind="ExternalOutput").ap()
    build_program(nc, A, C, out)
    result = run_bass_kernel_spmd(nc, [arrays], core_ids=[0])
    return result.results[0]["out"]
```

```python
import math

import concourse.bass as bass
import numpy as np
from concourse import mybir
from concourse.alu_op_type import AluOpType as ALU

F32 = mybir.dt.float32
F32R = mybir.dt.float32r
ACT = mybir.ActivationFunctionType
AX = mybir.AxisListType

P = 128
L = 512
D = 1024
KT = D // P
LT = L // P
FF = 2816
FT = FF // P
FH = FT // 2
EPS = 1e-6
HD = 64
HEADS = 16
KV_HEADS = 4
SWA_HEADS = 8
SWA_KV = 2
FOX_HEADS = 8
WINDOW = 128
NEG = -1e30
SCALE = HD ** -0.5
GRID_W = 64
ORDERS = 2
EMB = 33
FW = 64
CH = 256
NCH = D // CH
TWO_PI = 2.0 * math.pi
TWO_PI_HI = 6.28125
TWO_PI_LO = float(np.float32(TWO_PI - TWO_PI_HI))
ROUND = 1.5 * 2.0 ** 23
PI_BELOW = 3.1415925

VECTORS = [
    ("c", KT), ("c_2", KT), ("ada_b", 2 * 6 * KT), ("b_ada_2", 6 * KT),
    ("norm1_g", 2 * KT), ("norm2_g", 2 * KT), ("final_g", KT),
    ("g_attn_2", KT), ("g_mlp_2", KT), ("g_final_2", KT),
    ("ffn_conv_w", 2 * 3 * FT), ("ffn_conv_b", 2 * FT),
    ("hy_conv_w", 3 * 3 * KT), ("hy_conv_b", 3 * KT), ("hy_skip", ORDERS * KT),
    ("conv_w_2", 3 * 2 * FT), ("conv_b_2", 2 * FT),
]
COL = {}
_at = 0
for _name, _n in VECTORS:
    COL[_name] = _at
    _at += _n
VECTOR_ROWS = _at
PT_TILES = -(-VECTOR_ROWS // P)


def shape_constants():
    out = {}
    n = np.arange(L, dtype=np.float64)
    w = 2.0 * np.pi * (n + 0.5) / (2 * L)
    kern = np.outer(n, w)
    sig = np.outer(n + 0.5, w)
    out["dft_kernel"] = np.stack([np.cos(kern), np.sin(kern)]).astype(np.float32)
    out["dft_signal"] = np.stack([np.cos(sig), np.sin(sig)]).astype(np.float32)
    t = np.linspace(0.0, 1.0, L, dtype=np.float32)
    bands = (EMB - 1) // 2
    wl = (np.float32(2.0 * math.pi) * np.arange(L, dtype=np.float32) / np.float32(L)).astype(np.float32)
    f = np.linspace(1e-4, bands - 1, bands, dtype=np.float32)
    ang = (wl[:, None] * f[None, :]).astype(np.float32).astype(np.float64)
    out["pos_t"] = np.concatenate([t[:, None], np.cos(ang), -np.sin(ang)], axis=1).astype(np.float32).T.copy()
    deltas = np.abs(np.linspace(math.log(1e-2) / 1.5, math.log(1e-2) / 0.3, D, dtype=np.float32))
    out["decay"] = np.exp(-(t[:, None] * deltas[None, :]).astype(np.float64)).astype(np.float32)
    nf = HD // 4
    inv = (np.float32(1.0) / (np.float32(10000.0) ** (np.arange(nf, dtype=np.float32) / np.float32(nf)))).astype(np.float32)
    tok = np.arange(L)
    row = (tok // GRID_W).astype(np.float32)[:, None] * inv
    col = (tok % GRID_W).astype(np.float32)[:, None] * inv
    a = np.concatenate([row, col], axis=1).astype(np.float32).astype(np.float64)
    per_channel = np.repeat(a, 2, axis=1).T
    both = np.concatenate([per_channel, per_channel], axis=0)
    out["rope"] = np.stack([np.cos(both), np.sin(both)]).astype(np.float32)
    perm = np.zeros((P, P), np.float32)
    for m in range(0, P, 2):
        perm[m + 1, m] = -1.0
        perm[m, m + 1] = 1.0
    out["swap"] = perm
    out["identity"] = np.eye(P, dtype=np.float32)
    head_mean = np.zeros((P, 2), np.float32)
    head_mean[:HD, 0] = 1.0 / HD
    head_mean[HD:, 1] = 1.0 / HD
    out["head_mean"] = head_mean
    q = np.arange(P)[:, None]
    k = np.arange(2 * P)[None, :]
    dist = (P + q) - k
    valid = (dist >= 0) & (dist < WINDOW)
    slopes = np.exp2(-8.0 * (np.arange(SWA_HEADS, dtype=np.float32) + 1) / SWA_HEADS)
    b = -slopes[None, :, None] * dist[:, None, :].astype(np.float32)
    out["alibi"] = np.where(valid[:, None, :], b, np.float32(NEG)).astype(np.float32)
    out["causal"] = np.where(np.arange(P)[None, :] <= q, 0.0, NEG).astype(np.float32)
    return out


def build_program(nc, A, C, out):
    CONST0 = 16512
    X0 = CONST0 + 8192
    HH0 = X0 + KT * L * 4
    HL0 = HH0 + KT * L * 4
    UNIT = 2 * KT * P
    RAW0 = HL0 + KT * L * 4
    HI0 = RAW0 + 2 * UNIT * 4
    LO0 = HI0 + 2 * UNIT * 4
    AREA = LO0 + 2 * UNIT * 4
    TOP = 229344
    TRIPLE = 3 * D
    ADA0 = (TOP - 3 * TRIPLE * 4) // 32 * 32

    def at(name, offset, shape, dt=F32):
        return nc.alloc_sbuf_tensor_at(name, shape, dt, offset=offset)

    def sizeof(shape):
        return 4 * int(np.prod(shape[1:]))

    def region(start, *wanted):
        made = []
        for name, shape, dt in wanted:
            made.append(at(name, start, shape, dt))
            start += (sizeof(shape) + 31) // 32 * 32
            assert start <= TOP, name
        return made

    (ident, ones, eps_col, vec, mod, gsc, silu_c, head_mean, swap_m, gain_cols, fcols, rms_cols, rstd_cols,
     mxs, nmx, sums, recs, es, bf_col, sink_b, nrm_cols, fg2, fgs) = region(
        CONST0,
        ("ident", [P, P], F32), ("ones", [P, 32], F32), ("eps_col", [P, 1], F32),
        ("vec", [P, VECTOR_ROWS], F32), ("mod", [P, 3, 6 * KT], F32), ("gsc", [P, 3, 2, KT], F32),
        ("silu_c", [P, 2, KT], F32), ("head_mean", [P, 2], F32), ("swap_m", [P, P], F32),
        ("gain_cols", [P, 2], F32), ("fcols", [FW, 3], F32), ("rms_cols", [P, 2, 8], F32),
        ("rstd_cols", [P, 2, 8], F32), ("mxs", [P, 4], F32), ("nmx", [P, 4], F32), ("sums", [P, 4], F32),
        ("recs", [P, 4], F32), ("es", [P, 4], F32), ("bf_col", [FOX_HEADS, 1], F32),
        ("sink_b", [P, SWA_HEADS], F32), ("nrm_cols", [P, 4], F32), ("fg2", [P, KT, 2], F32), ("fgs", [P, KT], F32))
    x = at("x_res", X0, [P, KT, L])
    hh = at("h_hi", HH0, [P, KT, L], F32R)
    hl = at("h_lo", HL0, [P, KT, L], F32R)
    raw = [at(f"w_raw{i}", RAW0 + i * UNIT * 4, [P, UNIT]) for i in range(2)]
    whi = [at(f"w_hi{i}", HI0 + i * UNIT * 4, [P, UNIT], F32R) for i in range(2)]
    wlo = [at(f"w_lo{i}", LO0 + i * UNIT * 4, [P, UNIT], F32R) for i in range(2)]
    ada_raw = [at(f"ada_raw{i}", ADA0 + i * TRIPLE * 4, [P, TRIPLE]) for i in range(2)]
    ada_acc = at("ada_acc", ADA0 + 2 * TRIPLE * 4, [P, TRIPLE])
    bank = [nc.alloc_psum_tensor(f"bank{i}", [P, 512], F32) for i in range(8)]

    spectra = nc.dram_tensor("spectra", (ORDERS, NCH, P, LT, 2, CH), F32).ap()

    sum_f, dif_f = region(X0, ("sum_f", [P, LT, 512], F32), ("dif_f", [P, LT, 512], F32))
    decay = at("decay_sb", HH0, [P, LT, D])
    fw3 = at("fw3", HL0, [FW, 4 * D])
    fwd, bwd, afwd, abwd, asum, spec_out, rn_row, zt, a1, a2, fw1, fw2, vec_raw = region(
        HI0, ("fwd", [P, 2, 512], F32), ("bwd", [P, 2, 512], F32), ("afwd", [P, 512], F32),
        ("abwd", [P, 512], F32), ("asum", [P, 2, 512], F32), ("spec_out", [P, 2, 512], F32),
        ("rn_row", [P, 512], F32), ("pos_sb", [EMB, L], F32), ("a1", [FW, L], F32),
        ("a2", [FW, L], F32), ("fw1", [EMB, FW], F32), ("fw2", [FW, FW], F32),
        ("vec_raw", [P, PT_TILES, P], F32))
    assert HI0 + 29184 + sizeof([P, PT_TILES, P]) <= AREA
    tk_h, tk_l, sum_h, sum_l, dif_h, dif_l = region(
        AREA, ("tk_h", [P, 2, LT, 512], F32R), ("tk_l", [P, 2, LT, 512], F32R),
        ("sum_h", [P, LT, 512], F32R), ("sum_l", [P, LT, 512], F32R),
        ("dif_h", [P, LT, 512], F32R), ("dif_l", [P, LT, 512], F32R))
    assert AREA + 65536 <= ADA0
    arg, turns = region(AREA + 32768, ("sin_arg", [FW, L], F32), ("sin_turns", [FW, L], F32))
    x_rows = at("x_rows", HH0, [P, LT, D])

    NORM0 = AREA + 57344
    nsq, nt1, nacc = region(NORM0, ("norm_sq", [P, 2, 512], F32), ("norm_t", [P, 2, 512], F32),
                            ("norm_sum", [P, 512], F32))
    wacc, = region(AREA + 45056, ("norm_wsum", [P, 512], F32))
    ada_row, = region(NORM0 + 4096, ("ada_row", [3 * 32, 2, 512], F32))
    ada_rows, = region(NORM0 + 10240, ("ada_rows", [3 * KT, P], F32))
    assert NORM0 + 10752 <= ADA0

    qh, kh, vh, rope, qsq, qf, qt = region(
        AREA, ("q_heads", [HD, HEADS, L], F32), ("k_heads", [HD, KV_HEADS, L], F32),
        ("v_rows", [P, LT, KV_HEADS * HD], F32), ("rope_sb", [P, 2, L], F32),
        ("q_sq", [P, 2, 512], F32), ("q_f", [P, 2, 512], F32), ("q_t", [P, 2, 512], F32))
    rx, = region(AREA + 61440, ("head_factors", [P, 2, 512], F32))
    assert AREA + 65536 <= ADA0
    probs1, = region(AREA + 45056, ("probs1", [P, 2, 512], F32))
    probsT1, = region(AREA + 49152, ("probsT1", [P, 2, LT, 512], F32))

    hid_h, hid_l, fc, fs, fh = region(
        AREA, ("hid_h", [P, FH, L], F32R), ("hid_l", [P, FH, L], F32R), ("conv_g", [P, 2, L], F32),
        ("silu_g", [P, 2, L], F32), ("hid_f", [P, 2, L], F32))
    fv, = region(AREA + 69632, ("conv_v", [P, 2, L], F32))

    u, td_h, td_l, y_h, y_l, pt1, y_f = region(
        AREA, ("hyena_u", [P, 3 * KT, L], F32), ("td_h", [P, 2, LT, 512], F32R), ("td_l", [P, 2, LT, 512], F32R),
        ("y_h", [P, LT, 2, CH], F32R), ("y_l", [P, LT, 2, CH], F32R), ("pt1", [P, 2, CH], F32),
        ("y_f", [P, 2, CH], F32))
    assert sizeof([P, LT, 2, CH]) == UNIT * 4
    y_h = (at("y_h_even", HI0, [P, LT, 2, CH], F32R), y_h)
    y_l = (at("y_l_even", LO0, [P, LT, 2, CH], F32R), y_l)
    pt2, = region(CONST0 + 8192 - 2048, ("pt2", [P, 2, CH], F32))
    z_h = at("z_hi", AREA + KT * L * 4, [P, KT, L], F32R)
    z_l = at("z_lo", AREA + 2 * KT * L * 4, [P, KT, L], F32R)
    zt_h = hh[:].rearrange("p a b -> p (a b)").rearrange("p (n c) -> p n c", n=LT)
    zt_l = hl[:].rearrange("p a b -> p (a b)").rearrange("p (n c) -> p n c", n=LT)

    qa, ka, va, qfx, kfx, vfx, alibi, causal, probs2, probsT2, biased = region(
        AREA, ("qa", [HD, SWA_HEADS, L], F32), ("ka", [HD, SWA_KV, L], F32), ("va", [P, LT, SWA_KV * HD], F32),
        ("qfx", [HD + 2, FOX_HEADS, L], F32), ("kfx", [HD + 2, FOX_HEADS, L], F32),
        ("vfx", [P, LT, FOX_HEADS * HD], F32), ("alibi_sb", [P, SWA_HEADS, 2 * P], F32),
        ("causal_sb", [P, P], F32), ("probs2", [P, 2, 512], F32), ("probsT2", [P, 2, LT, 512], F32),
        ("biased", [P, 2, 2 * P], F32))
    wf, wf_h, wf_l = region(
        CONST0 + 8192 - 2048, ("wf", [P, KT, FOX_HEADS], F32), ("wf_h", [P, KT, FOX_HEADS], F32R),
        ("wf_l", [P, KT, FOX_HEADS], F32R))
    out_rows = at("out_rows", AREA, [P, LT, D])

    def sem(name):
        return nc.alloc_semaphore(name)

    def sems(prefix, names):
        return {n: sem(f"{prefix}_{n}") for n in names.split()}

    raw_in = [sem("raw_in0"), sem("raw_in1")]
    raw_done, hi_done, used = sem("raw_done"), sem("hi_done"), sem("units_used")
    ada_in = [sem("ada_in0"), sem("ada_in1")]
    ada_st, ada_mm, ada_ev = sem("ada_steps"), sem("ada_sums"), sem("ada_mods")
    ada_ro, ada_sd, ada_tr = sem("ada_rows_out"), sem("ada_spread"), sem("ada_turned")
    ada_sd0 = sem("ada_spread_first")
    prep = sems("prep", "small vecs consts x trans cols silu")
    sn = sems("sin", "pe chain act")
    fl = sems("filt", "in fb fbused fa as_ pm nmm nrec nbt nrow phi plo mhi mlo sp ev")
    xs = sems("xload", "in pe ev")

    own_step, own_steps = sem("vector_own_step"), [0]

    def counted(ins):
        own_steps[0] += 1
        ins.then_inc(own_step, 1)
        return own_steps[0]

    def chained(dve, ins):
        dve.wait_ge(own_step, counted(ins))

    def load(sp, r, it, parts):
        if r >= 2:
            sp.wait_ge(raw_done, r - 1 + 2 * it)
        for dst, src in parts(raw[r % 2]):
            sp.dma_start(dst, src).then_inc(raw_in[r % 2], 16)

    def split_hi(act, r, s, it, n):
        act.wait_ge(raw_in[r % 2], 32 * (r // 2 + 1) + 32 * it)
        if s >= 2:
            act.wait_ge(used, s - 1 + 2 * it)
        nc.scalar.activation(whi[s % 2][:, :n], raw[r % 2][:, :n], ACT.Copy).then_inc(hi_done, 1)

    def split_lo(dve, r, s, it, n):
        dve.wait_ge(hi_done, s + 1 + 2 * it)
        nc.vector.tensor_tensor(wlo[s % 2][:, :n], raw[r % 2][:, :n], whi[s % 2][:, :n].bitcast(F32),
                                ALU.subtract).then_inc(raw_done, 1)

    def three_pass(out_ap, lhs, rhs, first, last, check=True):
        nc.tensor.matmul(out_ap, lhs[0], rhs[0], start=first, stop=False)
        nc.tensor.matmul(out_ap, lhs[0], rhs[1], start=False, stop=False)
        return nc.tensor.matmul(out_ap, lhs[1], rhs[0], start=False, stop=last)

    def over(eng, n, body):
        pairs = n // 2
        if pairs > 1:
            with eng.Fori(0, pairs) as it:
                body(0, it)
                body(1, it)
        elif pairs == 1:
            body(0, 0)
            body(1, 0)
        if n % 2:
            body(n - 1, 0)

    def split_ahead(eng, split, n_units, r0, s0, n_el, nxt, body, take=2):
        def unit(c, it):
            split(eng, r0 + c + 2, s0 + c + 2, it, n_el)
            body(c, it)
        over(eng, n_units - 2, unit)
        for k in range(2):
            if nxt and k < take:
                split(eng, nxt[0] + k, nxt[1] + k, 0, nxt[2])
            body(n_units - 2 + k, 0)

    ring = {}
    r_at = s_at = 0
    for name, units, n_el, weights in (
            [("tk", 2, UNIT, False), ("qkv", 6, UNIT, True), ("wo", 4, UNIT, True)]
            + [(f"{k}0_{h}", FH if k == "up" else KT, UNIT if k == "up" else FH * P, True) for h in (0, 1) for k in ("up", "dn")]
            + [("hyin", 12, UNIT, True), ("td", 2, UNIT, False), ("spec", ORDERS * NCH, UNIT, False), ("hyout", 4, UNIT, True)]
            + [(f"{k}1_{h}", FH if k == "up" else KT, UNIT if k == "up" else FH * P, True) for h in (0, 1) for k in ("up", "dn")]
            + [("win", 9, UNIT, True), ("wout", 4, UNIT, True)]
            + [(f"{k}2_{h}", FH if k == "up" else KT, UNIT if k == "up" else FH * P, True) for h in (0, 1) for k in ("up", "dn")]):
        ring[name] = (r_at, s_at, n_el, units)
        r_at += units
        s_at += units if weights else 0

    def cols2(w, c0, it_step, it, c1=None):
        src = w.rearrange("(k p) n -> p k n", p=P)

        def parts(slot):
            v = slot[:].rearrange("p (k n) -> p k n", k=KT)
            if c1 is None:
                return [(v[:, k:k + KT // 2, :], src[:, k:k + KT // 2, bass.ds(c0 + it_step * it, 2 * P)])
                        for k in (0, KT // 2)]
            return [(v[:, :, 0:P], src[:, :, bass.ds(c0 + it_step * it, P)]),
                    (v[:, :, P:2 * P], src[:, :, bass.ds(c1 + it_step * it, P)])]
        return parts

    def down_parts(w, half, c, it):
        src = w[half * FH * P:(half + 1) * FH * P, :].rearrange("(k p) n -> p k n", p=P)

        def parts(slot):
            v = slot[:, :FH * P].rearrange("p (k n) -> p k n", k=FH)
            return [(v[:, a:b, :], src[:, a:b, bass.ds(c * P + 2 * P * it, P)]) for a, b in ((0, 6), (6, FH))]
        return parts

    def slot_w(s):
        return (whi[s % 2][:].rearrange("p (k n) -> p k n", k=KT), wlo[s % 2][:].rearrange("p (k n) -> p k n", k=KT))

    def slot_d(s):
        return tuple(w[s % 2][:, :FH * P].rearrange("p (k n) -> p k n", k=FH) for w in (whi, wlo))

    def col(name, i):
        return vec[:, COL[name] + i:COL[name] + i + 1]

    def dcol(name, i, it, step):
        if isinstance(it, int):
            return col(name, i + step * it)
        return vec[:, bass.ds(COL[name] + i + step * it, 1)]

    def tile_of(t, i, it, step, sl=slice(None)):
        if isinstance(it, int):
            return t[:, i + step * it, sl]
        return t[:, bass.ds(i + step * it, 1), sl].rearrange("p a n -> p (a n)")

    def ada_source(T, c, it):
        w = A["ada_w"][T // 2] if T < 4 else A["w_ada_2"]
        return w[bass.ds(c * P + 2 * P * it, P), (T % 2) * TRIPLE:(T % 2 + 1) * TRIPLE]

    def ada_load_one(pool, T, c, it):
        if c >= 2:
            pool.wait_ge(ada_st, 9 * T + c + 2 * it)
        elif T:
            pool.wait_ge(ada_st, 9 * T - 1 + c)
        pool.dma_start(ada_raw[c % 2][:], ada_source(T, c, it)).then_inc(ada_in[c % 2], 16)

    def ada_load_first(pool, T):
        ada_zero(pool, T)
        ada_load_one(pool, T, 0, 0)
        ada_load_one(pool, T, 1, 0)

    def ada_load_rest(pool, T, norm=None):
        if norm:
            norm.pool_zero(pool)
        with pool.Fori(0, KT // 2 - 1) as it:
            for c in range(2):
                ada_load_one(pool, T, 2 + c, it)
                if norm:
                    norm.pool_square(pool, c, it)

    def ada_zero(pool, T):
        if T:
            pool.wait_ge(ada_mm, T)
        nc.gpsimd.memset(ada_acc[:], 0.0).then_inc(ada_st, 1)

    def ada_step(dve, T, c, it):
        dve.wait_ge(ada_in[c % 2], 16 * (4 * T + c // 2 + 1) + 16 * it)
        dve.wait_ge(ada_st, 9 * T + 1 + c + 2 * it)
        which = T // 4
        s = silu_c[:, which, c:c + 1] if isinstance(it, int) else silu_c[:, which, bass.ds(c + 2 * it, 1)]
        nc.vector.scalar_tensor_tensor(ada_acc[:], ada_raw[c % 2][:], s, ada_acc[:], ALU.mult, ALU.add)\
          .then_inc(ada_st, 1)

    def ada_sum(pe, T):
        pe.wait_ge(ada_st, 9 * T + 9)
        for j in range(6):
            last = nc.tensor.matmul(bank[6 + j // 3][32 * (j % 3):32 * (j % 3) + 32, :], ones[:],
                                    ada_acc[:, j * 512:(j + 1) * 512], start=True, stop=True)
        last.then_inc(ada_mm, 1)

    def ada_evict(dve, T):
        dve.wait_ge(ada_mm, T + 1)
        for b in range(2):
            nc.vector.tensor_copy(ada_row[:, b], bank[6 + b][0:96, :]).then_inc(ada_ro, 1)

    def ada_spread(queue, T):
        for b in range(2):
            queue.wait_ge(ada_ro, 2 * T + b + 1)
            for a in range(3):
                r = 12 * b + 4 * a
                queue.dma_start(ada_rows[r:r + 4, :], ada_row[32 * a:32 * a + 1, b].rearrange("p (q c) -> p q c", c=P))\
                    .then_inc(ada_sd if T else ada_sd0, 16)

    def ada_turn(pe, T):
        pe.wait_ge(ada_sd if T else ada_sd0, 16 * 6 * max(T, 1))
        nc.tensor.transpose(bank[6][:, 0:3 * KT], ada_rows[:], ident[0:3 * KT, 0:3 * KT]).then_inc(ada_tr, 1)

    def ada_mods(dve, T):
        dve.wait_ge(ada_tr, T + 1)
        b, h = T // 2, T % 2
        bias = COL["ada_b"] + T * 3 * KT if T < 4 else COL["b_ada_2"] + h * 3 * KT
        gain = (COL["norm1_g"] if h == 0 else COL["norm2_g"]) + b * KT if b < 2 else \
            COL["g_attn_2"] if h == 0 else COL["g_mlp_2"]
        m = mod[:, b, h * 3 * KT:(h + 1) * 3 * KT]
        nc.vector.tensor_tensor(m, bank[6][:, 0:3 * KT], vec[:, bias:bias + 3 * KT], ALU.add).then_inc(ada_ev, 1)
        dve.wait_ge(ada_ev, 2 * T + 1)
        nc.vector.scalar_tensor_tensor(gsc[:, b, h, :], m[:, KT:2 * KT], 1.0, vec[:, gain:gain + KT],
                                       ALU.add, ALU.mult).then_inc(ada_ev, 1)

    vec_pieces = []
    for name, n in VECTORS:
        rows = A[name]
        rows = rows.rearrange(" ".join("abcd"[:len(rows.shape)]) + " -> (" + " ".join("abcd"[:len(rows.shape)]) + ")") \
            if len(rows.shape) > 1 else rows
        rows = rows.rearrange("(r p) -> r p", p=P)
        done = 0
        while done < n:
            g = COL[name] + done
            take = min(n - done, P - g % P)
            vec_pieces.append((vec_raw[g % P:g % P + take, g // P, :], rows[done:done + take, :]))
            done += take

    def column(name):
        a = A[name]
        return a.rearrange("a p -> p a") if len(a.shape) == 2 else a.rearrange("(p a) -> p a", a=1)

    SMALL = [(ident[:], C["identity"]), (head_mean[:], C["head_mean"]), (swap_m[:], C["swap"]),
             (gain_cols[0:HD, 0:1], column("attn_q_gain")), (gain_cols[HD:P, 0:1], column("attn_q_gain")),
             (gain_cols[0:HD, 1:2], column("attn_k_gain")), (gain_cols[HD:P, 1:2], column("attn_k_gain")),
             (bf_col[:], column("b_f_2")),
             (sink_b[:], A["sinks_2"].rearrange("(a h) -> a h", a=1).broadcast_to([P, SWA_HEADS]))]
    FIRST = [(zt[:], C["pos_t"]), (fw1[:], A["hy_f_w1"][0]), (fw2[:], A["hy_f_w2"][0]),
             (fcols[:, 0:1], column("hy_f_b1")), (fcols[:, 1:2], column("hy_f_b2")), (fcols[:, 2:3], column("hy_f_freq"))]
    FILT = [(fw3[:], A["hy_f_w3"][0]), (decay[:], C["decay"].rearrange("(t p) d -> p t d", p=P))]

    def table_parts(table, part):
        src = C[table][part].rearrange("(t p) k -> p t k", p=P)

        def parts(slot):
            v = slot[:].rearrange("p (t k) -> p t k", t=LT)
            return [(v[:, t:t + 2, :], src[:, t:t + 2, :]) for t in (0, 2)]
        return parts

    def prep_sp(sp):
        for dst, src in FIRST[:3]:
            sp.dma_start(dst, src).then_inc(prep["small"], 16)
        sp.wait_ge(prep["small"], 16 * len(FIRST))
        for dst, src in FILT:
            sp.dma_start(dst, src).then_inc(fl["in"], 16)
        for part in range(2):
            load(sp, ring["tk"][0] + part, 0, table_parts("dft_kernel", part))
        for dst, src in vec_pieces:
            sp.dma_start(dst, src).then_inc(prep["vecs"], 16)

    def prep_act(act):
        for dst, src in FIRST[3:]:
            act.dma_start(dst, src).then_inc(prep["small"], 16)
        for dst, src in SMALL:
            act.dma_start(dst, src).then_inc(prep["consts"], 16)

    def ones_dve(dve):
        nc.vector.memset(ones[:], 1.0)
        nc.vector.memset(eps_col[:], EPS).then_inc(prep["cols"], 1)

    def prep_dve(dve):
        dve.wait_ge(prep["trans"], 1)
        nc.vector.tensor_copy(vec[:, 0:4 * P], bank[4][:, 0:4 * P])
        nc.vector.tensor_copy(vec[:, 4 * P:VECTOR_ROWS], bank[5][:, 0:VECTOR_ROWS - 4 * P]).then_inc(prep["cols"], 1)

    def prep_pe(pe):
        pe.wait_ge(prep["vecs"], 16 * len(vec_pieces))
        pe.wait_ge(prep["consts"], 16 * len(SMALL))
        for t in range(PT_TILES):
            n = min(P, VECTOR_ROWS - t * P)
            last = nc.tensor.transpose(bank[4 + t // 4][:, (t % 4) * P:(t % 4) * P + n], vec_raw[0:n, t, :], ident[0:n, 0:n])
        last.then_inc(prep["trans"], 1)

    def silu_act(act):
        act.wait_ge(prep["cols"], 2)
        nc.scalar.activation(silu_c[:].rearrange("p a k -> p (a k)"), vec[:, COL["c"]:COL["c"] + 2 * KT], ACT.Silu)\
          .then_inc(prep["silu"], 1)

    def sin_pe(pe):
        pe.wait_ge(prep["small"], 16 * len(FIRST))
        nc.tensor.matmul(bank[0][0:FW, :], fw1[:], zt[:], start=True, stop=True).then_inc(sn["pe"], 1)
        pe.wait_ge(sn["act"], 1)
        nc.tensor.matmul(bank[1][0:FW, :], fw2[:], a1[:], start=True, stop=True).then_inc(sn["pe"], 1)

    def sin_dve(dve):
        n = 0
        for i in range(2):
            dve.wait_ge(sn["pe"], i + 1)
            for step in range(6):
                if n:
                    dve.wait_ge(sn["chain"], n)
                if step == 0:
                    if i:
                        dve.wait_ge(sn["act"], i)
                    ins = nc.vector.tensor_scalar(arg[:], bank[i][0:FW, :], fcols[:, i:i + 1], fcols[:, 2:3], ALU.add, ALU.mult)
                elif step == 1:
                    ins = nc.vector.tensor_scalar(turns[:], arg[:], 1.0 / TWO_PI, ROUND, ALU.mult, ALU.add)
                elif step == 2:
                    ins = nc.vector.tensor_scalar(turns[:], turns[:], ROUND, None, ALU.subtract)
                elif step == 3:
                    ins = nc.vector.scalar_tensor_tensor(arg[:], turns[:], -TWO_PI_HI, arg[:], ALU.mult, ALU.add)
                elif step == 4:
                    ins = nc.vector.scalar_tensor_tensor(arg[:], turns[:], -TWO_PI_LO, arg[:], ALU.mult, ALU.add)
                else:
                    ins = nc.vector.tensor_scalar(arg[:], arg[:], PI_BELOW, -PI_BELOW, ALU.min, ALU.max)
                ins.then_inc(sn["chain"], 1)
                n += 1

    def sin_act(act):
        for i, dst in enumerate((a1, a2)):
            act.wait_ge(sn["chain"], 6 * (i + 1))
            nc.scalar.activation(dst[:], arg[:], ACT.Sin).then_inc(sn["act"], 1)

    fl_st = [sem("filt_stored0"), sem("filt_stored1")]
    GROUPS = 2 * ORDERS
    tab_done = sem("tk_tables")

    def tables_act(act, name, hi, parts=(0, 1)):
        r0 = ring[name][0]
        for part in parts:
            act.wait_ge(raw_in[(r0 + part) % 2], 32 * ((r0 + part) // 2 + 1))
            nc.scalar.activation(hi[:, part], raw[(r0 + part) % 2][:].rearrange("p (t k) -> p t k", t=LT), ACT.Copy)\
              .then_inc(tab_done, 1)

    def tables_dve(dve, name, hi, lo, before, parts=(0, 1)):
        r0 = ring[name][0]
        for part in parts:
            dve.wait_ge(tab_done, before + part + 1)
            nc.vector.tensor_tensor(lo[:, part], raw[(r0 + part) % 2][:].rearrange("p (t k) -> p t k", t=LT),
                                    hi[:, part].bitcast(F32), ALU.subtract).then_inc(raw_done, 1)

    def filt_mm(pe, n):
        g, t = divmod(n, LT)
        o, dh = divmod(g, 2)
        if n >= 2:
            pe.wait_ge(fl["fbused"], n - 1)
        for d in range(2):
            c0 = (2 * o + d) * D + dh * 512
            ins = nc.tensor.matmul(bank[2 * (n % 2) + d][:], a2[:, t * P:(t + 1) * P], fw3[:, c0:c0 + 512], start=True, stop=True)
        ins.then_inc(fl["fb"], 1)

    def norm_mm(pe, n):
        pe.wait_ge(fl["fa"], n + 1)
        if n >= LT and n % LT == 0:
            pe.wait_ge(fl["nrec"], 2 * (n // LT))
        for b in range(4):
            ins = nc.tensor.matmul(bank[7][:, b:b + 1], asum[:, n % 2, b * P:(b + 1) * P], ones[:, 0:1],
                                   start=(n % LT == 0 and b == 0), stop=(n % LT == LT - 1), skip_group_check=True)
        ins.then_inc(fl["nmm"], 1)

    def norm_row_mm(pe, g):
        pe.wait_ge(fl["nrec"], 2 * g + 2)
        if g:
            pe.wait_ge(fl["nrow"], g)
        for b in range(4):
            ins = nc.tensor.transpose(bank[6][:, b * P:(b + 1) * P], nrm_cols[:, b:b + 1].broadcast_to([P, P]), ident[:])
        ins.then_inc(fl["nbt"], 1)

    def spectra_mm(pe, g, part, k):
        e = 8 * g + 4 * part + k
        if e >= 2:
            pe.wait_ge(fl["ev"], e - 1)
        src = ((sum_h, sum_l), (dif_h, dif_l))[part]
        for t in range(LT):
            if k == 0:
                pe.wait_ge(fl["mlo" if part else "plo"], LT * g + t + 1)
            ks = slice(k * P, (k + 1) * P)
            ins = three_pass(bank[4 + e % 2][:], (tk_h[:, part, t, ks], tk_l[:, part, t, ks]),
                             (src[0][:, t], src[1][:, t]), t == 0, t == LT - 1)
        ins.then_inc(fl["sp"], 1)

    def filter_pe(pe):
        pe.wait_ge(sn["act"], 2)
        pe.wait_ge(fl["in"], 32)
        for n in range(LT):
            filt_mm(pe, n)
        for t in range(LT):
            norm_mm(pe, t)
        prep_pe(pe)
        pe.wait_ge(raw_done, 2)
        pe.wait_ge(prep["cols"], 2)
        for g in range(GROUPS):
            for part in range(2):
                for k in range(LT):
                    spectra_mm(pe, g, part, k)
                    if part == 0 and k == 0:
                        norm_row_mm(pe, g)
                    nxt = {(0, 0): 0, (0, 1): 1, (0, 3): 2, (1, 0): 3}.get((part, k))
                    if nxt is not None and g + 1 < GROUPS:
                        filt_mm(pe, LT * (g + 1) + nxt)
                    for t in {(0, 3): [0], (1, 0): [1], (1, 1): [2], (1, 2): [3]}.get((part, k), []):
                        if g + 1 < GROUPS:
                            norm_mm(pe, LT * (g + 1) + t)

    def filter_dve(dve):
        def fb(n):
            g, t = divmod(n, LT)
            dve.wait_ge(fl["fb"], n + 1)
            if n >= 2:
                dve.wait_ge(fl["pm"], n - 1)
                dve.wait_ge(fl["as_"], n - 1)
            dec = decay[:, t, (g % 2) * 512:(g % 2) * 512 + 512]
            nc.vector.tensor_tensor(fwd[:, n % 2], bank[2 * (n % 2)][:], dec, ALU.mult)
            ins = nc.vector.tensor_tensor(bwd[:, n % 2], bank[2 * (n % 2) + 1][:], dec, ALU.mult)
            if t == 0:
                chained(dve, ins)
                ins = nc.vector.memset(bwd[0:1, n % 2, :], 0.0)
            ins.then_inc(fl["fbused"], 1)

        def asum_(n):
            dve.wait_ge(fl["as_"], n + 1)
            if n >= 2:
                dve.wait_ge(fl["nmm"], n - 1)
            nc.vector.tensor_tensor(asum[:, n % 2], afwd[:], abwd[:], ALU.add).then_inc(fl["fa"], 1)

        def lo(n, part):
            dve.wait_ge(fl["mhi" if part else "phi"], n + 1)
            src, h, l_ = ((sum_f, sum_h, sum_l), (dif_f, dif_h, dif_l))[part]
            nc.vector.tensor_tensor(l_[:, n % LT], src[:, n % LT], h[:, n % LT].bitcast(F32), ALU.subtract)\
              .then_inc(fl["mlo" if part else "plo"], 1)

        def rec(g):
            dve.wait_ge(fl["nmm"], LT * (g + 1))
            nc.vector.reciprocal(nrm_cols[:], bank[7][:, 0:4]).then_inc(fl["nrec"], 1)
            dve.wait_ge(fl["nrec"], 2 * g + 1)
            nc.vector.tensor_scalar(nrm_cols[:], nrm_cols[:], 1.0 / L, None, ALU.mult).then_inc(fl["nrec"], 1)

        def ev(g, part, k):
            e = 8 * g + 4 * part + k
            dve.wait_ge(fl["sp"], e + 1)
            dve.wait_ge(fl["nrow"], g + 1)
            if e >= 2:
                dve.wait_ge(fl_st[e % 2], 16 * (e // 2))
            nc.vector.tensor_tensor(spec_out[:, e % 2], bank[4 + e % 2][:], rn_row[:], ALU.mult).then_inc(fl["ev"], 1)

        dve.wait_ge(fl["in"], 32)
        for n in range(LT):
            fb(n)
            if n:
                asum_(n - 1)
        tables_dve(dve, "tk", tk_h, tk_l, 0)
        asum_(LT - 1)
        for n in range(LT):
            lo(n, 0)
        rec(0)
        prep_dve(dve)
        dve.wait_ge(prep["silu"], 1)
        for g in range(GROUPS):
            m = LT * (g + 1)
            more = g + 1 < GROUPS
            for t in range(LT):
                lo(LT * g + t, 1)
            ev(g, 0, 0)
            if more:
                fb(m)
            ev(g, 0, 1)
            if more:
                fb(m + 1)
                asum_(m)
            ev(g, 0, 2)
            ada_step(dve, 0, 2 * g, 0)
            if more:
                asum_(m + 1)
            ev(g, 0, 3)
            if more:
                fb(m + 2)
            ev(g, 1, 0)
            if more:
                fb(m + 3)
                asum_(m + 2)
            ev(g, 1, 1)
            if more:
                asum_(m + 3)
                for t in range(LT):
                    lo(m + t, 0)
            ev(g, 1, 2)
            if more:
                rec(g + 1)
            ada_step(dve, 0, 2 * g + 1, 0)
            ev(g, 1, 3)

    def filter_act(act):
        def abs_(n):
            act.wait_ge(fl["fbused"], n + 1)
            if n:
                act.wait_ge(fl["fa"], n)
            nc.scalar.activation(afwd[:], fwd[:, n % 2], ACT.Abs)
            nc.scalar.activation(abwd[:], bwd[:, n % 2], ACT.Abs).then_inc(fl["as_"], 1)

        def hi(n, part):
            act.wait_ge(fl["pm"], n + 1)
            if n >= LT:
                act.wait_ge(fl["sp"], 8 * (n // LT - 1) + 4 * (part + 1))
            src, h = ((sum_f, sum_h), (dif_f, dif_h))[part]
            nc.scalar.activation(h[:, n % LT], src[:, n % LT], ACT.Copy).then_inc(fl["mhi" if part else "phi"], 1)

        tables_act(act, "tk", tk_h)
        for n in range(LT):
            abs_(n)
        for n in range(LT):
            hi(n, 0)
        silu_act(act)
        for g in range(GROUPS):
            for t in range(LT):
                hi(LT * g + t, 1)
            act.wait_ge(fl["nbt"], g + 1)
            if g:
                act.wait_ge(fl["ev"], 8 * g)
            nc.scalar.activation(rn_row[:], bank[6][:], ACT.Copy).then_inc(fl["nrow"], 1)
            if g + 1 < GROUPS:
                for t in range(LT):
                    abs_(LT * (g + 1) + t)
                for t in range(LT):
                    hi(LT * (g + 1) + t, 0)

    def filter_pool(pool):
        for n in range(GROUPS * LT):
            t = n % LT
            pool.wait_ge(fl["fbused"], n + 1)
            if n >= LT:
                pool.wait_ge(fl["plo"], n - LT + 1)
                pool.wait_ge(fl["mlo"], n - LT + 1)
            nc.gpsimd.tensor_tensor(sum_f[:, t], fwd[:, n % 2], bwd[:, n % 2], ALU.add)
            nc.gpsimd.tensor_tensor(dif_f[:, t], fwd[:, n % 2], bwd[:, n % 2], ALU.subtract).then_inc(fl["pm"], 1)
            if t == LT - 1 and n >= LT:
                ada_load_one(pool, 0, n // LT * 2, 0)
                ada_load_one(pool, 0, n // LT * 2 + 1, 0)

    def filter_sp(sp):
        for e in range(8 * GROUPS):
            g, part, k = e // 8, e // 4 % 2, e % 4
            o, dh = divmod(g, 2)
            sp.wait_ge(fl["ev"], e + 1)
            if g == GROUPS - 1 and k % 2 == 0:
                xload_sp(sp, 2 * part + k // 2)
            sp.dma_start(spectra[o, 2 * dh:2 * dh + 2, :, k, part, :].rearrange("q p c -> p q c"),
                         spec_out[:, e % 2].rearrange("p (q c) -> p q c", q=2)).then_inc(fl_st[e % 2], 16)

    def xload_sp(sp, t):
        sp.wait_ge(fl["fbused"], GROUPS * LT)
        sp.dma_start(x_rows[:, t], A["x"][0, t * P:(t + 1) * P, :]).then_inc(xs["in"], 16)

    def xload_pe(pe):
        pe.wait_ge(xs["in"], 16 * LT)
        for k in range(KT):
            if k >= 4:
                pe.wait_ge(xs["ev"], k - 3)
            for t in range(LT):
                ins = nc.tensor.transpose(bank[k % 4][:, t * P:(t + 1) * P], x_rows[:, t, k * P:(k + 1) * P], ident[:])
            ins.then_inc(xs["pe"], 1)

    def xload_act(act, norm):
        act.wait_ge(fl["plo"], GROUPS * LT)
        act.wait_ge(fl["mlo"], GROUPS * LT)
        for k in range(KT):
            act.wait_ge(xs["pe"], k + 1)
            nc.scalar.activation(x[:, k], bank[k % 4][:], ACT.Copy).then_inc(xs["ev"], 1)
            norm.square(act, k)
            if k == 3:
                for i in range(2):
                    act.wait_ge(fl_st[i], 16 * 4 * GROUPS)
                split_hi(act, qkv_r, qkv_s, 0, UNIT)

    dn = sems("double", "g w c rt bc x")
    norm_sems = sems("norm", "sq pq ac st rt rc bc t1 hi lo")
    EARLY = KT - 2
    ADDS = EARLY + 1
    norm_count = {"norms": 0, "modulated": 0}

    def keep_warm(n):
        for _ in range(n):
            nc.tensor.matmul(bank[4][:], ident[:], vec[:, 0:512], start=True, stop=True)

    class Norm:
        def __init__(self, ready, scale, shift, mods, nxt=None):
            self.s = norm_sems
            self.late = (ring[nxt][0] + 1, ring[nxt][1] + 1, ring[nxt][2]) if nxt else None
            self.ready, self.scale, self.shift, self.mods = ready, scale, shift, mods
            self.a, self.b, self.m = KT * norm_count["norms"], norm_count["norms"], KT * norm_count["modulated"]
            self.ac0, self.pq0 = ADDS * self.b, EARLY * (self.b - 1)
            self.sq0 = EARLY + 2 * self.b
            norm_count["norms"] += 1
            norm_count["modulated"] += shift is not None
            self.done = (norm_sems["lo"], self.a)

        def square(self, act, t):
            act.wait_ge(self.ready[0], self.ready[1] + t + 1)
            if self.b == 0 and t >= 2:
                act.wait_ge(self.s["ac"], t)
            elif t == KT - 1:
                act.wait_ge(self.s["ac"], self.ac0 + ADDS)
            nc.scalar.activation(nsq[:, t % 2], x[:, t], ACT.Square).then_inc(self.s["sq"], 1)

        def act(self, act):
            act.preload_act_table(ACT.Sqrt)
            for t in range(EARLY, KT):
                self.square(act, t)
            self.factors_act(act)

        def factors_act(self, act):
            s = self.s
            if self.b == 0:
                act.preload_act_table(ACT.Sqrt)
            act.wait_ge(s["st"], self.b + 1)
            nc.scalar.activation(rms_cols[:, 0, 0:LT], bank[7][:, 0:LT], ACT.Sqrt, bias=eps_col[:], scale=1.0 / D)\
              .then_inc(s["rt"], 1)
            self.split_and_shift(act)

        def split_and_shift(self, act):
            s = self.s
            if self.late:
                r, su, n_el = self.late
                split_hi(act, r, su, 0, n_el)
            if self.shift is not None:
                for t in range(KT):
                    act.wait_ge(s["t1"], self.m + t + 1)
                    nc.scalar.activation(hh[:, t], nt1[:, t % 2], ACT.Identity, bias=self.shift(t)).then_inc(s["hi"], 1)

        def add_squares(self, eng):
            s = self.s
            nc.vector.memset(nacc[:], 0.0).then_inc(s["ac"], 1)
            for t in range(EARLY):
                eng.wait_ge(s["sq"], t + 1)
                eng.wait_ge(s["ac"], t + 1)
                nc.vector.tensor_tensor(nacc[:], nacc[:], nsq[:, t % 2], ALU.add).then_inc(s["ac"], 1)

        def pool_zero(self, pool):
            pool.wait_ge(self.s["st"], self.b)
            nc.gpsimd.memset(nacc[:], 0.0).then_inc(self.s["ac"], 1)

        def pool_square(self, pool, c, it):
            s = self.s
            pool.wait_ge(self.ready[0], self.ready[1] + c + 1 + 2 * it)
            pool.wait_ge(s["ac"], self.ac0 + c + 1 + 2 * it)
            xt = tile_of(x, c, it, 2)
            nc.gpsimd.tensor_tensor(nsq[:, 1], xt, xt, ALU.mult).then_inc(s["pq"], 1)
            pool.wait_ge(s["pq"], self.pq0 + c + 1 + 2 * it)
            nc.gpsimd.tensor_tensor(nacc[:], nacc[:], nsq[:, 1], ALU.add).then_inc(s["ac"], 1)

        def pool(self, pool):
            pool.wait_ge(self.ready[0], self.ready[1] + 1)
            self.pool_zero(pool)
            for t in range(EARLY):
                self.pool_square(pool, t, 0)
            self.split_late(pool)

        def split_late(self, pool):
            if self.late:
                r, su, n_el = self.late
                pool.wait_ge(hi_done, su + 1)
                pool.wait_ge(raw_done, r)
                nc.gpsimd.tensor_tensor(wlo[su % 2][:, :n_el], raw[r % 2][:, :n_el], whi[su % 2][:, :n_el].bitcast(F32),
                                        ALU.subtract).then_inc(raw_done, 1)

        def pe(self, pe):
            s = self.s
            pe.wait_ge(s["ac"], self.ac0 + ADDS)
            for t, src in enumerate((nacc, nsq[:, 0], nsq[:, 1])):
                if t:
                    if t == 2:
                        keep_warm(1)
                    pe.wait_ge(s["sq"], self.sq0 + t)
                for b in range(LT):
                    ins = nc.tensor.matmul(bank[7][:, b:b + 1], src[:, b * P:(b + 1) * P], ones[:, 0:1],
                                           start=(t == 0 and b == 0), stop=(t == 2), skip_group_check=True)
            ins.then_inc(s["st"], 1)
            keep_warm(1)
            pe.wait_ge(s["rc"], self.b + 1)
            for b in range(LT):
                ins = nc.tensor.transpose(bank[6][:, b * P:(b + 1) * P], rstd_cols[:, 0, b:b + 1].broadcast_to([P, P]), ident[:])
            ins.then_inc(s["bc"], 1)
            if self.shift is not None:
                keep_warm(2)

        def dve(self, dve):
            s = self.s
            dve.wait_ge(s["rt"], self.b + 1)
            nc.vector.reciprocal(rstd_cols[:, 0, 0:LT], rms_cols[:, 0, 0:LT]).then_inc(s["rc"], 1)
            if self.mods is not None:
                dve.wait_ge(ada_ev, self.mods)
            dve.wait_ge(s["bc"], self.b + 1)
            self.modulate(dve)

        def modulate(self, dve):
            s = self.s
            dve.wait_ge(self.ready[0], self.ready[1] + KT)
            for t in range(KT + 1):
                if self.shift is None:
                    if t < KT:
                        nc.vector.scalar_tensor_tensor(x[:, t], x[:, t], self.scale(t), bank[6][:], ALU.mult, ALU.mult)\
                          .then_inc(s["lo"], 1)
                    continue
                if t < KT:
                    if t >= 2:
                        dve.wait_ge(s["lo"], self.a + t - 1)
                    nc.vector.scalar_tensor_tensor(nt1[:, t % 2], x[:, t], self.scale(t), bank[6][:], ALU.mult, ALU.mult)\
                      .then_inc(s["t1"], 1)
                if t >= 1:
                    dve.wait_ge(s["hi"], self.m + t)
                    nc.vector.scalar_tensor_tensor(hl[:, t - 1], nt1[:, (t - 1) % 2], self.shift(t - 1),
                                                   hh[:, t - 1].bitcast(F32), ALU.add, ALU.subtract).then_inc(s["lo"], 1)
            if self.late:
                dve.wait_ge(raw_done, self.late[0] + 1)

    class DoubleNorm(Norm):
        def gain2(self, dve):
            g = vec[:, COL["final_g"]:COL["final_g"] + KT]
            nc.vector.tensor_tensor(fg2[:, :, 1], g, g, ALU.mult)
            nc.vector.memset(fg2[:, :, 0], 1.0).then_inc(dn["g"], 1)

        def square(self, act, t):
            if t == KT - 1:
                act.wait_ge(dn["w"], 2 * EARLY + 1)
            super().square(act, t)

        def pool_square(self, pool, c, it):
            pool.wait_ge(dn["w"], 2 * c + 1)
            super().pool_square(pool, c, it)
            pool.wait_ge(self.s["ac"], self.ac0 + c + 2)
            nc.gpsimd.tensor_scalar(nsq[:, 1], nsq[:, 1], fg2[:, c, 1:2], None, ALU.mult).then_inc(dn["w"], 1)
            pool.wait_ge(dn["w"], 2 * c + 2)
            nc.gpsimd.tensor_tensor(wacc[:], wacc[:], nsq[:, 1], ALU.add).then_inc(dn["w"], 1)

        def factors_act(self, act):
            s = self.s
            act.wait_ge(s["st"], self.b + 1)
            nc.scalar.activation(rms_cols[:, 0, 0:LT], bank[7][:, 0:2 * LT:2], ACT.Sqrt, bias=eps_col[:], scale=1.0 / D)\
              .then_inc(s["rt"], 1)
            act.wait_ge(dn["c"], 3)
            nc.scalar.activation(rms_cols[:, 1, 0:LT], rstd_cols[:, 1, 0:LT], ACT.Sqrt, bias=eps_col[:], scale=1.0 / D)\
              .then_inc(dn["rt"], 1)
            self.split_and_shift(act)

        def pe(self, pe):
            s = self.s
            pe.wait_ge(s["ac"], self.ac0 + ADDS)
            pe.wait_ge(dn["w"], 2 * EARLY + 1)
            for b in range(LT):
                for i, src in enumerate((nacc, wacc)):
                    nc.tensor.matmul(bank[7][:, 2 * b + i:2 * b + i + 1], src[:, b * P:(b + 1) * P], ones[:, 0:1],
                                     start=(b == 0 and i == 0), stop=False, skip_group_check=True)
            for t in range(2):
                if t == 1:
                    keep_warm(1)
                pe.wait_ge(s["sq"], self.sq0 + t + 1)
                for b in range(LT):
                    ins = nc.tensor.matmul(bank[7][:, 2 * b:2 * b + 2], nsq[:, t, b * P:(b + 1) * P], fg2[:, EARLY + t, :],
                                           start=False, stop=t == 1, skip_group_check=True)
            ins.then_inc(s["st"], 1)
            keep_warm(3)
            pe.wait_ge(s["rc"], self.b + 1)
            for b in range(LT):
                ins = nc.tensor.transpose(bank[6][:, b * P:(b + 1) * P], rstd_cols[:, 0, LT + b:LT + b + 1].broadcast_to([P, P]), ident[:])
            ins.then_inc(s["bc"], 1)
            for b in range(LT):
                ins = nc.tensor.transpose(bank[5][:, b * P:(b + 1) * P], rstd_cols[:, 0, b:b + 1].broadcast_to([P, P]), ident[:])
            ins.then_inc(dn["bc"], 1)
            keep_warm(1)

        def dve(self, dve):
            s = self.s
            n = [0]

            def link(ins):
                n[0] += 1
                ins.then_inc(dn["c"], 1)
                dve.wait_ge(dn["c"], n[0])

            r1, m2 = rstd_cols[:, 0, 0:LT], rstd_cols[:, 1, 0:LT]
            dve.wait_ge(s["rt"], self.b + 1)
            link(nc.vector.reciprocal(r1, rms_cols[:, 0, 0:LT]))
            link(nc.vector.tensor_tensor(m2, bank[7][:, 1:2 * LT:2], r1, ALU.mult))
            link(nc.vector.tensor_tensor(m2, m2, r1, ALU.mult))
            dve.wait_ge(dn["rt"], 1)
            link(nc.vector.reciprocal(rstd_cols[:, 1, LT:2 * LT], rms_cols[:, 1, 0:LT]))
            nc.vector.tensor_tensor(rstd_cols[:, 0, LT:2 * LT], rstd_cols[:, 1, LT:2 * LT], r1, ALU.mult).then_inc(s["rc"], 1)
            dve.wait_ge(ada_ev, self.mods)
            link(nc.vector.tensor_tensor(fgs[:], vec[:, COL["final_g"]:COL["final_g"] + KT], gsc[:, 2, 0, :], ALU.mult))
            dve.wait_ge(s["bc"], self.b + 1)
            self.modulate(dve)

        def residual(self, dve):
            dve.wait_ge(dn["bc"], 1)
            for t in range(KT):
                nc.vector.scalar_tensor_tensor(x[:, t], x[:, t], col("final_g", t), bank[5][:], ALU.mult, ALU.mult)\
                  .then_inc(dn["x"], 1)

    def mod_norm(ready, b, h, nxt=None):
        return Norm(ready, lambda t: gsc[:, b, h, t:t + 1],
                    lambda t: mod[:, b, h * 3 * KT + t:h * 3 * KT + t + 1], 2 * (2 * b + h) + 2, nxt)

    def gate(b, h, i, it, step):
        c0 = h * 3 * KT + 2 * KT + i
        if isinstance(it, int):
            return mod[:, b, c0 + step * it:c0 + step * it + 1]
        return mod[:, b, bass.ds(c0 + step * it, 1)]

    rp_in, qk = sem("rope_in"), sems("qk", "h0 qf st sw t rt rc rx bc done vd rot")
    NQK = 2 * 5
    qkv_r, qkv_s = ring["qkv"][0], ring["qkv"][1]

    def qkv_sp(sp):
        for i in range(6):
            load(sp, qkv_r + i, 0, cols2(A["attn_w_qkv"][0], 2 * P * i, 0, 0))
            if i == 0:
                sp.dma_start(rope[:], C["rope"].rearrange("s p l -> p s l")).then_inc(rp_in, 16)

    def project(s, h, dst):
        w = slot_w(s)
        for k in range(KT):
            ks = slice(h * P, (h + 1) * P)
            ins = three_pass(dst, (w[0][:, k, ks], w[1][:, k, ks]), (hh[:, k], hl[:, k]), k == 0, k == KT - 1)
        return ins

    def project_pair(pe, s, dsts, ready):
        w = slot_w(s)
        for k in range(KT):
            pe.wait_ge(ready[0], ready[1] + k + 1)
            for h in range(2):
                ks = slice(h * P, (h + 1) * P)
                ins = three_pass(dsts[h], (w[0][:, k, ks], w[1][:, k, ks]), (hh[:, k], hl[:, k]), k == 0, k == KT - 1)
                if h == 0:
                    first = ins
        return first, ins

    def project_rows(s, c0, n, dst, between=None):
        w = slot_w(s)
        for t in range(LT):
            for k in range(KT):
                ts = slice(t * P, (t + 1) * P)
                ins = three_pass(dst(t), (hh[:, k, ts], hl[:, k, ts]), (w[0][:, k, c0:c0 + n], w[1][:, k, c0:c0 + n]),
                                 k == 0, k == KT - 1)
            if between and t < LT - 1:
                between(t)
        return ins

    def qkv_pe(pe, norm):
        def stat(T):
            pe.wait_ge(qk["qf"], T + 1)
            if T >= 1:
                pe.wait_ge(qk["rt"], T)
            for b in range(LT):
                ins = nc.tensor.matmul(bank[7][:, 2 * b:2 * b + 2], qsq[:, T % 2, b * P:(b + 1) * P], head_mean[:],
                                       start=True, stop=True)
            ins.then_inc(qk["st"], 1)
            if T >= 2:
                pe.wait_ge(qk["t"], T - 1)
            nc.tensor.matmul(bank[4 + T % 2][:], swap_m[:], qf[:, T % 2], start=True, stop=True).then_inc(qk["sw"], 1)

        def factors(T):
            pe.wait_ge(qk["rx"], T + 1)
            if T >= 1:
                pe.wait_ge(qk["done"], T)
            for b in range(LT):
                ins = nc.tensor.transpose(bank[6][:, b * P:(b + 1) * P], rx[:, T % 2, b * P:(b + 1) * P], ident[:])
            ins.then_inc(qk["bc"], 1)

        for i in range(6):
            pe.wait_ge(raw_done, qkv_r + i + 1)
            if i < 5:
                for h in range(2):
                    T = 2 * i + h
                    if T >= 4:
                        pe.wait_ge(qk["qf"], T - 3)
                    if T == 0:
                        first, second = project_pair(pe, qkv_s, (bank[0][:], bank[1][:]), norm.done)
                        first.then_inc(qk["h0"], 1)
                        second.then_inc(used, 1)
                    elif T > 1:
                        project(qkv_s + i, h, bank[T % 4][:]).then_inc(used if h else qk["h0"], 1)
                    if T >= 2:
                        stat(T - 2)
                    if T >= 3:
                        factors(T - 3)
            else:
                pe.wait_ge(qk["qf"], 8)
                def between(t):
                    if t < 2:
                        stat(8 + t)
                    factors(7 + t)
                project_rows(qkv_s + i, 0, KV_HEADS * HD,
                             lambda t: bank[2 + t // 2][:, (t % 2) * 256:(t % 2) * 256 + 256], between).then_inc(used, 1)

    def qkv_pool(pool):
        for T in range(NQK):
            pool.wait_ge(qk["rc"], T + 1)
            if T >= 2:
                pool.wait_ge(qk["bc"], T - 1)
            nc.gpsimd.tensor_copy(rx[:, T % 2].rearrange("p (a c) -> p a c", c=HD),
                                  rstd_cols[:, T % 2, :].unsqueeze(2).broadcast_to([P, 2 * LT, HD])).then_inc(qk["rx"], 1)

    def head_dst(T, h):
        return qh[:, 2 * T + h] if T < 8 else kh[:, 2 * (T - 8) + h]

    def qkv_act(act, splits):
        def tile_in(T):
            if T % 2:
                act.wait_ge(used, qkv_s + T // 2 + 1)
            else:
                act.wait_ge(qk["h0"], T // 2 + 1)
            if T >= 2:
                act.wait_ge(qk["st"], T - 1)
                act.wait_ge(qk["rot"], T - 1)
            nc.scalar.activation(qsq[:, T % 2], bank[T % 4][:], ACT.Square)
            g = 0 if T < 8 else 1
            nc.scalar.activation(qf[:, T % 2], bank[T % 4][:], ACT.Copy, scale=gain_cols[:, g:g + 1]).then_inc(qk["qf"], 1)

        def root(T):
            act.wait_ge(qk["st"], T + 1)
            if T >= 2:
                act.wait_ge(qk["rc"], T - 1)
            nc.scalar.activation(rms_cols[:, T % 2, :], bank[7][:, 0:8], ACT.Sqrt, bias=eps_col[:]).then_inc(qk["rt"], 1)

        for T in range(NQK):
            if T % 2 == 0:
                splits(T // 2)
            tile_in(T)
            if T >= 1:
                root(T - 1)
        root(NQK - 1)
        act.wait_ge(used, qkv_s + 6)
        nc.scalar.activation(vh[:, 0:2].rearrange("p t n -> p (t n)"), bank[2][:], ACT.Copy)
        nc.scalar.activation(vh[:, 2:4].rearrange("p t n -> p (t n)"), bank[3][:], ACT.Copy).then_inc(qk["vd"], 1)

    def qkv_dve(dve, splits):
        dve.wait_ge(rp_in, 16)
        def link(ins):
            chained(dve, ins)

        def rotate(T):
            dve.wait_ge(qk["sw"], T + 1)
            if T >= 2:
                dve.wait_ge(qk["done"], T - 1)
            nc.vector.tensor_tensor(qt[:, T % 2], bank[4 + T % 2][:], rope[:, 1], ALU.mult).then_inc(qk["t"], 1)
            link(nc.vector.tensor_tensor(qf[:, T % 2], qf[:, T % 2], rope[:, 0], ALU.mult))
            dve.wait_ge(qk["t"], T + 1)
            nc.vector.tensor_tensor(qt[:, T % 2], qt[:, T % 2], qf[:, T % 2], ALU.add).then_inc(qk["rot"], 1)

        def rec(T):
            dve.wait_ge(qk["rt"], T + 1)
            if T >= 2:
                dve.wait_ge(qk["rx"], T - 1)
            nc.vector.reciprocal(rstd_cols[:, T % 2, :], rms_cols[:, T % 2, :]).then_inc(qk["rc"], 1)

        def scale(T):
            dve.wait_ge(qk["bc"], T + 1)
            dve.wait_ge(qk["rot"], T + 1)
            nc.vector.tensor_tensor(head_dst(T, 0), qt[0:HD, T % 2], bank[6][0:HD, :], ALU.mult)
            nc.vector.tensor_tensor(head_dst(T, 1), qt[HD:P, T % 2], bank[6][HD:P, :], ALU.mult).then_inc(qk["done"], 1)

        for T in range(NQK):
            if T % 2 == 0:
                splits(T // 2)
            rec(T)
            rotate(T)
            if T >= 1:
                scale(T - 1)
        scale(NQK - 1)

    attend_sems = sems("attend", "sc nm ex pr tr pt o oh ol")
    attend_heads = [0]

    class Attend:
        def __init__(self, name, heads, q, k, v, first, kind, tile0, probs, probsT):
            self.s = attend_sems
            self.heads, self.q, self.k, self.v, self.first, self.kind = heads, q, k, v, first, kind
            self.tile0, self.probs, self.probsT = tile0, probs, probsT
            self.steps = [(h, t) for h in range(heads) for t in range(LT)]
            self.i0, self.h0, self.j0 = LT * attend_heads[0], attend_heads[0], attend_heads[0] // 2
            attend_heads[0] += heads

        def last(self, t):
            return LT - 1 if self.kind == "plain" else t

        def width(self, t):
            return (self.last(t) - self.first(t) + 1) * P

        def pe(self, pe, start_waits):
            s, steps = self.s, self.steps
            for sm, v in start_waits:
                pe.wait_ge(sm, v)

            def scores(i):
                h, t = steps[i]
                if i >= 3:
                    pe.wait_ge(s["ex"], self.i0 + i - 2)
                nc.tensor.matmul(bank[i % 3][:, 0:self.width(t)], self.q(h, t), self.k(h, t), start=True, stop=True)\
                  .then_inc(s["sc"], 1)

            def turn(i):
                h, t = steps[i]
                pe.wait_ge(s["pr"], self.i0 + i + 1)
                if i >= 2:
                    pe.wait_ge(s["pt"], self.i0 + i - 1)
                for b in range(self.width(t) // P):
                    ins = nc.tensor.transpose(bank[3 + i % 2][:, b * P:(b + 1) * P], self.probs[:, i % 2, b * P:(b + 1) * P], ident[:])
                ins.then_inc(s["tr"], 1)

            def values(h):
                pe.wait_ge(s["pt"], self.i0 + LT * (h + 1))
                if h >= 2 and h % 2 == 0:
                    pe.wait_ge(s["ol"], self.j0 + h // 2)
                o = bank[5][HD * (h % 2):HD * (h % 2) + HD, :]
                pT = self.probsT[:, h % 2]
                if self.kind == "alibi":
                    for t in range(LT):
                        for k in range(self.first(t), t + 1):
                            ins = nc.tensor.matmul(o[:, t * P:(t + 1) * P], self.v(h, k), pT[:, k - self.first(t), t * P:(t + 1) * P],
                                                   start=k == self.first(t), stop=k == t)
                else:
                    for k in range(LT):
                        c0 = k * P if self.kind == "causal" else 0
                        ins = nc.tensor.matmul(o[:, c0:L], self.v(h, k), pT[:, k, c0:L], start=k == 0, stop=k == LT - 1,
                                               skip_group_check=self.kind == "causal")
                ins.then_inc(s["o"], 1)

            scores(0)
            scores(1)
            for i in range(len(steps)):
                if i + 2 < len(steps):
                    scores(i + 2)
                turn(i)
                if i % LT == 1 and i > LT:
                    values(i // LT - 1)
            values(self.heads - 1)

        def act(self, act, extra=None):
            s, steps = self.s, self.steps

            def move(i):
                h, t = steps[i]
                act.wait_ge(s["tr"], self.i0 + i + 1)
                if h >= 2:
                    act.wait_ge(s["o"], self.h0 + h - 1)
                n = self.width(t) // P
                nc.scalar.activation(self.probsT[:, h % 2, 0:n, t * P:(t + 1) * P],
                                     bank[3 + i % 2][:, 0:n * P].rearrange("p (k q) -> p k q", k=n), ACT.Copy).then_inc(s["pt"], 1)

            def heads_out(j):
                act.wait_ge(s["o"], self.h0 + 2 * j + 2)
                nc.scalar.activation(hh[:, self.tile0 + j], bank[5][:], ACT.Copy).then_inc(s["oh"], 1)

            for i, (h, t) in enumerate(steps):
                act.wait_ge(s["nm"], self.i0 + i + 1)
                if i >= 2:
                    act.wait_ge(s["tr"], self.i0 + i - 1)
                w = self.width(t)
                if self.kind == "alibi":
                    nc.scalar.activation(es[:, i % 4:i % 4 + 1], sink_b[:, h:h + 1], ACT.Exp, bias=nmx[:, i % 4:i % 4 + 1])
                    src, sc = biased[:, i % 2, 0:w], 1.0
                else:
                    src, sc = bank[i % 3][:, 0:w], SCALE
                nc.scalar.activation(self.probs[:, i % 2, 0:w], src, ACT.Exp, bias=nmx[:, i % 4:i % 4 + 1], scale=sc,
                                     accum_out=sums[:, i % 4:i % 4 + 1]).then_inc(s["ex"], 1)
                if i >= 1:
                    move(i - 1)
                if i % LT == 2 and i // LT >= 2 and i // LT % 2 == 0:
                    heads_out(i // LT // 2 - 1)
                if extra is not None:
                    extra(i)
            move(len(steps) - 1)
            heads_out(self.heads // 2 - 1)

        def dve(self, dve, extra=None):
            s, steps = self.s, self.steps

            def heads_out(j):
                dve.wait_ge(s["oh"], self.j0 + j + 1)
                nc.vector.tensor_tensor(hl[:, self.tile0 + j], bank[5][:], hh[:, self.tile0 + j].bitcast(F32), ALU.subtract)\
                  .then_inc(s["ol"], 1)

            def bias(i):
                h, t = steps[i]
                w = self.width(t)
                dve.wait_ge(s["sc"], self.i0 + i + 1)
                src = bank[i % 3][:, 0:w]
                if self.kind == "causal":
                    return src, counted(nc.vector.tensor_tensor(src[:, w - P:w], src[:, w - P:w], causal[:], ALU.add))
                if self.kind == "alibi":
                    if i >= 2:
                        dve.wait_ge(s["ex"], self.i0 + i - 1)
                    src = biased[:, i % 2, 0:w]
                    return src, counted(nc.vector.scalar_tensor_tensor(
                        src, bank[i % 3][:, 0:w], SCALE, alibi[:, h, 2 * P - w:2 * P], ALU.mult, ALU.add))
                return src, None

            def maximum(i, src, ready):
                c = slice(i % 4, i % 4 + 1)
                if ready:
                    dve.wait_ge(own_step, ready)
                return counted(nc.vector.reduce_max(mxs[:, c], src, axis=AX.X))

            def negated(i, ready):
                h, t = steps[i]
                c = slice(i % 4, i % 4 + 1)
                dve.wait_ge(own_step, ready)
                if i >= 4:
                    dve.wait_ge(s["ex"], self.i0 + i - 3)
                if self.kind == "alibi":
                    ins = nc.vector.tensor_scalar(nmx[:, c], mxs[:, c], sink_b[:, h:h + 1], -1.0, ALU.max, ALU.mult)
                else:
                    ins = nc.vector.tensor_scalar(nmx[:, c], mxs[:, c], -SCALE, None, ALU.mult)
                ins.then_inc(s["nm"], 1)

            def inverse_sum(i, ready):
                c = slice(i % 4, i % 4 + 1)
                if ready:
                    dve.wait_ge(own_step, ready)
                return counted(nc.vector.reciprocal(recs[:, c], sums[:, c]))

            def normalise(i, ready):
                h, t = steps[i]
                w, c = self.width(t), slice(i % 4, i % 4 + 1)
                dve.wait_ge(own_step, ready)
                nc.vector.tensor_scalar(self.probs[:, i % 2, 0:w], self.probs[:, i % 2, 0:w], recs[:, c], None, ALU.mult)\
                  .then_inc(s["pr"], 1)

            src, b = bias(0)
            negated(0, maximum(0, src, b))
            for i in range(len(steps)):
                c = slice(i % 4, i % 4 + 1)
                more = i + 1 < len(steps)
                if more:
                    src, b = bias(i + 1)
                if more and self.kind == "plain":
                    negated(i + 1, maximum(i + 1, src, b))
                dve.wait_ge(s["ex"], self.i0 + i + 1)
                if self.kind == "alibi":
                    total = counted(nc.vector.tensor_tensor(sums[:, c], sums[:, c], es[:, c], ALU.add))
                else:
                    inv = inverse_sum(i, None)
                if more and self.kind != "plain":
                    m = maximum(i + 1, src, b)
                if self.kind == "alibi":
                    inv = inverse_sum(i, total)
                if more and self.kind != "plain":
                    negated(i + 1, m)
                normalise(i, inv)
                if i % LT == 3 and i // LT >= 2 and i // LT % 2 == 0:
                    heads_out(i // LT // 2 - 1)
                if extra is not None:
                    extra(i)
            heads_out(self.heads // 2 - 1)

    G = HEADS // KV_HEADS
    attn1 = Attend("attn", HEADS, lambda h, t: qh[:, h, t * P:(t + 1) * P], lambda h, t: kh[:, h // G, :],
                   lambda h, k: vh[:, k, (h // G) * HD:(h // G + 1) * HD], lambda t: 0, "plain", 0, probs1, probsT1)
    GA = SWA_HEADS // SWA_KV
    swa = Attend("swa", SWA_HEADS, lambda h, t: qa[:, h, t * P:(t + 1) * P],
                 lambda h, t: ka[:, h // GA, max(t - 1, 0) * P:(t + 1) * P],
                 lambda h, k: va[:, k, (h // GA) * HD:(h // GA + 1) * HD], lambda t: max(t - 1, 0), "alibi", 0, probs2, probsT2)
    fox = Attend("fox", FOX_HEADS, lambda h, t: qfx[:, h, t * P:(t + 1) * P], lambda h, t: kfx[:, h, 0:(t + 1) * P],
                 lambda h, k: vfx[:, k, h * HD:(h + 1) * HD], lambda t: 0, "causal", SWA_HEADS // 2, probs2, probsT2)

    back_sems = sems("back", "t0 x")
    backs = [0]

    class Back:
        def __init__(self, key, w, b, src, ready):
            self.s, self.t, self.x0 = back_sems, 4 * backs[0], KT * backs[0]
            backs[0] += 1
            self.r0, self.s0 = ring[key][0:2]
            self.w, self.b, self.src, self.ready = w, b, src, ready

        def sp(self, sp):
            for i in range(4):
                load(sp, self.r0 + i, 0, cols2(self.w, 2 * P * i, 0, 0))

        def pe(self, pe):
            for i in range(4):
                pe.wait_ge(raw_done, self.r0 + i + 1)
                w = slot_w(self.s0 + i)
                for h in range(2):
                    if i >= 2:
                        pe.wait_ge(self.s["x"], self.x0 + 2 * i + h - 3)
                    for k in range(KT):
                        if i == 0 and h == 0:
                            for sm, v in self.ready(k):
                                pe.wait_ge(sm, v)
                        ks = slice(h * P, (h + 1) * P)
                        ins = three_pass(bank[(2 * i + h) % 4][:], (w[0][:, k, ks], w[1][:, k, ks]),
                                         (self.src[0][:, k], self.src[1][:, k]), k == 0, k == KT - 1)
                    ins.then_inc(used if h else self.s["t0"], 1)

        def dve(self, dve, split):
            for i in range(4):
                for h in range(2):
                    m = 2 * i + h
                    dve.wait_ge(self.s["t0"], self.t + i + 1)
                    if h:
                        dve.wait_ge(used, self.s0 + i + 1)
                        split(i)
                    nc.vector.scalar_tensor_tensor(x[:, m], bank[m % 4][:], gate(self.b, 0, m, 0, 0), x[:, m],
                                                   ALU.mult, ALU.add).then_inc(self.s["x"], 1)

        def act(self, act, split):
            for i in range(4):
                split(i)

    class Ffn:
        def __init__(self, b, w_up, w_down, norm, conv_w, conv_b, gate_off, both, nxt, T):
            self.s = sems(f"ffn{b}", "t0 a1 cv cg sl hd hi hl dn xd")
            self.b, self.w_up, self.w_down, self.norm = b, w_up, w_down, norm
            self.conv_w, self.conv_b, self.gate_off, self.both = conv_w, conv_b, gate_off, both
            self.nxt, self.T = nxt, T
            self.up = [ring[f"up{b}_{h}"] for h in (0, 1)]
            self.dn = [ring[f"dn{b}_{h}"] for h in (0, 1)]
            self.val_off = FF - gate_off

        def sp(self, sp):
            for half in (0, 1):
                def up(c, it, half=half):
                    c0 = (FH * half + c) * P
                    load(sp, self.up[half][0] + c, it, cols2(self.w_up, self.gate_off + c0, 2 * P, it, self.val_off + c0))
                over(sp, FH, up)

                def down(c, it, half=half):
                    load(sp, self.dn[half][0] + c, it, down_parts(self.w_down, half, c, it))
                over(sp, KT, down)

        def pe(self, pe):
            s = self.s
            for half in (0, 1):
                r0, s0 = self.up[half][0:2]

                def up(c, it, half=half, r0=r0, s0=s0, gated=False):
                    U = FH * half + c
                    pe.wait_ge(raw_done, r0 + c + 1 + 2 * it)
                    if U >= 2:
                        pe.wait_ge(s["hd"], U - 1 + 2 * it)
                    banks = (bank[2 * (U % 2)][:], bank[2 * (U % 2) + 1][:])
                    if gated:
                        first, second = project_pair(pe, s0 + c, banks, self.norm.done)
                        first.then_inc(s["t0"], 1)
                        second.then_inc(used, 1)
                    else:
                        project(s0 + c, 0, banks[0]).then_inc(s["t0"], 1)
                        project(s0 + c, 1, banks[1]).then_inc(used, 1)
                if half == 0:
                    up(0, 0, gated=True)
                    up(1, 0)
                    over(pe, FH - 2, lambda c, it: up(c + 2, it))
                else:
                    up(0, 0)
                    if self.T is not None:
                        ada_sum(pe, self.T)
                    up(1, 0)
                    over(pe, FH - 2, lambda c, it: up(c + 2, it))
                    if self.T is not None:
                        ada_turn(pe, self.T)
                r0, s0 = self.dn[half][0:2]

                def down(c, it, half=half, r0=r0, s0=s0):
                    V = KT * half + c
                    pe.wait_ge(raw_done, r0 + c + 1 + 2 * it)
                    if V >= 2:
                        pe.wait_ge(s["xd"], V - 1 + 2 * it)
                    w = slot_d(s0 + c)
                    for k in range(FH):
                        if isinstance(it, int) and c == 0:
                            pe.wait_ge(s["hl"], FH * half + k + 1)
                        ins = three_pass(bank[4 + V % 2][:], (w[0][:, k], w[1][:, k]), (hid_h[:, k], hid_l[:, k]),
                                         k == 0, k == FH - 1)
                    ins.then_inc(used, 1)
                down(0, 0)
                down(1, 0)
                over(pe, KT - 2, lambda c, it: down(c + 2, it))

        def act(self, act):
            s = self.s
            for half in (0, 1):
                r0, s0, n_el, n = self.up[half]

                def up(c, it, half=half, s0=s0):
                    U = FH * half + c
                    p = U % 2
                    act.wait_ge(s["t0"], U + 1 + 2 * it)
                    g = self.cols(half, c, it, "g")
                    mid = g[2] if self.both else g[1]
                    nc.scalar.activation(fc[:, p], bank[2 * p][:], ACT.Identity, bias=g[3], scale=mid).then_inc(s["a1"], 1)
                    act.wait_ge(used, s0 + c + 1 + 2 * it)
                    if self.both:
                        v = self.cols(half, c, it, "v")
                        nc.scalar.activation(fv[:, p], bank[2 * p + 1][:], ACT.Identity, bias=v[3], scale=v[2]).then_inc(s["a1"], 1)
                    act.wait_ge(s["cg"], U + 1 + 2 * it)
                    nc.scalar.activation(fs[:, p], fc[:, p], ACT.Silu).then_inc(s["sl"], 1)
                    act.wait_ge(s["hd"], U + 1 + 2 * it)
                    nc.scalar.activation(tile_of(hid_h, c, it, 2), fh[:, p], ACT.Copy).then_inc(s["hi"], 1)
                act.preload_act_table(ACT.Silu)
                split_ahead(act, split_hi, n, r0, s0, n_el, self.dn[half][0:3], up)
                nxt = self.up[1][0:3] if half == 0 else self.nxt
                r0, s0, n_el, n = self.dn[half]
                split_ahead(act, split_hi, n, r0, s0, n_el, nxt, lambda c, it: None, 2 - half)

        def cols(self, half, c, it, which):
            n = 2 * FT if self.both else FT
            w0 = 0 if self.both else self.b * 3 * FT
            b0 = 0 if self.both else self.b * FT
            off = FH * half + c + ((self.gate_off if which == "g" else self.val_off) // P if self.both else 0)
            return [dcol(self.conv_w, w0 + tap * n + off, it, 2) for tap in range(3)] + [dcol(self.conv_b, b0 + off, it, 2)]

        def dve(self, dve):
            s = self.s
            for half in (0, 1):
                r0, s0, n_el, n = self.up[half]

                def up(c, it, half=half):
                    U = FH * half + c
                    p = U % 2
                    g = self.cols(half, c, it, "g")
                    if not self.both:
                        dve.wait_ge(s["a1"], U + 1 + 2 * it)
                        nc.vector.scalar_tensor_tensor(fc[:, p, 1:L], bank[2 * p][:, 0:L - 1], g[0], fc[:, p, 1:L],
                                                       ALU.mult, ALU.add).then_inc(s["cv"], 1)
                        dve.wait_ge(s["cv"], U + 1 + 2 * it)
                        nc.vector.scalar_tensor_tensor(fc[:, p, 0:L - 1], bank[2 * p][:, 1:L], g[2], fc[:, p, 0:L - 1],
                                                       ALU.mult, ALU.add).then_inc(s["cg"], 1)
                        val = bank[2 * p + 1][:]
                    else:
                        v = self.cols(half, c, it, "v")
                        dve.wait_ge(s["a1"], 2 * U + 1 + 4 * it)
                        nc.vector.scalar_tensor_tensor(fc[:, p, 1:L], bank[2 * p][:, 0:L - 1], g[1], fc[:, p, 1:L],
                                                       ALU.mult, ALU.add).then_inc(s["cv"], 1)
                        dve.wait_ge(s["cv"], 3 * U + 1 + 6 * it)
                        nc.vector.scalar_tensor_tensor(fc[:, p, 2:L], bank[2 * p][:, 0:L - 2], g[0], fc[:, p, 2:L],
                                                       ALU.mult, ALU.add).then_inc(s["cg"], 1)
                        dve.wait_ge(s["a1"], 2 * U + 2 + 4 * it)
                        nc.vector.scalar_tensor_tensor(fv[:, p, 1:L], bank[2 * p + 1][:, 0:L - 1], v[1], fv[:, p, 1:L],
                                                       ALU.mult, ALU.add).then_inc(s["cv"], 1)
                        dve.wait_ge(s["cv"], 3 * U + 2 + 6 * it)
                        nc.vector.scalar_tensor_tensor(fv[:, p, 2:L], bank[2 * p + 1][:, 0:L - 2], v[0], fv[:, p, 2:L],
                                                       ALU.mult, ALU.add).then_inc(s["cv"], 1)
                        dve.wait_ge(s["cv"], 3 * U + 3 + 6 * it)
                        val = fv[:, p]
                    dve.wait_ge(s["sl"], U + 1 + 2 * it)
                    nc.vector.tensor_tensor(fh[:, p], fs[:, p], val, ALU.mult).then_inc(s["hd"], 1)
                    dve.wait_ge(s["hi"], U + 1 + 2 * it)
                    nc.vector.tensor_tensor(tile_of(hid_l, c, it, 2), fh[:, p], tile_of(hid_h, c, it, 2).bitcast(F32),
                                            ALU.subtract).then_inc(s["hl"], 1)
                if self.T is not None and half:
                    ada_evict(dve, self.T)
                split_ahead(dve, split_lo, n, r0, s0, n_el, self.dn[half][0:3], up)
                nxt = self.up[1][0:3] if half == 0 else self.nxt
                r0, s0, n_el, n = self.dn[half]
                if self.T is not None:
                    if half:
                        ada_mods(dve, self.T)

                def down(c, it, half=half, s0=s0):
                    V = KT * half + c
                    dve.wait_ge(used, s0 + c + 1 + 2 * it)
                    xt = tile_of(x, c, it, 2)
                    nc.vector.scalar_tensor_tensor(xt, bank[4 + V % 2][:], gate(self.b, 1, c, it, 2), xt,
                                                   ALU.mult, ALU.add).then_inc(s["xd"], 1)
                    if self.T is not None and not (half and c == KT - 1):
                        ada_step(dve, self.T + half, c, it)
                split_ahead(dve, split_lo, n, r0, s0, n_el, nxt, down, 2 - half)

    hs = sems("hyena", "t0 m d1 d2 zh zl f px yf yh yl iv ze zu zh2 zl2 tr")
    in_r, in_s, in_n, IN_UNITS = ring["hyin"]
    spec_r = ring["spec"][0]
    out_r, out_s, out_n, _ = ring["hyout"]
    CHUNKS = ORDERS * NCH

    def hyena_sp(sp):
        over(sp, IN_UNITS, lambda c, it: load(sp, in_r + c, it, cols2(A["hy_w_in"][0], 2 * P * c, 4 * P, it)))
        for part in range(2):
            load(sp, ring["td"][0] + part, 0, table_parts("dft_signal", part))
        for i in range(2):
            sp.wait_ge(fl_st[i], 16 * 4 * GROUPS)
        for g in range(CHUNKS):
            src = spectra[g // NCH, g % NCH].rearrange("p k s c -> p (k s c)")
            load(sp, spec_r + g, 0, lambda slot: [(slot[:, a:a + UNIT // 2], src[:, a:a + UNIT // 2]) for a in (0, UNIT // 2)])

    def hyena_in_pe(pe, norm):
        def unit(c, it, gated=False):
            pe.wait_ge(raw_done, in_r + c + 1 + 2 * it)
            if c >= 2:
                pe.wait_ge(hs["d2"], 2 * (c - 1) + 4 * it)
            banks = (bank[2 * (c % 2)][:], bank[2 * (c % 2) + 1][:])
            if gated:
                first, second = project_pair(pe, in_s + c, banks, norm.done)
                first.then_inc(hs["t0"], 1)
                second.then_inc(used, 1)
            else:
                project(in_s + c, 0, banks[0]).then_inc(hs["t0"], 1)
                project(in_s + c, 1, banks[1]).then_inc(used, 1)
        unit(0, 0, gated=True)
        ada_sum(pe, 3)
        unit(1, 0)
        ada_turn(pe, 3)
        over(pe, IN_UNITS - 2, lambda c, it: unit(c + 2, it))

    def u_tile(c, it, h, sl=slice(None)):
        return tile_of(u, 2 * c + h, it, 4, sl)

    def hyena_in_act(act):
        act.preload_act_table(ACT.Identity)

        def unit(c, it):
            act.wait_ge(hs["t0"], c + 1 + 2 * it)
            for h in range(2):
                if h:
                    act.wait_ge(used, in_s + c + 1 + 2 * it)
                nc.scalar.activation(u_tile(c, it, h), bank[2 * (c % 2) + h][:], ACT.Identity,
                                     bias=dcol("hy_conv_b", 2 * c + h, it, 4),
                                     scale=dcol("hy_conv_w", 3 * KT + 2 * c + h, it, 4)).then_inc(hs["m"], 1)
        def split_and_unit(c, it):
            split_hi(act, in_r + c + 2, in_s + c + 2, it, in_n)
            unit(c, it)
        over(act, IN_UNITS - 2, split_and_unit)
        act.wait_ge(ada_tr, 4)
        for part in range(2):
            tables_act(act, "td", td_h, [part])
            unit(IN_UNITS - 2 + part, 0)

    def hyena_in_dve(dve):
        def unit(c, it):
            for h in range(2):
                dve.wait_ge(hs["m"], 2 * c + h + 1 + 4 * it)
                t1 = u_tile(c, it, h, slice(1, L))
                nc.vector.scalar_tensor_tensor(t1, bank[2 * (c % 2) + h][:, 0:L - 1], dcol("hy_conv_w", 2 * c + h, it, 4), t1,
                                               ALU.mult, ALU.add).then_inc(hs["d1"], 1)
            for h in range(2):
                dve.wait_ge(hs["d1"], 2 * c + h + 1 + 4 * it)
                t0 = u_tile(c, it, h, slice(0, L - 1))
                nc.vector.scalar_tensor_tensor(t0, bank[2 * (c % 2) + h][:, 1:L], dcol("hy_conv_w", 6 * KT + 2 * c + h, it, 4), t0,
                                               ALU.mult, ALU.add).then_inc(hs["d2"], 1)
        def split_and_unit(c, it):
            split_lo(dve, in_r + c + 2, in_s + c + 2, it, in_n)
            unit(c, it)
        over(dve, IN_UNITS - 2, split_and_unit)
        ada_mods(dve, 3)
        for part in range(2):
            tables_dve(dve, "td", td_h, td_l, 2, [part])
            unit(IN_UNITS - 2 + part, 0)

    def turn_pe(pe, n):
        if n < KT:
            pe.wait_ge(hs["d2"], n + 1)
            pe.wait_ge(ada_ev, 2 * 3 + 1)
        else:
            pe.wait_ge(hs["zu"], n - KT + 1)
        if n >= 2:
            pe.wait_ge(hs["zl"], n - 1)
        for t in range(LT):
            ins = nc.tensor.transpose(bank[6 + n % 2][:, t * P:(t + 1) * P], u[:, n % KT, t * P:(t + 1) * P], ident[:])
        ins.then_inc(hs["tr"], 1)

    def turned(w, n):
        return w[:, :, (n % KT) * P:(n % KT + 1) * P]

    def turn_act(act, n):
        act.wait_ge(hs["tr"], n + 1)
        if n >= KT:
            act.wait_ge(hs["f"], LT * ((n - KT) // 2 + 1))
        nc.scalar.activation(turned(zt_h, n), bank[6 + n % 2][:].rearrange("p (t c) -> p t c", t=LT), ACT.Copy)\
          .then_inc(hs["zh"], 1)

    def turn_dve(dve, n):
        dve.wait_ge(hs["zh"], n + 1)
        nc.vector.tensor_tensor(turned(zt_l, n), bank[6 + n % 2][:].rearrange("p (t c) -> p t c", t=LT),
                                turned(zt_h, n).bitcast(F32), ALU.subtract).then_inc(hs["zl"], 1)

    def forward_pe(pe, g):
        q = g % NCH
        pe.wait_ge(hs["zl"], KT * (g // NCH) + 2 * q + 2)
        for k in range(LT):
            if g:
                pe.wait_ge(hs["px"], LT * (g - 1) + k + 1)
            for part in range(2):
                for t in range(LT):
                    ks, cs = slice(k * P, (k + 1) * P), slice(q * CH, (q + 1) * CH)
                    ins = three_pass(bank[k][:, part * CH:(part + 1) * CH], (td_h[:, part, t, ks], td_l[:, part, t, ks]),
                                     (zt_h[:, t, cs], zt_l[:, t, cs]), t == 0, t == LT - 1)
            ins.then_inc(hs["f"], 1)

    def inverse_pe(pe, g):
        for c in range(2):
            if g:
                pe.wait_ge(hs["ze"], 2 * (g - 1) + c + 1)
            for k in range(LT):
                if c == 0:
                    pe.wait_ge(hs["yl"], LT * g + k + 1)
                for part in range(2):
                    cs = slice(c * P, (c + 1) * P)
                    ins = three_pass(bank[4 + c][:], (y_h[g % 2][:, k, part, cs], y_l[g % 2][:, k, part, cs]),
                                     (td_h[:, part, k], td_l[:, part, k]), k == 0 and part == 0, k == LT - 1 and part == 1)
            ins.then_inc(hs["iv"], 1)

    def hyena_pe(pe):
        for n in range(KT):
            turn_pe(pe, n)
        pe.wait_ge(raw_done, ring["td"][0] + 2)
        forward_pe(pe, 0)
        for g in range(CHUNKS):
            if g + 1 < CHUNKS:
                forward_pe(pe, g + 1)
            if 1 <= g <= NCH:
                turn_pe(pe, KT + 2 * (g - 1))
                turn_pe(pe, KT + 2 * (g - 1) + 1)
            inverse_pe(pe, g)

    def hyena_dve(dve):
        for n in range(KT):
            turn_dve(dve, n)

        def low(i):
            dve.wait_ge(hs["yh"], i + 1)
            yh, yl = y_h[i // LT % 2], y_l[i // LT % 2]
            nc.vector.tensor_tensor(yl[:, i % LT], y_f[:], yh[:, i % LT].bitcast(F32), ALU.subtract).then_inc(hs["yl"], 1)

        def product(g):
            r = spec_r + g
            h = raw[r % 2][:].rearrange("p (k s c) -> p k s c", k=LT, s=2)
            dve.wait_ge(raw_in[r % 2], 32 * (r // 2 + 1))
            for k in range(LT):
                i = LT * g + k
                xk = bank[k][:].rearrange("p (s c) -> p s c", s=2)
                dve.wait_ge(hs["f"], i + 1)
                if i:
                    dve.wait_ge(hs["yf"], i)
                nc.vector.tensor_tensor(pt1[:], xk, h[:, k, 0, :].unsqueeze(1).broadcast_to([P, 2, CH]), ALU.mult)
                nc.vector.tensor_tensor(pt2[:], xk, h[:, k, 1, :].unsqueeze(1).broadcast_to([P, 2, CH]), ALU.mult)\
                  .then_inc(hs["px"], 1)
                if i:
                    low(i - 1)
                    dve.wait_ge(hs["yl"], i)
                dve.wait_ge(hs["px"], i + 1)
                ins = nc.vector.tensor_tensor(y_f[:, 0], pt1[:, 0], pt2[:, 1], ALU.subtract)
                if k == LT - 1:
                    ins.then_inc(raw_done, 1)
                nc.vector.tensor_tensor(y_f[:, 1], pt1[:, 1], pt2[:, 0], ALU.add).then_inc(hs["yf"], 1)

        def result(g):
            o, q = divmod(g, NCH)
            for c in range(2):
                ct, i = 2 * q + c, 2 * g + c
                z = u[:, ct]
                dve.wait_ge(hs["iv"], i + 1)
                nc.vector.scalar_tensor_tensor(z, z, col("hy_skip", o * KT + ct), bank[4 + c][:], ALU.mult, ALU.add)\
                  .then_inc(hs["ze"], 1)
                dve.wait_ge(hs["ze"], i + 1)
                nc.vector.tensor_tensor(z, z, u[:, KT * (1 + o) + ct], ALU.mult).then_inc(hs["zu"], 1)
                if o == 1:
                    dve.wait_ge(hs["zh2"], ct + 1)
                    nc.vector.tensor_tensor(z_l[:, ct], z, z_h[:, ct].bitcast(F32), ALU.subtract).then_inc(hs["zl2"], 1)

        product(0)
        for g in range(CHUNKS):
            if g + 1 < CHUNKS:
                product(g + 1)
            else:
                low(LT * CHUNKS - 1)
            if g == CHUNKS - 1:
                for k in range(2):
                    split_lo(dve, out_r + k, out_s + k, 0, out_n)
            if 1 <= g <= NCH:
                turn_dve(dve, KT + 2 * (g - 1))
                turn_dve(dve, KT + 2 * (g - 1) + 1)
            result(g)

    def hyena_act(act):
        for n in range(KT):
            turn_act(act, n)

        def high(g):
            for k in range(LT):
                i = LT * g + k
                act.wait_ge(hs["yf"], i + 1)
                if g >= 2 and k == 0:
                    act.wait_ge(hs["iv"], 2 * (g - 1))
                nc.scalar.activation(y_h[g % 2][:, k], y_f[:], ACT.Copy).then_inc(hs["yh"], 1)

        high(0)
        for g in range(CHUNKS):
            if g + 1 < CHUNKS:
                high(g + 1)
            else:
                act.wait_ge(hs["iv"], 2 * (CHUNKS - 1))
                for k in range(2):
                    split_hi(act, out_r + k, out_s + k, 0, out_n)
            if 1 <= g <= NCH:
                turn_act(act, KT + 2 * (g - 1))
                turn_act(act, KT + 2 * (g - 1) + 1)
            if g >= NCH:
                for c in range(2):
                    act.wait_ge(hs["zu"], 2 * g + c + 1)
                    nc.scalar.activation(z_h[:, 2 * (g % NCH) + c], u[:, 2 * (g % NCH) + c], ACT.Copy).then_inc(hs["zh2"], 1)

    hy = sems("hybrid", "in hp ea ed ft fb ch fa aux wfh stored ones wf")
    win_r, win_s = ring["win"][0:2]
    gates = nc.dram_tensor("gates", (2, FOX_HEADS, L), F32).ap()
    f_x, f_n, f_l, f_8, f_m8, f_one = [at(f"f_{i}", AREA + 72192 + 2048 * i, [FOX_HEADS, L]) for i in range(6)]

    def hybrid_sp(sp):
        for i in range(9):
            load(sp, win_r + i, 0, cols2(A["w_in_2"], 2 * P * i, 0, 0))
            if i == 1:
                c0 = 9 * 2 * P
                sp.dma_start(wf[:], A["w_in_2"][:, c0:c0 + FOX_HEADS].rearrange("(k p) n -> p k n", p=P)).then_inc(hy["wf"], 16)
            if i == 4:
                sp.wait_ge(ada_tr, 6)
                sp.dma_start(alibi[:], C["alibi"]).then_inc(hy["in"], 16)
                sp.dma_start(causal[:], C["causal"]).then_inc(hy["in"], 16)
        sp.wait_ge(hy["fb"], 1)
        for i, src in enumerate((f_8, f_m8)):
            sp.dma_start(gates[i], src[:]).then_inc(hy["stored"], 16)
        sp.wait_ge(hy["stored"], 32)
        sp.wait_ge(hy["ones"], 1)
        for i, dst in enumerate((qfx[HD:HD + 1], kfx[HD + 1:HD + 2])):
            sp.dma_start(dst, gates[i].unsqueeze(0)).then_inc(hy["aux"], 16)

    def hybrid_pool(pool):
        pool.wait_ge(n6.done[0], n6.done[1] + KT)
        pool.wait_ge(raw_done, win_r + 2)
        nc.gpsimd.memset(qfx[HD:HD + 2], 1.0)
        nc.gpsimd.memset(kfx[HD:HD + 2], 1.0).then_inc(hy["ones"], 1)

    HEAD_TILES = {}
    for T in range(14):
        i, h = divmod(T, 2)
        if i < 2:
            HEAD_TILES[T] = (qa[:, 2 * T], qa[:, 2 * T + 1])
        elif i == 2:
            if h == 0:
                HEAD_TILES[T] = (ka[:, 0], ka[:, 1])
        elif i < 5:
            j = T - 6
            HEAD_TILES[T] = (qfx[0:HD, 2 * j], qfx[0:HD, 2 * j + 1])
        else:
            j = T - 10
            HEAD_TILES[T] = (kfx[0:HD, 2 * j], kfx[0:HD, 2 * j + 1])

    def odd_heads(tiles):
        return sum(T in HEAD_TILES for T in range(tiles))

    def hybrid_pe(pe, norm):
        for i in range(9):
            pe.wait_ge(raw_done, win_r + i + 1)
            s = win_s + i
            for h in range(2):
                T = 2 * i + h
                if T >= 4:
                    pe.wait_ge(hy["ea"], T - 3)
                    pe.wait_ge(hy["ed"], odd_heads(T - 3))
                if T == 0:
                    first, second = project_pair(pe, s, (bank[0][:], bank[1][:]), norm.done)
                    first.then_inc(hy["hp"], 1)
                    second.then_inc(used, 1)
                    continue
                if T == 1:
                    continue
                if i >= 7:
                    w = slot_w(s)
                    for t in (2 * h, 2 * h + 1):
                        for k in range(KT):
                            ts = slice(t * P, (t + 1) * P)
                            ins = three_pass(bank[T % 4][:, (t % 2) * 256:(t % 2) * 256 + 256], (hh[:, k, ts], hl[:, k, ts]),
                                             (w[0][:, k], w[1][:, k]), k == 0, k == KT - 1)
                elif T == 5:
                    ins = project_rows(s, P, P, lambda t: bank[T % 4][:, t * P:(t + 1) * P])
                else:
                    ins = project(s, h, bank[T % 4][:])
                ins.then_inc(used if h else hy["hp"], 1)
            if i == 0:
                ada_sum(pe, 5)
            if i == 1:
                ada_turn(pe, 5)
            if i == 2:
                pe.wait_ge(ada_ev, 2 * 5 + 1)
                pe.wait_ge(hy["wfh"], 2)
                for k in range(KT):
                    ins = three_pass(bank[6][0:FOX_HEADS, :], (wf_h[:, k], wf_l[:, k]), (hh[:, k], hl[:, k]),
                                     k == 0, k == KT - 1)
                ins.then_inc(hy["ft"], 1)

    def tile_ready(eng, T):
        if T % 2:
            eng.wait_ge(used, win_s + T // 2 + 1)
        else:
            eng.wait_ge(hy["hp"], T // 2 + 1)

    def hybrid_act(act, splits):
        act.wait_ge(hy["wf"], 16)
        nc.scalar.activation(wf_h[:], wf[:], ACT.Copy).then_inc(hy["wfh"], 1)
        for T in range(18):
            if T % 2 == 0:
                splits(T // 2)
            tile_ready(act, T)
            if T in HEAD_TILES:
                ins = nc.scalar.activation(HEAD_TILES[T][0], bank[T % 4][0:HD, :], ACT.Copy)
            elif T == 5:
                ins = nc.scalar.activation(va[:].rearrange("p t n -> p (t n)"), bank[T % 4][:], ACT.Copy)
            else:
                i, h = divmod(T, 2)
                ins = nc.scalar.activation(vfx[:, 2 * h:2 * h + 2, (i - 7) * 256:(i - 7) * 256 + 256],
                                           bank[T % 4][:].rearrange("p (t n) -> p t n", t=2), ACT.Copy)
            ins.then_inc(hy["ea"], 1)
            if T == 8:
                act.wait_ge(hy["ch"], 2)
                nc.scalar.activation(f_l[:], f_n[:], ACT.Exp).then_inc(hy["fa"], 1)
                act.wait_ge(hy["fa"], 1)
                nc.scalar.activation(f_l[:], f_l[:], ACT.Ln, bias=1.0).then_inc(hy["fa"], 1)

    def hybrid_dve(dve, splits):
        n = [0]

        def link(ins):
            n[0] += 1
            ins.then_inc(hy["ch"], 1)
            dve.wait_ge(hy["ch"], n[0])

        dve.wait_ge(hy["wfh"], 1)
        nc.vector.tensor_tensor(wf_l[:], wf[:], wf_h[:].bitcast(F32), ALU.subtract).then_inc(hy["wfh"], 1)
        for T in range(18):
            if T % 2 == 0:
                splits(T // 2)
            tile_ready(dve, T)
            if T in HEAD_TILES:
                nc.vector.tensor_copy(HEAD_TILES[T][1], bank[T % 4][HD:P, :]).then_inc(hy["ed"], 1)
            if T == 3:
                ada_mods(dve, 5)
            if T == 7:
                dve.wait_ge(hy["ft"], 1)
                link(nc.vector.tensor_scalar(f_x[:], bank[6][0:FOX_HEADS, :], bf_col[:], None, ALU.add))
                link(nc.vector.scalar_tensor_tensor(f_n[:], f_x[:], -1.0, f_x[:], ALU.mult, ALU.min))
            if T == 10:
                dve.wait_ge(hy["fa"], 2)
                link(nc.vector.scalar_tensor_tensor(f_x[:], f_x[:], 0.0, f_l[:], ALU.min, ALU.subtract))
                nc.vector.memset(f_one[:], 1.0).then_inc(hy["ch"], 1)
                n[0] += 1
                dve.wait_ge(hy["ch"], n[0])
                link(nc.vector.tensor_tensor_scan(f_n[:], f_one[:], f_x[:], 0.0, ALU.mult, ALU.add))
                nc.vector.tensor_scalar(f_8[:], f_n[:], 1.0 / SCALE, None, ALU.mult)
                nc.vector.tensor_scalar(f_m8[:], f_n[:], -1.0 / SCALE, None, ALU.mult).then_inc(hy["fb"], 1)

    fo = sems("out", "pe ev")
    fo_dma = sem("out_stored")

    def out_pe(pe, norm):
        for i in range(2 * LT):
            half, t = divmod(i, LT)
            if t == 0:
                pe.wait_ge(norm.done[0], norm.done[1] + 4 * (half + 1))
            if i >= 4:
                pe.wait_ge(fo["ev"], i - 3)
            for k in range(4):
                ins = nc.tensor.transpose(bank[i % 4][:, k * P:(k + 1) * P], x[:, 4 * half + k, t * P:(t + 1) * P], ident[:])
            ins.then_inc(fo["pe"], 1)

    def out_act(act):
        for i in range(2 * LT):
            half, t = divmod(i, LT)
            act.wait_ge(fo["pe"], i + 1)
            nc.scalar.activation(out_rows[:, t, half * 512:half * 512 + 512], bank[i % 4][:], ACT.Copy).then_inc(fo["ev"], 1)

    def out_sp(sp):
        for i in range(2 * LT):
            half, t = divmod(i, LT)
            cs = slice(half * 512, half * 512 + 512)
            sp.wait_ge(fo["ev"], i + 1)
            sp.dma_start(out[0, t * P:(t + 1) * P, cs], out_rows[:, t, cs]).then_inc(fo_dma, 16)
        sp.wait_ge(fo_dma, 16 * 2 * LT)

    back1 = Back("wo", A["attn_w_o"][0], 0, (hh, hl), lambda k: [(attn1.s["ol"], attn1.j0 + k + 1)])
    back2 = Back("hyout", A["hy_w_out"][0], 1, (z_h, z_l), lambda k: [(hs["zl2"], k + 1)])
    back3 = Back("wout", A["w_out_2"], 2, (hh, hl),
                 lambda k: [(swa.s["ol"], swa.j0 + k + 1)] if k < 4 else [(fox.s["ol"], fox.j0 + k - 3)])
    n1 = mod_norm((xs["ev"], 0), 0, 0, "qkv")
    n2 = mod_norm((back1.s["x"], back1.x0), 0, 1, "up0_0")
    ffn0 = Ffn(0, A["ffn_w_up"][0], A["ffn_w_down"][0], n2, "ffn_conv_w", "ffn_conv_b", 0, False, ring["hyin"][0:3], 2)
    n3 = mod_norm((ffn0.s["xd"], KT), 1, 0, "hyin")
    n4 = mod_norm((back2.s["x"], back2.x0), 1, 1, "up1_0")
    ffn1 = Ffn(1, A["ffn_w_up"][1], A["ffn_w_down"][1], n4, "ffn_conv_w", "ffn_conv_b", 0, False, ring["win"][0:3], 4)
    n6 = DoubleNorm((ffn1.s["xd"], KT), lambda t: fgs[:, t:t + 1], lambda t: mod[:, 2, t:t + 1], 2 * 4 + 2, "win")
    n7 = mod_norm((back3.s["x"], back3.x0), 2, 1, "up2_0")
    ffn2 = Ffn(2, A["w_up_2"], A["w_down_2"], n7, "conv_w_2", "conv_b_2", FF, True, None, None)
    n8 = Norm((ffn2.s["xd"], KT), lambda t: col("g_final_2", t), None, None)

    def ahead(split, eng, key, nxt):
        r0, s0, n_el, n = ring[key]

        def go(i):
            if i + 2 < n:
                split(eng, r0 + i + 2, s0 + i + 2, 0, n_el)
            elif nxt and not (i + 1 == n and nxt.startswith("up")):
                r, s, m, _ = ring[nxt]
                split(eng, r + i + 2 - n, s + i + 2 - n, 0, m)
        return go

    with nc.Block() as block:

        @block.sync
        def _(sp):
            prep_sp(sp)
            for i in range(2):
                load(sp, qkv_r + i, 0, cols2(A["attn_w_qkv"][0], 2 * P * i, 0, 0))
            filter_sp(sp)
            ada_spread(sp, 0)
            sp.dma_start(rope[:], C["rope"].rearrange("s p l -> p s l")).then_inc(rp_in, 16)
            for i in range(2, 6):
                load(sp, qkv_r + i, 0, cols2(A["attn_w_qkv"][0], 2 * P * i, 0, 0))
            back1.sp(sp)
            ffn0.sp(sp)
            hyena_sp(sp)
            back2.sp(sp)
            ffn1.sp(sp)
            hybrid_sp(sp)
            back3.sp(sp)
            ffn2.sp(sp)
            out_sp(sp)

        @block.gpsimd
        def _(pool):
            pool.wait_ge(fl["in"], 32)
            ada_load_first(pool, 0)
            filter_pool(pool)
            ada_load_first(pool, 1)
            n1.split_late(pool)
            qkv_pool(pool)
            ada_load_rest(pool, 1)
            ada_spread(pool, 1)
            n2.pool(pool)
            ada_load_first(pool, 2)
            ada_load_rest(pool, 2)
            ada_spread(pool, 2)
            ada_load_first(pool, 3)
            ada_load_rest(pool, 3, n3)
            n3.split_late(pool)
            ada_spread(pool, 3)
            n4.pool(pool)
            pool.wait_ge(used, out_s + 4)
            ada_load_first(pool, 4)
            ada_load_rest(pool, 4)
            ada_spread(pool, 4)
            ada_load_first(pool, 5)
            pool.wait_ge(ffn1.s["hl"], 2 * FH)
            pool.wait_ge(dn["g"], 1)
            nc.gpsimd.memset(wacc[:], 0.0).then_inc(dn["w"], 1)
            n6.pool_zero(pool)
            for c in range(EARLY):
                ada_load_one(pool, 5, 2 + c, 0)
                n6.pool_square(pool, c, 0)
            n6.split_late(pool)
            ada_spread(pool, 5)
            hybrid_pool(pool)
            n7.pool(pool)
            n8.pool(pool)

        @block.scalar
        def _(act):
            prep_act(act)
            sin_act(act)
            filter_act(act)
            xload_act(act, n1)
            n1.factors_act(act)
            qkv_act(act, ahead(split_hi, act, "qkv", "wo"))
            attn1.act(act, lambda i: ahead(split_hi, act, "qkv", "wo")(5) if i == 8 else None)
            back1.act(act, ahead(split_hi, act, "wo", "up0_0"))
            n2.act(act)
            ffn0.act(act)
            n3.act(act)
            hyena_in_act(act)
            hyena_act(act)
            back2.act(act, ahead(split_hi, act, "hyout", "up1_0"))
            n4.act(act)
            ffn1.act(act)
            n6.act(act)
            hybrid_act(act, ahead(split_hi, act, "win", "wout"))
            swa.act(act)
            fox.act(act)
            back3.act(act, ahead(split_hi, act, "wout", "up2_0"))
            n7.act(act)
            ffn2.act(act)
            n8.act(act)
            out_act(act)

        @block.vector
        def _(dve):
            ones_dve(dve)
            sin_dve(dve)
            filter_dve(dve)
            ada_evict(dve, 0)
            n1.add_squares(dve)
            split_lo(dve, qkv_r, qkv_s, 0, UNIT)
            ada_mods(dve, 0)
            n1.dve(dve)
            qkv_dve(dve, ahead(split_lo, dve, "qkv", "wo"))

            def beside_attention(i):
                if i == 9:
                    ahead(split_lo, dve, "qkv", "wo")(5)
                if i % 8 == 5:
                    ada_step(dve, 1, i // 8, 0)
            attn1.dve(dve, beside_attention)
            ada_evict(dve, 1)
            back1.dve(dve, ahead(split_lo, dve, "wo", "up0_0"))
            ada_mods(dve, 1)
            n2.dve(dve)
            ffn0.dve(dve)
            n3.dve(dve)
            ada_step(dve, 3, KT - 1, 0)
            ada_evict(dve, 3)
            hyena_in_dve(dve)
            hyena_dve(dve)
            back2.dve(dve, ahead(split_lo, dve, "hyout", "up1_0"))
            n4.dve(dve)
            n6.gain2(dve)
            ffn1.dve(dve)
            n6.dve(dve)
            n6.residual(dve)
            ada_step(dve, 5, KT - 1, 0)
            ada_evict(dve, 5)
            hybrid_dve(dve, ahead(split_lo, dve, "win", "wout"))
            swa.dve(dve)
            fox.dve(dve)
            dve.wait_ge(dn["x"], KT)
            back3.dve(dve, ahead(split_lo, dve, "wout", "up2_0"))
            n7.dve(dve)
            ffn2.dve(dve)
            n8.dve(dve)

        @block.tensor
        def _(pe):
            sin_pe(pe)
            filter_pe(pe)
            ada_sum(pe, 0)
            xload_pe(pe)
            ada_turn(pe, 0)
            n1.pe(pe)
            qkv_pe(pe, n1)
            attn1.pe(pe, [(qk["done"], NQK), (qk["vd"], 1)])
            ada_sum(pe, 1)
            back1.pe(pe)
            ada_turn(pe, 1)
            n2.pe(pe)
            ffn0.pe(pe)
            n3.pe(pe)
            hyena_in_pe(pe, n3)
            hyena_pe(pe)
            back2.pe(pe)
            n4.pe(pe)
            ffn1.pe(pe)
            n6.pe(pe)
            hybrid_pe(pe, n6)
            pe.wait_ge(hy["in"], 32)
            swa.pe(pe, [(hy["ea"], 18), (hy["ed"], len(HEAD_TILES)), (hy["aux"], 32)])
            fox.pe(pe, [(hy["aux"], 32), (swa.s["ol"], swa.j0 + SWA_HEADS // 2)])
            back3.pe(pe)
            n7.pe(pe)
            ffn2.pe(pe)
            n8.pe(pe)
            out_pe(pe, n8)


USED_INPUTS = ["x", "c", "ada_w", "ada_b", "norm1_g", "norm2_g", "final_g", "attn_w_qkv", "attn_w_o", "attn_q_gain",
               "attn_k_gain", "hy_w_in", "hy_conv_w", "hy_conv_b", "hy_f_w1", "hy_f_b1", "hy_f_w2", "hy_f_b2", "hy_f_w3",
               "hy_f_freq", "hy_skip", "hy_w_out", "ffn_w_up", "ffn_conv_w", "ffn_conv_b", "ffn_w_down", "c_2", "w_ada_2",
               "b_ada_2", "g_attn_2", "w_in_2", "b_f_2", "sinks_2", "w_out_2", "g_mlp_2", "w_up_2", "conv_w_2", "conv_b_2",
               "w_down_2", "g_final_2"]


def kernel(**inputs):
    import concourse.bacc as bacc
    from concourse.bass_utils import run_bass_kernel_spmd

    nc = bacc.Bacc("TRN2", target_bir_lowering=False, num_devices=1)
    arrays, A, C = {}, {}, {}
    for name in USED_INPUTS:
        a = np.ascontiguousarray(inputs[name])
        arrays[f"in_{name}"] = a
        A[name] = nc.dram_tensor(f"in_{name}", a.shape, mybir.dt.from_np(a.dtype), kind="ExternalInput").ap()
    for name, a in shape_constants().items():
        a = np.ascontiguousarray(a)
        arrays[f"table_{name}"] = a
        C[name] = nc.dram_tensor(f"table_{name}", a.shape, mybir.dt.from_np(a.dtype), kind="ExternalInput").ap()
    out = nc.dram_tensor("out", (1, L, D), F32, kind="ExternalOutput").ap()
    build_program(nc, A, C, out)
    result = run_bass_kernel_spmd(nc, [arrays], core_ids=[0])
    return result.results[0]["out"]
```
